# Optimizing a Trainium2 kernel written in Bass

```python
import math
import jax, jax.numpy as jnp
from jax import lax
import numpy as np

D_MODEL = 1024
BATCH = 1
SEQ = 256
DEPTH = 2

GRID_W = 64
CTX_LEN = 256
HEAD_DIM = 64
ROPE_THETA = 10000.0
NORM_EPS = 1e-6
NEG_INF = -1e30

A_HEADS = 8
A_KV_HEADS = 2
A_WINDOW = 128
A_BLOCK = 128
B_HEADS = 8
NA_ROWS = 8
NA_COLS = 16
NA_COL_BLOCK = 16
NA_BAND = 32
C_HEADS = 4
C_VDIM = 2 * HEAD_DIM
C_BLOCK = 128
PEER_HEADS = 8
PEER_KEYS = 128
PEER_TOPK = 16
PEER_QDIM = 256
N_EXPERTS = PEER_KEYS * PEER_KEYS
PEER_CHUNK = 128

A_Q_W = A_HEADS * HEAD_DIM
A_KV_W = A_KV_HEADS * HEAD_DIM
B_W = B_HEADS * HEAD_DIM
C_QK_W = C_HEADS * 2 * HEAD_DIM
C_V_W = C_HEADS * C_VDIM
IN_SPLITS = (A_Q_W, A_KV_W, A_KV_W, B_W, B_W, B_W, C_QK_W, C_QK_W, C_V_W, D_MODEL, D_MODEL, D_MODEL)
IN_W = 6912

kernel_name = "hybrid_dit_gqa_natten_diffattn_peer"

def rms_norm(x, g):
    xf = x.astype(jnp.float32)
    y = xf * lax.rsqrt(jnp.mean(xf * xf, axis=-1, keepdims=True) + NORM_EPS)
    return (y * g.astype(jnp.float32)).astype(x.dtype)

def split_cols(p):
    idx = np.cumsum(np.array(IN_SPLITS))[:-1].tolist()
    return jnp.split(p, idx, axis=-1)

def axial_rope(n):
    t = jnp.arange(n, dtype=jnp.int32)
    row = (t // GRID_W).astype(jnp.float32)
    col = (t % GRID_W).astype(jnp.float32)
    n_freq = HEAD_DIM // 4
    inv = ROPE_THETA ** (-jnp.arange(n_freq, dtype=jnp.float32) / n_freq)
    ang = jnp.concatenate([row[:, None] * inv, col[:, None] * inv], axis=-1)
    return jnp.cos(ang), jnp.sin(ang)

def apply_rope(x, cos, sin):
    half = HEAD_DIM // 2
    xf = x.astype(jnp.float32)
    x1, x2 = xf[..., :half], xf[..., half:]
    cs, sn = cos[None, :, None, :], sin[None, :, None, :]
    return jnp.concatenate([x1 * cs - x2 * sn, x2 * cs + x1 * sn], axis=-1).astype(x.dtype)

def project_heads(h, w, rope):
    p = split_cols(h @ w)
    B, n = h.shape[:2]
    aq = p[0].reshape(B, n, A_HEADS, HEAD_DIM)
    ak = p[1].reshape(B, n, A_KV_HEADS, HEAD_DIM)
    av = p[2].reshape(B, n, A_KV_HEADS, HEAD_DIM)
    bq = p[3].reshape(B, n, B_HEADS, HEAD_DIM)
    bk = p[4].reshape(B, n, B_HEADS, HEAD_DIM)
    bv = p[5].reshape(B, n, B_HEADS, HEAD_DIM)
    cq = p[6].reshape(B, n, C_HEADS * 2, HEAD_DIM)
    ck = p[7].reshape(B, n, C_HEADS * 2, HEAD_DIM)
    cv = p[8].reshape(B, n, C_HEADS, C_VDIM)
    if rope is not None:
        cos, sin = rope
        aq, ak = apply_rope(aq, cos, sin), apply_rope(ak, cos, sin)
        cq, ck = apply_rope(cq, cos, sin), apply_rope(ck, cos, sin)
    cq = cq.reshape(B, n, C_HEADS, 2, HEAD_DIM)
    ck = ck.reshape(B, n, C_HEADS, 2, HEAD_DIM)
    return {"aq": aq, "ak": ak, "av": av, "bq": bq, "bk": bk, "bv": bv,
            "cq": cq, "ck": ck, "cv": cv, "ga": p[9], "gb": p[10], "gc": p[11]}

def context_attention(q, k, v, sink=None):
    B, L, H, D = q.shape
    G = k.shape[2]
    R = H // G
    qg = q.reshape(B, L, G, R, D)
    s = jnp.einsum('blgrd,bmgd->bgrlm', qg, k).astype(jnp.float32) * (D ** -0.5)
    if sink is not None:
        sk = jnp.broadcast_to(sink.reshape(G, R, 1, 1).astype(jnp.float32), s.shape[:-1] + (1,))
        s = jnp.concatenate([s, sk], axis=-1)
    p = jax.nn.softmax(s, axis=-1)[..., :L].astype(v.dtype)
    return jnp.einsum('bgrlm,bmgd->blgrd', p, v).reshape(B, L, H * D)

def window_gqa_latent(q, k, v, kc, vc, sink):
    B, N = q.shape[:2]
    L = kc.shape[1]
    nb = N // A_BLOCK
    G, R = A_KV_HEADS, A_HEADS // A_KV_HEADS
    scale = HEAD_DIM ** -0.5
    qb = q.reshape(B, nb, A_BLOCK, G, R, HEAD_DIM)

    def band(t):
        tp = jnp.pad(t, ((0, 0), (A_BLOCK, A_BLOCK), (0, 0), (0, 0))).reshape(B, nb + 2, A_BLOCK, G, HEAD_DIM)
        return jnp.concatenate([tp[:, :-2], tp[:, 1:-1], tp[:, 2:]], axis=2)

    kb, vb = band(k), band(v)
    nk = 3 * A_BLOCK
    qpos = jnp.arange(nb)[:, None] * A_BLOCK + jnp.arange(A_BLOCK)[None, :]
    kpos = jnp.arange(nb)[:, None] * A_BLOCK - A_BLOCK + jnp.arange(nk)[None, :]
    valid = ((jnp.abs(qpos[:, :, None] - kpos[:, None, :]) <= A_WINDOW)
             & (kpos[:, None, :] >= 0) & (kpos[:, None, :] < N))
    s_loc = jnp.einsum('bnqgrd,bnkgd->bgrnqk', qb, kb).astype(jnp.float32) * scale
    s_loc = jnp.where(valid, s_loc, NEG_INF)
    s_ctx = jnp.einsum('bnqgrd,blgd->bgrnql', qb, kc).astype(jnp.float32) * scale
    sk = jnp.broadcast_to(sink.reshape(G, R, 1, 1, 1).astype(jnp.float32), s_loc.shape[:-1] + (1,))
    p = jax.nn.softmax(jnp.concatenate([s_loc, s_ctx, sk], axis=-1), axis=-1).astype(v.dtype)
    o = (jnp.einsum('bgrnqk,bnkgd->bnqgrd', p[..., :nk], vb)
         + jnp.einsum('bgrnql,blgd->bnqgrd', p[..., nk:nk + L], vc))
    return o.reshape(B, N, A_HEADS * HEAD_DIM)

def na_column_tables():
    n_cb = GRID_W // NA_COL_BLOCK
    band0 = np.clip(np.arange(n_cb) * NA_COL_BLOCK - NA_COLS // 2, 0, GRID_W - NA_BAND)
    kcol = band0[:, None] + np.arange(NA_BAND)[None, :]
    qcol = np.arange(n_cb)[:, None] * NA_COL_BLOCK + np.arange(NA_COL_BLOCK)[None, :]
    cstart = np.clip(qcol - NA_COLS // 2, 0, GRID_W - NA_COLS)
    valid = (kcol[:, None, :] >= cstart[:, :, None]) & (kcol[:, None, :] < cstart[:, :, None] + NA_COLS)
    dc = np.clip(kcol[:, None, :] - qcol[:, :, None], -(NA_COLS - 1), NA_COLS - 1) + NA_COLS - 1
    return jnp.asarray(kcol), jnp.asarray(valid), jnp.asarray(dc)

def neighborhood_latent(q, k, v, kc, vc, rpb):
    B, N = q.shape[:2]
    rows = N // GRID_W
    kr = min(NA_ROWS, rows)
    n_cb = GRID_W // NA_COL_BLOCK
    H, D = B_HEADS, HEAD_DIM
    scale = D ** -0.5
    kcol, valid, dc = na_column_tables()
    qg = q.reshape(B, rows, GRID_W, H, D)
    kg = k.reshape(B, rows, GRID_W, H, D)
    vg = v.reshape(B, rows, GRID_W, H, D)
    nloc = kr * NA_BAND

    def row_step(r):
        rs = jnp.clip(r - kr // 2, 0, rows - kr)
        kw = lax.dynamic_slice_in_dim(kg, rs, kr, axis=1)[:, :, kcol]
        vw = lax.dynamic_slice_in_dim(vg, rs, kr, axis=1)[:, :, kcol]
        qr = lax.dynamic_index_in_dim(qg, r, axis=1, keepdims=False).reshape(B, n_cb, NA_COL_BLOCK, H, D)
        s = jnp.einsum('bnqhd,bknjhd->bhnqkj', qr, kw).astype(jnp.float32) * scale
        dr = rs + jnp.arange(kr) - r + NA_ROWS - 1
        bias = rpb[:, dr[None, None, :, None], dc[:, :, None, :]].astype(jnp.float32)
        s = jnp.where(valid[:, :, None, :], s + bias, NEG_INF)
        s_c = jnp.einsum('bnqhd,blhd->bhnql', qr, kc).astype(jnp.float32) * scale
        logits = jnp.concatenate([s.reshape(B, H, n_cb, NA_COL_BLOCK, nloc), s_c], axis=-1)
        p = jax.nn.softmax(logits, axis=-1).astype(v.dtype)
        p_loc = p[..., :nloc].reshape(B, H, n_cb, NA_COL_BLOCK, kr, NA_BAND)
        o = (jnp.einsum('bhnqkj,bknjhd->bnqhd', p_loc, vw)
             + jnp.einsum('bhnql,blhd->bnqhd', p[..., nloc:], vc))
        return o.reshape(B, GRID_W, H * D)

    o = lax.map(row_step, jnp.arange(rows, dtype=jnp.int32))
    return jnp.moveaxis(o, 0, 1).reshape(B, N, H * D)

def diff_lambda(lam, lam_init):
    lf = lam.astype(jnp.float32)
    return jnp.exp(jnp.sum(lf[0] * lf[1])) - jnp.exp(jnp.sum(lf[2] * lf[3])) + lam_init

def diff_attention_block(qb, k, v, lam):
    s = jnp.einsum('bqhmd,bkhmd->bhmqk', qb, k).astype(jnp.float32) * (HEAD_DIM ** -0.5)
    p = jax.nn.softmax(s, axis=-1)
    a = (p[:, :, 0] - lam * p[:, :, 1]).astype(v.dtype)
    return jnp.einsum('bhqk,bkhd->bqhd', a, v)

def diff_attention_latent(q, k, v, kc, vc, lam):
    B, N = q.shape[:2]
    nb = N // C_BLOCK
    kall = jnp.concatenate([k, kc], axis=1)
    vall = jnp.concatenate([v, vc], axis=1)
    qb = jnp.moveaxis(q.reshape(B, nb, C_BLOCK, C_HEADS, 2, HEAD_DIM), 1, 0)
    o = lax.map(lambda t: diff_attention_block(t, kall, vall, lam), qb)
    return jnp.moveaxis(o, 0, 1).reshape(B, N, C_HEADS, C_VDIM)

def diff_head_norm(o, g, lam_init):
    B, n = o.shape[:2]
    y = rms_norm(o, g.reshape(C_HEADS, C_VDIM)) * (1.0 - lam_init)
    return y.reshape(B, n, C_V_W)

def merge_branches(hd, ya, yb, yc, wa, wb, wc, wo):
    m = (jax.nn.sigmoid(hd["ga"]) * (ya @ wa) + jax.nn.sigmoid(hd["gb"]) * (yb @ wb)
         + jax.nn.sigmoid(hd["gc"]) * (yc @ wc))
    return m @ wo

def peer_ffn(h, wq, keys, u, v):
    shp = h.shape
    t = h.reshape(-1, PEER_CHUNK, shp[-1])

    def chunk(tc):
        q = (tc @ wq).reshape(PEER_CHUNK, PEER_HEADS, 2, PEER_QDIM // 2)
        s = jnp.einsum('thpd,hpkd->thpk', q, keys).astype(jnp.float32)
        sv, si = lax.top_k(s, PEER_TOPK)
        cand_s = (sv[:, :, 0, :, None] + sv[:, :, 1, None, :]).reshape(PEER_CHUNK, PEER_HEADS, PEER_TOPK * PEER_TOPK)
        cand_i = (si[:, :, 0, :, None] * PEER_KEYS + si[:, :, 1, None, :]).reshape(PEER_CHUNK, PEER_HEADS, PEER_TOPK * PEER_TOPK)
        top_s, pos = lax.top_k(cand_s, PEER_TOPK)
        e = jnp.take_along_axis(cand_i, pos, axis=-1)
        g = jax.nn.softmax(top_s, axis=-1)
        act = jax.nn.gelu(jnp.einsum('thkd,td->thk', u[e], tc).astype(jnp.float32), approximate=False)
        return jnp.einsum('thk,thkd->td', (g * act).astype(tc.dtype), v[e])

    return lax.map(chunk, t).reshape(shp)

def setup_inputs(seed: int = 0) -> dict:
    key = jax.random.key(seed)
    ks = jax.random.split(key, 24)
    D = D_MODEL

    def nrm(k, shape, s):
        return jax.random.normal(k, shape, jnp.float32) * s

    return {
        "x": nrm(ks[0], (BATCH, SEQ, D), 1.0),
        "c": nrm(ks[1], (BATCH, D), 1.0),
        "ctx": nrm(ks[2], (BATCH, CTX_LEN, D), 1.0),
        "c_ctx": nrm(ks[3], (D,), 1.0),
        "w_mod": nrm(ks[4], (DEPTH, D, 6 * D), 0.5 * D ** -0.5),
        "b_mod": nrm(ks[5], (DEPTH, 6 * D), 0.01),
        "g_norm1": 1.0 + nrm(ks[6], (DEPTH, D), 0.05),
        "g_norm2": 1.0 + nrm(ks[7], (DEPTH, D), 0.05),
        "w_in": nrm(ks[8], (DEPTH, D, IN_W), D ** -0.5),
        "a_sink": nrm(ks[9], (DEPTH, A_HEADS), 0.5),
        "b_rpb": nrm(ks[10], (DEPTH, B_HEADS, 2 * NA_ROWS - 1, 2 * NA_COLS - 1), 0.1),
        "c_lambda": nrm(ks[11], (DEPTH, 4, HEAD_DIM), 0.1),
        "c_subln": 1.0 + nrm(ks[12], (DEPTH, C_V_W), 0.05),
        "w_branch_a": nrm(ks[13], (DEPTH, A_Q_W, D), A_Q_W ** -0.5),
        "w_branch_b": nrm(ks[14], (DEPTH, B_W, D), B_W ** -0.5),
        "w_branch_c": nrm(ks[15], (DEPTH, C_V_W, D), C_V_W ** -0.5),
        "w_out": nrm(ks[16], (DEPTH, D, D), D ** -0.5),
        "peer_wq": nrm(ks[17], (DEPTH, D, PEER_HEADS * PEER_QDIM), D ** -0.5),
        "peer_keys": nrm(ks[18], (DEPTH, PEER_HEADS, 2, PEER_KEYS, PEER_QDIM // 2), (PEER_QDIM // 2) ** -0.5),
        "peer_u": nrm(ks[19], (DEPTH, N_EXPERTS, D), D ** -0.5),
        "peer_v": nrm(ks[20], (DEPTH, N_EXPERTS, D), PEER_HEADS ** -0.5),
        "g_final": 1.0 + nrm(ks[21], (D,), 0.05),
    }

def reference(x, c, ctx, c_ctx, w_mod, b_mod, g_norm1, g_norm2, w_in, a_sink, b_rpb, c_lambda,
              c_subln, w_branch_a, w_branch_b, w_branch_c, w_out, peer_wq, peer_keys, peer_u,
              peer_v, g_final):
    N = x.shape[1]
    rope = axial_rope(N)
    xc = ctx
    for l in range(DEPTH):
        last = l == DEPTH - 1
        lam_init = 0.8 - 0.6 * math.exp(-0.3 * l)
        lam = diff_lambda(c_lambda[l], lam_init)
        mod = (jax.nn.silu(c) @ w_mod[l] + b_mod[l])[:, None, :]
        mod_c = jax.nn.silu(c_ctx) @ w_mod[l] + b_mod[l]
        sh1, sc1, gt1, sh2, sc2, gt2 = jnp.split(mod, 6, axis=-1)
        sh1c, sc1c, gt1c, sh2c, sc2c, gt2c = jnp.split(mod_c, 6, axis=-1)

        h = rms_norm(x, g_norm1[l]) * (1.0 + sc1) + sh1
        hc = rms_norm(xc, g_norm1[l]) * (1.0 + sc1c) + sh1c
        lat = project_heads(h, w_in[l], rope)
        con = project_heads(hc, w_in[l], None)
        ya = window_gqa_latent(lat["aq"], lat["ak"], lat["av"], con["ak"], con["av"], a_sink[l])
        yb = neighborhood_latent(lat["bq"], lat["bk"], lat["bv"], con["bk"], con["bv"], b_rpb[l])
        yc = diff_head_norm(diff_attention_latent(lat["cq"], lat["ck"], lat["cv"], con["ck"], con["cv"], lam),
                            c_subln[l], lam_init)
        x = x + gt1 * merge_branches(lat, ya, yb, yc, w_branch_a[l], w_branch_b[l], w_branch_c[l], w_out[l])

        h2 = rms_norm(x, g_norm2[l]) * (1.0 + sc2) + sh2
        x = x + gt2 * peer_ffn(h2, peer_wq[l], peer_keys[l], peer_u[l], peer_v[l])

        if not last:
            ya_c = context_attention(con["aq"], con["ak"], con["av"], a_sink[l])
            yb_c = context_attention(con["bq"], con["bk"], con["bv"])
            yc_c = diff_head_norm(diff_attention_block(con["cq"], con["ck"], con["cv"], lam), c_subln[l], lam_init)
            xc = xc + gt1c * merge_branches(con, ya_c, yb_c, yc_c, w_branch_a[l], w_branch_b[l], w_branch_c[l], w_out[l])
            h2c = rms_norm(xc, g_norm2[l]) * (1.0 + sc2c) + sh2c
            xc = xc + gt2c * peer_ffn(h2c, peer_wq[l], peer_keys[l], peer_u[l], peer_v[l])
    return rms_norm(x, g_final)


_drawn_inputs = setup_inputs


def setup_inputs(seed=0):
    import zlib

    import numpy as np

    out = dict(_drawn_inputs(seed))
    spreads = {}
    factors = {'b_mod': 3.599,
     'g_norm1': 3.926,
     'g_norm2': 2.738,
     'a_sink': 8.0,
     'b_rpb': 8.0,
     'c_lambda': 3.005,
     'c_subln': 4.996}
    for name, (base, spread) in spreads.items():
        noise = np.random.default_rng([zlib.crc32(name.encode()), seed]).standard_normal(out[name].shape)
        drawn = base * np.exp(spread * noise) if base else spread * noise
        out[name] = __import__('jax').numpy.asarray(drawn.astype(out[name].dtype))
    for name, factor in factors.items():
        out[name] = (out[name] * factor).astype(out[name].dtype)
    return out
```

```python
import math
from contextlib import ExitStack

import numpy as np
import concourse.bass as bass
from concourse import mybir

P = 128
D = 1024
DC = D // P
N_LAT = 256
N_CTX = 256
T = N_LAT + N_CTX
TT = T // P
DEPTH = 2
GRID_W = 64
HD = 64
KEYS = 128
PH = 8
TOPK = 16
HK = PH * TOPK
EPS = 1e-6
NEG = -1e30
USED = -3.0e38
LAM_INIT = [0.8 - 0.6 * math.exp(-0.3 * l) for l in range(DEPTH)]

RING = 4
BLOCKS = 16
PAIR = BLOCKS * P
MOD_UNITS = 6 * DC
MOD_PAIRS = MOD_UNITS // 2
QKV_PAIRS = 15
MERGE_PAIRS = 18
WOUT_PAIRS = 4
PQ_PAIRS = 9
HALVES = 2
ROWS = KEYS // HALVES
LAYER_PAIRS = MOD_PAIRS + QKV_PAIRS + MERGE_PAIRS + WOUT_PAIRS + PQ_PAIRS

UNITS = ([("aq", u) for u in range(4)] + [("ak", 0)] + [("bq", u) for u in range(4)] + [("bk", u) for u in range(4)]
         + [("cq", u) for u in range(4)] + [("ck", u) for u in range(4)])
NU = len(UNITS)
ROPED = [k for k, (name, _) in enumerate(UNITS) if name[0] != "b"]
UNIT_AT = {unit: k for k, unit in enumerate(UNITS)}

STREAMS = [[0, 1], [0]]
PASSES = [(0, 1), (0, 0), (1, 0)]
STEPS = [[(l, s, u, qt) for s in STREAMS[l] for u in range(12) for qt in range(2)] for l in range(DEPTH)]
STEP0 = [0, len(STEPS[0])]
BIASED = {}
for _l in range(DEPTH):
    for _n, (_, _s, _u, _q) in enumerate(STEPS[_l]):
        if _s == 0 and 4 <= _u < 8:
            BIASED[STEP0[_l] + _n] = len(BIASED)

MOD_AT, QKV_AT, MERGE_AT, WOUT_AT, PQ_AT, UV_AT = [], [], [], {}, {}, {}
_p = 0
for _l in range(DEPTH):
    MOD_AT.append(_p); _p += MOD_PAIRS
    QKV_AT.append(_p); _p += QKV_PAIRS
    MERGE_AT.append(_p); _p += MERGE_PAIRS
    WOUT_AT[_l] = _p; _p += WOUT_PAIRS
    for _r, (_pl, _ps) in enumerate(PASSES):
        if _pl == _l:
            PQ_AT[_r] = _p; _p += PQ_PAIRS
            UV_AT[_r] = _p; _p += KEYS
TOTAL_PAIRS = _p

C_G1, C_G2, C_BMOD, C_SUBLN = 0, DC, 2 * DC, 2 * DC + MOD_UNITS
C_LAYER = C_SUBLN + 4
C_GF = DEPTH * C_LAYER
C_COND = C_GF + DC
C_SINK = C_COND + 2 * DC
C_LAM = C_SINK + DEPTH * 8
C_ALL = C_LAM + DEPTH * 4 * HD
K_IDENT, K_ONES, K_IOTA, K_ROT, K_ZERO, K_COS, K_SIN, K_MASK, K_ALL = 0, 128, 256, 384, 512, 640, 896, 1152, 1664


def build(nc, x_in, small_in, const_in_dram, bias_in, stream_in, experts_in, out):
    fp32 = mybir.dt.float32
    u32 = mybir.dt.uint32
    ALU = mybir.AluOpType
    ACT = mybir.ActivationFunctionType
    AX = mybir.AxisListType

    ctx = ExitStack()
    with ctx:
        def sb(name, shape, dt=fp32):
            return ctx.enter_context(nc.sbuf_tensor(name, shape, dt))

        def sem(name):
            return ctx.enter_context(nc.semaphore(name))

        x = sb("x", [P, DC, T])
        h2 = sb("h2", [P, DC, N_LAT])
        ring = sb("ring", [P, RING, PAIR])
        big = sb("big", [P, 32768])
        small = sb("small", [P, C_ALL])
        const = sb("const", [P, K_ALL])
        cond = sb("cond", [P, DC, 2])
        modc = sb("modc", [P, MOD_UNITS, 2])
        a1 = sb("a1", [P, DC, 2])
        a2 = sb("a2", [P, DC, 2])
        stat = sb("stat", [P, 2, 12])
        lam = sb("lam", [P, 8])
        ps = ctx.enter_context(nc.psum_tensor("ps", [P, 8, 512], fp32))

        ident = const[:, K_IDENT:K_IDENT + P]
        ones = const[:, K_ONES:K_ONES + P]
        iota = const[:, K_IOTA:K_IOTA + P]
        rot = const[:, K_ROT:K_ROT + P]
        zero = const[:, K_ZERO:K_ZERO + P]
        cos = const[:, K_COS:K_COS + N_LAT]
        sin = const[:, K_SIN:K_SIN + N_LAT]
        finite = const[:, K_COS:K_COS + 512]
        mask = const[:, K_MASK:K_MASK + 512].rearrange("p (q k) -> p q k", q=2)

        feat = big[:, 0:NU * T].rearrange("p (u t) -> p u t", u=NU)
        o = NU * T
        va = big[:, o:o + TT * 128].rearrange("p (t c) -> p t c", t=TT)
        vb = big[:, o + 512:o + 2560].rearrange("p (t c) -> p t c", t=TT)
        vc = big[:, o + 2560:o + 4608].rearrange("p (t c) -> p t c", t=TT)
        o += 4608
        yt = big[:, o:o + 12 * T].rearrange("p (u t) -> p u t", u=12)
        o += 12 * T
        h1 = big[:, o:o + DC * T].rearrange("p (c t) -> p c t", c=DC)
        o += DC * T
        prob = big[:, o:o + 2048].rearrange("p (b m k) -> p b m k", b=2, m=2)
        probt = big[:, o + 2048:o + 4096].rearrange("p (b m k) -> p b m k", b=2, m=2)
        sq = big[:, o:o + 1024].rearrange("p (b t) -> p b t", b=2)
        rstd = big[:, o + 1024:o + 1536]
        ropet = big[:, o + 1536:o + 2048].rearrange("p (b t) -> p b t", b=2)
        sig = big[:, o + 2048:o + 3072].rearrange("p (b t) -> p b t", b=2)
        prodt = big[:, o + 3072:o + 4096].rearrange("p (b t) -> p b t", b=2)
        o += 4096
        bias = big[:, o:o + 1024].rearrange("p (b m k) -> p b m k", b=2, m=2)
        mt = big[:, 0:DC * T].rearrange("p (c t) -> p c t", c=DC)
        gates = big[:, 0:ROWS * N_LAT].rearrange("p (i t) -> p i t", i=ROWS)
        pq = big[:, 0:16 * N_LAT].rearrange("p (u t) -> p u t", u=16)
        o = 16 * N_LAT
        sv = big[:, o:o + 256].rearrange("p (u k) -> p u k", u=16)
        si = big[:, o + 256:o + 512].bitcast(u32).rearrange("p (u k) -> p u k", u=16)
        sif = big[:, o + 512:o + 768].rearrange("p (u k) -> p u k", u=16)
        work = big[:, o + 768:o + 1792]
        cand = big[:, o + 1792:o + 3840].rearrange("p (h k) -> p h k", h=PH)
        tv = big[:, o + 3840:o + 3968].rearrange("p (h k) -> p h k", h=PH)
        pos = big[:, o + 3968:o + 4096].bitcast(u32)
        pos2 = big[:, o + 4096:o + 4352].bitcast(u32)
        posf = big[:, o + 4352:o + 4608]
        hot = big[:, o + 4608:o + 6656].rearrange("p (h k i) -> p h k i", h=PH, k=TOPK)
        ex = big[:, o + 6656:o + 6784].rearrange("p (h k) -> p h k", h=PH)
        exs = big[:, o + 6784:o + 6800]
        picks = big[:, o + 6912:o + 7680].rearrange("p (b w k) -> p b w k", b=2, w=3)
        o = ROWS * N_LAT
        pickt = big[:, o:o + 768].rearrange("p (w t) -> p w t", w=3)
        o += 768
        hot_i = big[:, o:o + 1024].rearrange("p (b q i) -> p b q i", b=2, q=8)
        o += 1024
        hot_j = big[:, o:o + 2048].rearrange("p (b q j) -> p b q j", b=2, q=8)
        o += 2048
        wts = big[:, o:o + 512].rearrange("p (b t) -> p b t", b=2)
        o += 512
        accs = big[:, o:o + 2048].rearrange("p (b d) -> p b d", b=2)

        arrived = [sem(f"arrived{i}") for i in range(RING)]
        released = sem("released")
        inputs_in = sem("inputs_in")
        bias_arrived = [sem(f"bias_arrived{i}") for i in range(2)]
        cond_ready = sem("cond_ready")
        mod_units_done = sem("mod_units_done")
        mod_ready = sem("mod_ready")
        lam_dots = sem("lam_dots")
        lam_exps = sem("lam_exps")
        lam_ready = sem("lam_ready")
        sq_ready = sem("sq_ready")
        inverse_ready = sem("inverse_ready")
        root_ready = sem("root_ready")
        sq_summed = sem("sq_summed")
        scaled = sem("scaled")
        h_ready = sem("h_ready")
        proj_done = sem("proj_done")
        proj_copied = sem("proj_copied")
        rot_done = sem("rot_done")
        roped = sem("roped")
        v_done = sem("v_done")
        v_copied = sem("v_copied")
        scores_done = sem("scores_done")
        max_ready = sem("max_ready")
        exp_ready = sem("exp_ready")
        prob_ready = sem("prob_ready")
        probt_done = sem("probt_done")
        probt_copied = sem("probt_copied")
        y_done = sem("y_done")
        y_copied = sem("y_copied")
        cn_sq = sem("cn_sq")
        cn_sum = sem("cn_sum")
        cn_ready = sem("cn_ready")
        merge_done = sem("merge_done")
        sig_ready = sem("sig_ready")
        prod_done = sem("prod_done")
        m_ready = sem("m_ready")
        wout_done = sem("wout_done")
        x_ready = sem("x_ready")
        pq_done = sem("pq_done")
        pq_copied = sem("pq_copied")
        keys_done = sem("keys_done")
        topd_ready = sem("topd_ready")
        topexp_ready = sem("topexp_ready")
        picks_ready = sem("picks_ready")
        pickt_done = sem("pickt_done")
        pickt_copied = sem("pickt_copied")
        hot_ready = sem("hot_ready")
        hot_used = sem("hot_used")
        gates_copied = sem("gates_copied")
        s_done = sem("s_done")
        gelu_done = sem("gelu_done")
        w_ready = sem("w_ready")
        acc_done = sem("acc_done")
        acc_copied = sem("acc_copied")
        outt_done = sem("outt_done")
        out_ready = sem("out_ready")
        out_stored = sem("out_stored")
        dve_order = sem("dve_order")
        act_order = sem("act_order")

        def wait_pair(eng, p, i=0):
            eng.wait_ge(arrived[p % RING], i * 16 + 16 * (p // RING + 1))

        def block_of(p, b):
            q = p + b // BLOCKS
            return ring[:, q % RING, (b % BLOCKS) * P:(b % BLOCKS + 1) * P]

        def root_at(n=None, l=None, h=None):
            return (0, 5, 6, 7, 12, 13)[n] if n is not None else (1, 8)[l] + h

        def norm_x(n):
            return [(0, 0, T), (8, N_LAT, T), (16, 0, N_LAT), (24, 0, T), (32, 0, N_LAT), (40, 0, N_LAT)][n]

        block = ctx.enter_context(nc.Block())

        @block.sync
        def _(sp):
            sp.dma_start(small[:, :], small_in).then_inc(inputs_in, 16)

            def load(p, src, i=0):
                if p >= RING or not isinstance(i, int):
                    sp.wait_ge(released, i * RING + (p - RING + 1))
                sp.dma_start(ring[:, p % RING, :], src).then_inc(arrived[p % RING], 16)

            def load_run(p, count, src):
                for k in range(min(count, RING)):
                    load(p + k, src(k))
                rounds = count // RING
                if rounds > 1:
                    with sp.Fori(1, rounds) as i:
                        for k in range(RING):
                            load(p + k, src(i * RING + k), i)
                for k in range(max(rounds, 1) * RING, count):
                    load(p + k, src(k))

            for l in range(DEPTH):
                def weights(first):
                    return lambda k: stream_in[l, k + first, :, :]
                head = MOD_PAIRS + QKV_PAIRS + MERGE_PAIRS + WOUT_PAIRS
                load_run(MOD_AT[l], head, weights(0))
                for r, (pl, s) in enumerate(PASSES):
                    if pl == l:
                        load_run(PQ_AT[r], PQ_PAIRS, weights(head))
                        load_run(UV_AT[r], KEYS, lambda k: experts_in[l, k, :, :])
            sp.wait_ge(out_ready, 1)
            sp.dma_start(out, h2[:, :, :]).then_inc(out_stored, 16)
            sp.wait_ge(out_stored, 16)

        @block.tensor
        def _(pe):
            mm = nc.tensor.matmul

            def mod(l):
                p0 = MOD_AT[l]
                with pe.Fori(0, MOD_PAIRS // RING) as i:
                    for k in range(RING):
                        wait_pair(pe, p0 + k, i)
                        for u in range(2):
                            for c in range(DC):
                                last = mm(ps[:, 7, bass.ds(i * (4 * RING) + (4 * k + 2 * u), 2)],
                                          block_of(p0 + k, u * DC + c), cond[:, c, :],
                                          start=(c == 0), stop=(c == DC - 1))
                            if u == 0:
                                last.then_inc(mod_units_done, 1)
                        last.then_inc(released, 1)

            def sums(n):
                _, c0, c1 = norm_x(n)
                for c in range(DC):
                    m = n * DC + c
                    pe.wait_ge(sq_ready, m + 1)
                    mm(ps[:, 0, 0:c1 - c0], ones, sq[:, c % 2, 0:c1 - c0], start=(c == 0), stop=(c == DC - 1))\
                        .then_inc(sq_summed, 1)

            def proj(l):
                p0 = QKV_AT[l]

                def rotate(r):
                    k = ROPED[r]
                    g = l * len(ROPED) + r
                    pe.wait_ge(proj_copied, l * NU + k + 1)
                    if g >= 2:
                        pe.wait_ge(roped, g - 1)
                    mm(ps[:, 4 + g % 2, 0:N_LAT], rot, feat[:, k, 0:N_LAT], start=True, stop=True)\
                        .then_inc(rot_done, 1)

                turn = 0
                for k, (name, u) in enumerate(UNITS):
                    n = N_LAT if (l == DEPTH - 1 and name[1] == "q") else T
                    if k % 2 == 0:
                        wait_pair(pe, p0 + k // 2)
                    if k == 0:
                        pe.wait_ge(h_ready, (0 if l == 0 else 3) * DC + DC)
                    if k >= 4:
                        pe.wait_ge(proj_copied, l * NU + k - 3)
                    for c in range(DC):
                        last = mm(ps[:, k % 4, 0:n], block_of(p0, k * DC + c), h1[:, c, 0:n],
                                  start=(c == 0), stop=(c == DC - 1))
                    last.then_inc(proj_done, 1)
                    if k % 2 == 1:
                        pe.wait_ge(proj_done, l * NU + k + 1)
                        pe.sem_inc(released, 1)
                    while turn < len(ROPED) and ROPED[turn] < k:
                        rotate(turn)
                        turn += 1
                for t in range(TT):
                    for c in range(DC):
                        last = mm(ps[:, 6, t * P:(t + 1) * P], h1[:, c, t * P:(t + 1) * P],
                                  block_of(p0, NU * DC + c), start=(c == 0), stop=(c == DC - 1))
                last.then_inc(v_done, 1)
                while turn < len(ROPED):
                    rotate(turn)
                    turn += 1
                pe.wait_ge(v_done, 9 * l + 1)
                pe.sem_inc(released, 1)
                for w in range(2):
                    q0 = p0 + 11 + 2 * w
                    if w == 0:
                        pe.wait_ge(proj_copied, l * NU + NU)
                    else:
                        pe.wait_ge(roped, (l + 1) * len(ROPED))
                        pe.wait_ge(v_copied, 9 * l + 1)
                    for c in range(DC):
                        if c % 4 == 0:
                            wait_pair(pe, q0 + c // 4)
                        q = (q0 + c // 4) % RING
                        for t in range(TT):
                            last = mm(ps[:, 4 * w + t, :], h1[:, c, t * P:(t + 1) * P],
                                      ring[:, q, (c % 4) * 512:(c % 4 + 1) * 512],
                                      start=(c == 0), stop=(c == DC - 1))
                            if c == DC - 1 and t < TT - 1:
                                last.then_inc(v_done, 1)
                        if c == 3:
                            last.then_inc(released, 1)
                    last.then_inc(v_done, 1)
                    pe.wait_ge(v_done, 9 * l + 1 + 4 * (w + 1))
                    pe.sem_inc(released, 1)

            def attention(l):
                steps = STEPS[l]

                def keys_of(s):
                    return (0, T) if s == 0 else (N_LAT, T)

                def scores(n):
                    _, s, u, qt = steps[n]
                    a = STEP0[l] + n
                    k0, k1 = keys_of(s)
                    q = UNIT_AT[("abc"[u // 4] + "q", u % 4)]
                    k = UNIT_AT[("abc"[u // 4] + "k", 0 if u < 4 else u % 4)]
                    if n >= 2:
                        pe.wait_ge(exp_ready, a - 1)
                    t0 = s * N_LAT + qt * P
                    for m in range(2):
                        last = mm(ps[:, 2 * (a % 2) + m, 0:k1 - k0], feat[64 * m:64 * m + 64, q, t0:t0 + P],
                                  feat[64 * m:64 * m + 64, k, k0:k1], start=True, stop=True)
                    last.then_inc(scores_done, 1)

                def transposes(n):
                    _, s, u, qt = steps[n]
                    a = STEP0[l] + n
                    k0, k1 = keys_of(s)
                    pe.wait_ge(prob_ready, a + 1)
                    if a >= 1:
                        pe.wait_ge(probt_copied, a)
                    for m in range(2 if u < 8 else 1):
                        for t in range((k1 - k0) // P):
                            last = nc.tensor.transpose(ps[:, 4 + m, t * P:(t + 1) * P],
                                                       prob[:, a % 2, m, t * P:(t + 1) * P], ident)
                    last.then_inc(probt_done, 1)

                def values(n):
                    _, s, u, qt = steps[n]
                    a = STEP0[l] + n
                    k0, k1 = keys_of(s)
                    nt = (k1 - k0) // P
                    pe.wait_ge(probt_copied, a + 1)
                    if a >= 2:
                        pe.wait_ge(y_copied, a - 1)
                    y = ps[:, 6 + a % 2, 0:P]
                    for m in range(2 if u < 8 else 1):
                        for t in range(nt):
                            tile = k0 // P + t
                            if u < 4:
                                v, rows = va[:, tile, 64 * m:64 * m + 64], slice(64 * m, 64 * m + 64)
                            elif u < 8:
                                c0 = 128 * (u - 4) + 64 * m
                                v, rows = vb[:, tile, c0:c0 + 64], slice(64 * m, 64 * m + 64)
                            else:
                                v, rows = vc[:, tile, 128 * (u - 8):128 * (u - 7)], slice(0, 128)
                            last = mm(y[rows, :], v, probt[:, a % 2, m, t * P:(t + 1) * P],
                                      start=(t == 0), stop=(t == nt - 1))
                    last.then_inc(y_done, 1)

                pe.wait_ge(roped, (l + 1) * len(ROPED))
                pe.wait_ge(v_copied, 9 * (l + 1))
                scores(0)
                scores(1)
                for n in range(len(steps)):
                    transposes(n)
                    if n + 2 < len(steps):
                        scores(n + 2)
                    values(n)

            def head_norm(l):
                n = T if len(STREAMS[l]) == 2 else N_LAT
                for h in range(4):
                    g = 4 * l + h
                    pe.wait_ge(cn_sq, g + 1)
                    mm(ps[:, h, 0:n], ones, sq[:, h % 2, 0:n], start=True, stop=True).then_inc(cn_sum, 1)

            def merge(l):
                n = T if len(STREAMS[l]) == 2 else N_LAT
                p0 = MERGE_AT[l]
                pe.wait_ge(cn_ready, 4 * (l + 1))
                b = 0
                for item in range(6 * DC):
                    g = 6 * DC * l + item
                    branch = item % 6 // 2
                    bank = item % 8
                    if item >= 8:
                        pe.wait_ge(prod_done, 3 * DC * l + (item - 8) // 2 + 1)
                    count = DC if item % 2 == 0 else 4
                    for c in range(count):
                        if b % BLOCKS == 0:
                            wait_pair(pe, p0 + b // BLOCKS)
                        src = h1[:, c, 0:n] if item % 2 == 0 else yt[:, 4 * branch + c, 0:n]
                        last = mm(ps[:, bank, 0:n], block_of(p0, b), src, start=(c == 0), stop=(c == count - 1))
                        b += 1
                        if b % BLOCKS == 0:
                            if c == count - 1:
                                last.then_inc(merge_done, 1)
                                pe.wait_ge(merge_done, g + 1)
                                pe.sem_inc(released, 1)
                            else:
                                last.then_inc(released, 1)
                        elif c == count - 1:
                            last.then_inc(merge_done, 1)

            def w_out(l):
                n = T if len(STREAMS[l]) == 2 else N_LAT
                p0 = WOUT_AT[l]
                pe.wait_ge(m_ready, DC * (l + 1))
                for j in range(DC):
                    if j % 2 == 0:
                        wait_pair(pe, p0 + j // 2)
                    for c in range(DC):
                        last = mm(ps[:, j, 0:n], block_of(p0, j * DC + c), mt[:, c, 0:n],
                                  start=(c == 0), stop=(c == DC - 1))
                    last.then_inc(wout_done, 1)
                    if j % 2 == 1:
                        pe.wait_ge(wout_done, DC * l + j + 1)
                        pe.sem_inc(released, 1)

            def peer(r):
                p0 = PQ_AT[r]
                pe.wait_ge(h_ready, (1, 2, 4)[r] * DC + DC)
                for u in range(16):
                    if u % 2 == 0:
                        wait_pair(pe, p0 + u // 2)
                    if u >= 4:
                        pe.wait_ge(pq_copied, 16 * r + u - 3)
                    for c in range(DC):
                        last = mm(ps[:, u % 4, 0:N_LAT], block_of(p0, u * DC + c), h2[:, c, :],
                                  start=(c == 0), stop=(c == DC - 1))
                    last.then_inc(pq_done, 1)
                    if u % 2 == 1:
                        pe.wait_ge(pq_done, 16 * r + u + 1)
                        pe.sem_inc(released, 1)
                wait_pair(pe, p0 + 8)
                pe.wait_ge(pq_copied, 16 * (r + 1))
                for tt in range(2):
                    for u in range(16):
                        last = mm(ps[:, 4 * (1 - tt) + u // 4, (u % 4) * P:(u % 4 + 1) * P],
                                  pq[:, u, tt * P:(tt + 1) * P], block_of(p0 + 8, u), start=True, stop=True)
                        if u % 4 == 3:
                            last.then_inc(keys_done, 1)
                pe.wait_ge(keys_done, 8 * (r + 1))
                pe.sem_inc(released, 1)
                for tt in range(2):
                    pe.wait_ge(picks_ready, 2 * r + tt + 1)
                    for w in range(3):
                        last = nc.tensor.transpose(ps[:, 4 * (1 - tt), w * P:(w + 1) * P], picks[:, tt, w, :], ident)
                    last.then_inc(pickt_done, 1)
                pe.wait_ge(pickt_copied, 2 * (r + 1))
                for b in range(4):
                    mm(ps[:, 4 + b, :], zero, finite, start=True, stop=False)

                for half in range(HALVES):
                    g0 = (r * HALVES + half) * 32
                    n0 = (r * HALVES + half) * ROWS
                    q0 = UV_AT[r] + half * ROWS

                    def gate_group(i, k):
                        pe.wait_ge(hot_ready, i * 2 + (g0 + k + 1))
                        if not isinstance(i, int) or g0 + k >= 2:
                            pe.wait_ge(gates_copied, i * 2 + (g0 + k - 1))
                        for q in range(8):
                            last = mm(ps[:, k, q * ROWS:(q + 1) * ROWS], hot_j[:, k, q, :], hot_i[:, k, q, :],
                                      start=True, stop=True)
                        last.then_inc(hot_used, 1)

                    for k in range(2):
                        gate_group(0, k)
                    with pe.Fori(1, 16) as i:
                        for k in range(2):
                            gate_group(i, k)
                    pe.wait_ge(gates_copied, g0 + 32)

                    def expert_scores(i, k):
                        wait_pair(pe, q0 + k, i)
                        if not isinstance(i, int) or n0 + k >= 4:
                            pe.wait_ge(w_ready, i * 4 + (n0 + k - 3))
                        for c in range(DC):
                            last = mm(ps[:, k, 0:N_LAT], block_of(q0 + k, c), h2[:, c, :],
                                      start=(c == 0), stop=(c == DC - 1))
                        last.then_inc(s_done, 1)

                    def expert_values(i, k):
                        pe.wait_ge(w_ready, i * 4 + (n0 + k + 1))
                        for tt in range(2):
                            for d in range(2):
                                last = mm(ps[:, 4 + 2 * tt + d, :], wts[:, k % 2, tt * P:(tt + 1) * P],
                                          ring[:, (q0 + k) % RING, D + 512 * d:D + 512 * (d + 1)],
                                          start=False, stop=False)
                        last.then_inc(released, 1)

                    expert_scores(0, 0)
                    for k in range(1, 4):
                        expert_scores(0, k)
                        expert_values(0, k - 1)
                    with pe.Fori(1, ROWS // 4) as i:
                        for k in range(4):
                            expert_scores(i, k)
                            if k == 0:
                                expert_values(i - 1, 3)
                            else:
                                expert_values(i, k - 1)
                    expert_values(ROWS // 4 - 1, 3)
                for b in range(4):
                    last = mm(ps[:, 4 + b, :], zero, finite, start=False, stop=True)
                last.then_inc(acc_done, 1)
                for c in range(DC):
                    if c == 0:
                        pe.wait_ge(acc_copied, 4 * (r + 1))
                    for tt in range(2):
                        o = (c % 2) * 256 + tt * P
                        last = nc.tensor.transpose(ps[:, c // 2, o:o + P], accs[:, tt, c * P:(c + 1) * P], ident)
                    if c % 2 == 1:
                        last.then_inc(outt_done, 1)

            pe.wait_ge(inputs_in, 48)
            pe.wait_ge(cond_ready, 1)
            n = 0
            for l in range(DEPTH):
                mod(l)
                sums((0, 3)[l])
                proj(l)
                attention(l)
                head_norm(l)
                merge(l)
                w_out(l)
                for r, (pl, s) in enumerate(PASSES):
                    if pl == l:
                        sums((1, 2, 4)[r])
                        peer(r)
            sums(5)

        @block.scalar
        def _(act):
            act.dma_start(const[:, :], const_in_dram).then_inc(inputs_in, 16)
            act.dma_start(x[:, :, :], x_in).then_inc(inputs_in, 16)
            order = [0]

            def link(ins):
                order[0] += 1
                ins.then_inc(act_order, 1)
                act.wait_ge(act_order, order[0])

            def root(at, w):
                act.wait_ge(inverse_ready, at + 1)
                nc.scalar.activation(rstd[:, 0:w], rstd[:, 0:w], ACT.Sqrt).then_inc(root_ready, 1)

            def squares(n):
                need, c0, c1 = norm_x(n)
                if need:
                    act.wait_ge(x_ready, need)
                for c in range(DC):
                    m = n * DC + c
                    if m >= 2:
                        act.wait_ge(sq_summed, m - 1)
                    nc.scalar.activation(sq[:, c % 2, 0:c1 - c0], x[:, c, c0:c1], ACT.Square).then_inc(sq_ready, 1)
                root(root_at(n), c1 - c0)

            def shifts(n, l, kind, streams, dst):
                for c in range(DC):
                    act.wait_ge(scaled, n * DC + c + 1)
                    for at, s in enumerate(streams):
                        o = dst[:, c, at * N_LAT:(at + 1) * N_LAT]
                        last = nc.scalar.activation(o, o, ACT.Identity, bias=modc[:, kind * DC + c, s:s + 1])
                    last.then_inc(h_ready, 1)

            act.wait_ge(inputs_in, 48)
            nc.scalar.activation(cond[:, :, :], small[:, C_COND:C_COND + 2 * DC].rearrange("p (c s) -> p c s", s=2),
                                 ACT.Silu).then_inc(cond_ready, 1)
            for l in range(DEPTH):
                streams = STREAMS[l]
                n = T if len(streams) == 2 else N_LAT
                act.wait_ge(lam_dots, l + 1)
                nc.scalar.activation(lam[:, 2:4], lam[:, 0:2], ACT.Exp).then_inc(lam_exps, 1)
                squares((0, 3)[l])
                shifts((0, 3)[l], l, 0, [0, 1], h1)
                for k, (name, u) in enumerate(UNITS):
                    w = N_LAT if (l == DEPTH - 1 and name[1] == "q") else T
                    act.wait_ge(proj_done, l * NU + k + 1)
                    nc.scalar.activation(feat[:, k, 0:w], ps[:, k % 4, 0:w], ACT.Copy,
                                         scale=HD ** -0.5 if name[1] == "q" else 1.0).then_inc(proj_copied, 1)
                steps = STEPS[l]

                def exps(i):
                    _, s, u, qt = steps[i]
                    a = STEP0[l] + i
                    nk = T if s == 0 else N_CTX
                    act.wait_ge(max_ready, a + 1)
                    if i >= 2:
                        act.wait_ge(probt_done, a - 1)
                    st = stat[:, a % 2, :]
                    if u < 4:
                        nc.scalar.activation(st[:, 6:8], st[:, 10:12], ACT.Exp)
                    for m in range(2):
                        last = nc.scalar.activation(prob[:, a % 2, m, 0:nk], ps[:, 2 * (a % 2) + m, 0:nk], ACT.Exp,
                                                    bias=st[:, 2 + m:3 + m], accum_out=st[:, 4 + m:5 + m])
                    last.then_inc(exp_ready, 1)

                def copy_probt(i):
                    _, s, u, qt = steps[i]
                    a = STEP0[l] + i
                    nk = T if s == 0 else N_CTX
                    m = 2 if u < 8 else 1
                    act.wait_ge(probt_done, a + 1)
                    if a >= 2:
                        act.wait_ge(y_done, a - 1)
                    nc.scalar.activation(probt[:, a % 2, 0:m, 0:nk], ps[:, 4:4 + m, 0:nk], ACT.Copy)\
                        .then_inc(probt_copied, 1)

                exps(0)
                for i in range(len(steps)):
                    if i + 1 < len(steps):
                        exps(i + 1)
                    copy_probt(i)
                act.wait_ge(y_copied, STEP0[l] + len(steps))
                for h in range(4):
                    if h >= 2:
                        act.wait_ge(cn_sum, 4 * l + h - 1)
                    nc.scalar.activation(sq[:, h % 2, 0:n], yt[:, 8 + h, 0:n], ACT.Square).then_inc(cn_sq, 1)
                    if h >= 1:
                        root(root_at(l=l, h=h - 1), n)
                root(root_at(l=l, h=3), n)
                for g in range(3 * DC):
                    m = 3 * DC * l + g
                    act.wait_ge(merge_done, 6 * DC * l + 2 * g + 1)
                    if g >= 2:
                        act.wait_ge(prod_done, m - 1)
                    nc.scalar.activation(sig[:, g % 2, 0:n], ps[:, (2 * g) % 8, 0:n], ACT.Sigmoid)\
                        .then_inc(sig_ready, 1)
                for r, (pl, s) in enumerate(PASSES):
                    if pl != l:
                        continue
                    squares((1, 2, 4)[r])
                    shifts((1, 2, 4)[r], l, 3, [s], h2)
                    for u in range(16):
                        act.wait_ge(pq_done, 16 * r + u + 1)
                        nc.scalar.activation(pq[:, u, :], ps[:, u % 4, 0:N_LAT], ACT.Copy).then_inc(pq_copied, 1)
                    for tt in range(2):
                        act.wait_ge(topd_ready, 2 * r + tt + 1)
                        nc.scalar.activation(ex, tv, ACT.Exp).then_inc(topexp_ready, 1)
                        act.wait_ge(pickt_done, 2 * r + tt + 1)
                        nc.scalar.activation(pickt[:, :, tt * P:(tt + 1) * P],
                                             ps[:, 4 * (1 - tt), 0:3 * P].rearrange("p (w t) -> p w t", w=3),
                                             ACT.Copy).then_inc(pickt_copied, 1)
                    for half in range(HALVES):
                        g0 = (r * HALVES + half) * 32
                        n0 = (r * HALVES + half) * ROWS

                        def copy_gates(i, k):
                            act.wait_ge(hot_used, i * 2 + (g0 + k + 1))
                            nc.scalar.activation(gates[:, :, bass.ds(i * 16 + k * 8, 8)],
                                                 ps[:, k, :].rearrange("p (q i) -> p i q", q=8),
                                                 ACT.Copy).then_inc(gates_copied, 1)

                        if half:
                            act.wait_ge(w_ready, n0)
                        for k in range(2):
                            copy_gates(0, k)
                        with act.Fori(1, 16) as i:
                            for k in range(2):
                                copy_gates(i, k)
                        with act.Fori(0, ROWS // 4) as i:
                            for k in range(4):
                                act.wait_ge(s_done, i * 4 + (n0 + k + 1))
                                nc.scalar.activation(ps[:, k, 0:N_LAT], ps[:, k, 0:N_LAT], ACT.Gelu)\
                                    .then_inc(gelu_done, 1)
                    act.wait_ge(acc_done, r + 1)
                    for b in range(4):
                        nc.scalar.activation(accs[:, b // 2, (b % 2) * 512:(b % 2 + 1) * 512], ps[:, 4 + b, :],
                                             ACT.Copy).then_inc(acc_copied, 1)
            squares(5)

        @block.gpsimd
        def _(pool):
            for l in range(DEPTH):
                for a, b in BIASED.items():
                    if (a >= STEP0[1]) != (l == 1):
                        continue
                    if b % 8 >= 2:
                        back = [k for k, v in BIASED.items() if v == b - 2][0]
                        pool.wait_ge(max_ready, back + 1)
                    elif l > 0:
                        pool.wait_ge(h_ready, 3 * DC + DC)
                    u = b % 8
                    pool.dma_start(bias[:, b % 2, :, :], bias_in[l, u // 2, u % 2, :, :, :])\
                        .then_inc(bias_arrived[b % 2], 16)

        @block.vector
        def _(dve):
            v = nc.vector
            order = [0]

            def link(ins):
                order[0] += 1
                ins.then_inc(dve_order, 1)
                dve.wait_ge(dve_order, order[0])

            def inverse_root(at, src, dst, count):
                link(v.tensor_scalar(dst, src, 1.0 / count, EPS, ALU.mult, ALU.add))
                v.reciprocal(dst, dst).then_inc(inverse_ready, 1)
                dve.wait_ge(root_ready, at + 1)

            def norm(n, gain, streams, dst):
                need, c0, c1 = norm_x(n)
                dve.wait_ge(sq_summed, (n + 1) * DC)
                inverse_root(root_at(n), ps[:, 0, 0:c1 - c0], rstd[:, 0:c1 - c0], D)
                for c in range(DC):
                    for at, s in enumerate(streams):
                        cols = slice(at * N_LAT, (at + 1) * N_LAT)
                        last = v.scalar_tensor_tensor(dst[:, c, cols], x[:, c, c0 + at * N_LAT:c0 + (at + 1) * N_LAT],
                                                      gain[:, c, s:s + 1], rstd[:, cols], ALU.mult, ALU.mult)
                    last.then_inc(scaled, 1)

            def modulation(l):
                base = l * C_LAYER
                sm = small[:, C_LAM + l * 4 * HD:C_LAM + (l + 1) * 4 * HD]
                for d in range(2):
                    last = v.tensor_tensor_reduce(out=rstd[:, d * HD:(d + 1) * HD], in0=sm[:, 2 * d * HD:(2 * d + 1) * HD],
                                                  in1=sm[:, (2 * d + 1) * HD:(2 * d + 2) * HD], scale=1.0, scalar=0.0,
                                                  op0=ALU.mult, op1=ALU.add, accum_out=lam[:, d:d + 1])
                last.then_inc(lam_dots, 1)
                dve.wait_ge(lam_exps, l + 1)
                link(v.tensor_tensor(lam[:, 4:5], lam[:, 3:4], lam[:, 2:3], ALU.subtract))
                v.tensor_scalar(lam[:, 5:6], lam[:, 4:5], -LAM_INIT[l], None, ALU.add).then_inc(lam_ready, 1)
                dve.wait_ge(mod_units_done, MOD_PAIRS * (l + 1))
                dve.wait_ge(released, MOD_AT[l] + MOD_PAIRS)
                link(v.tensor_tensor(modc[:, :, :], ps[:, 7, 0:2 * MOD_UNITS].rearrange("p (u s) -> p u s", s=2),
                                     small[:, base + C_BMOD:base + C_BMOD + MOD_UNITS].unsqueeze(2)
                                     .to_broadcast([P, MOD_UNITS, 2]), ALU.add))
                for kind, gcol, dst in ((1, C_G1, a1), (4, C_G2, a2)):
                    last = v.scalar_tensor_tensor(dst[:, :, :], modc[:, kind * DC:(kind + 1) * DC, :], 1.0,
                                                  small[:, base + gcol:base + gcol + DC].unsqueeze(2)
                                                  .to_broadcast([P, DC, 2]), ALU.add, ALU.mult)
                last.then_inc(mod_ready, 1)
                dve.wait_ge(mod_ready, l + 1)

            def rope(l):
                for r, k in enumerate(ROPED):
                    g = l * len(ROPED) + r
                    dve.wait_ge(rot_done, g + 1)
                    t = ropet[:, g % 2, :]
                    f = feat[:, k, 0:N_LAT]
                    v.tensor_tensor(t, ps[:, 4 + g % 2, 0:N_LAT], sin, ALU.mult)
                    link(v.tensor_tensor(f, f, cos, ALU.mult))
                    v.tensor_tensor(f, f, t, ALU.add).then_inc(roped, 1)
                dve.wait_ge(v_done, 9 * l + 1)
                v.tensor_copy(va, ps[:, 6, :].rearrange("p (t c) -> p t c", t=TT)).then_inc(v_copied, 1)
                for w, dst in enumerate((vb, vc)):
                    for t in range(TT):
                        dve.wait_ge(v_done, 9 * l + 2 + 4 * w + t)
                        v.tensor_copy(dst[:, t, :], ps[:, 4 * w + t, :]).then_inc(v_copied, 1)

            def attention(l):
                steps = STEPS[l]
                sinks = small[:, C_SINK + 8 * l:C_SINK + 8 * (l + 1)]

                def maxima(i):
                    _, s, u, qt = steps[i]
                    a = STEP0[l] + i
                    nk = T if s == 0 else N_CTX
                    st = stat[:, a % 2, :]
                    b = 2 * (a % 2)
                    dve.wait_ge(scores_done, a + 1)
                    if s == 0 and u < 8:
                        if u < 4:
                            add = mask[:, qt, :].unsqueeze(1).to_broadcast([P, 2, N_LAT])
                        else:
                            tile = BIASED[a]
                            dve.wait_ge(bias_arrived[tile % 2], 16 * (tile // 2 + 1))
                            add = bias[:, tile % 2, :, :]
                        link(v.tensor_tensor(ps[:, b:b + 2, 0:N_LAT], ps[:, b:b + 2, 0:N_LAT], add, ALU.add))
                    link(v.tensor_reduce(st[:, 0:2], ps[:, b:b + 2, 0:nk], AX.X, ALU.max))
                    if u < 4:
                        link(v.tensor_tensor(st[:, 0:2], st[:, 0:2], sinks[:, 2 * u:2 * u + 2], ALU.max))
                        v.tensor_tensor(st[:, 10:12], sinks[:, 2 * u:2 * u + 2], st[:, 0:2], ALU.subtract)
                    v.tensor_scalar(st[:, 2:4], st[:, 0:2], -1.0, None, ALU.mult).then_inc(max_ready, 1)

                def normalise(i):
                    _, s, u, qt = steps[i]
                    a = STEP0[l] + i
                    nk = T if s == 0 else N_CTX
                    st = stat[:, a % 2, :]
                    dve.wait_ge(exp_ready, a + 1)
                    if u < 4:
                        link(v.tensor_tensor(st[:, 4:6], st[:, 4:6], st[:, 6:8], ALU.add))
                    link(v.reciprocal(st[:, 8:10], st[:, 4:6]))
                    p0, p1 = prob[:, a % 2, 0, 0:nk], prob[:, a % 2, 1, 0:nk]
                    if u < 8:
                        v.tensor_scalar(p0, p0, st[:, 8:9], None, ALU.mult)
                        v.tensor_scalar(p1, p1, st[:, 9:10], None, ALU.mult).then_inc(prob_ready, 1)
                    else:
                        link(v.tensor_scalar(p1, p1, st[:, 9:10], lam[:, 5:6], ALU.mult, ALU.mult))
                        v.scalar_tensor_tensor(p0, p0, st[:, 8:9], p1, ALU.mult, ALU.add).then_inc(prob_ready, 1)

                def copy_y(i):
                    _, s, u, qt = steps[i]
                    a = STEP0[l] + i
                    dve.wait_ge(y_done, a + 1)
                    t0 = s * N_LAT + qt * P
                    v.tensor_copy(yt[:, u, t0:t0 + P], ps[:, 6 + a % 2, 0:P]).then_inc(y_copied, 1)

                maxima(0)
                for i in range(len(steps)):
                    if i + 1 < len(steps):
                        maxima(i + 1)
                    normalise(i)
                    if i >= 1:
                        copy_y(i - 1)
                copy_y(len(steps) - 1)

            def head_norm(l):
                n = T if len(STREAMS[l]) == 2 else N_LAT
                for h in range(4):
                    dve.wait_ge(cn_sum, 4 * l + h + 1)
                    inverse_root(root_at(l=l, h=h), ps[:, h, 0:n], rstd[:, 0:n], P)
                    link(v.scalar_tensor_tensor(yt[:, 8 + h, 0:n], yt[:, 8 + h, 0:n],
                                                small[:, l * C_LAYER + C_SUBLN + h:l * C_LAYER + C_SUBLN + h + 1],
                                                rstd[:, 0:n], ALU.mult, ALU.mult))
                    v.tensor_scalar(yt[:, 8 + h, 0:n], yt[:, 8 + h, 0:n], 1.0 - LAM_INIT[l], None, ALU.mult)\
                        .then_inc(cn_ready, 1)

            def merge(l):
                n = T if len(STREAMS[l]) == 2 else N_LAT
                for j in range(DC):
                    for b in range(3):
                        g = 3 * j + b
                        m = 3 * DC * l + g
                        dve.wait_ge(sig_ready, m + 1)
                        dve.wait_ge(merge_done, 6 * DC * l + 2 * g + 2)
                        dst = mt[:, j, 0:n] if b == 0 else prodt[:, b % 2, 0:n]
                        v.tensor_tensor(dst, ps[:, (2 * g + 1) % 8, 0:n], sig[:, g % 2, 0:n], ALU.mult)\
                            .then_inc(prod_done, 1)
                        if b:
                            dve.wait_ge(prod_done, m + 1)
                            add = v.tensor_tensor(mt[:, j, 0:n], mt[:, j, 0:n], dst, ALU.add)
                            if b == 1:
                                link(add)
                            else:
                                add.then_inc(m_ready, 1)
                for j in range(DC):
                    dve.wait_ge(wout_done, DC * l + j + 1)
                    for at, s in enumerate(STREAMS[l]):
                        cols = slice(at * N_LAT, (at + 1) * N_LAT)
                        last = v.scalar_tensor_tensor(x[:, j, cols], ps[:, j, cols], modc[:, 2 * DC + j, s:s + 1],
                                                      x[:, j, cols], ALU.mult, ALU.add)
                    last.then_inc(x_ready, 1)

            def top16(srcs, values, indices):
                for q in range(0, len(srcs), 4):
                    four = range(q, q + 4)
                    size = 1024 // 4
                    for u in four:
                        last = v.max(values[u][:, 0:8], srcs[u])
                    link(last)
                    for u in four:
                        w = work[:, (u - q) * size:(u - q) * size + srcs[u].shape[-1]]
                        last = v.match_replace(w, values[u][:, 0:8], srcs[u], USED)
                    link(last)
                    for u in four:
                        w = work[:, (u - q) * size:(u - q) * size + srcs[u].shape[-1]]
                        last = v.max(values[u][:, 8:16], w)
                    link(last)
                    for u in four:
                        w = work[:, (u - q) * size:(u - q) * size + srcs[u].shape[-1]]
                        v.max_index(indices[u][:, 0:8], values[u][:, 0:8], srcs[u])
                        last = v.max_index(indices[u][:, 8:16], values[u][:, 8:16], w)
                link(last)

            def picks_of(r, tt):
                for q in range(4):
                    dve.wait_ge(keys_done, 8 * r + 4 * tt + q + 1)
                srcs = [ps[:, 4 * (1 - tt) + u // 4, (u % 4) * P:(u % 4 + 1) * P] for u in range(16)]
                top16(srcs, [sv[:, u, :] for u in range(16)], [si[:, u, :] for u in range(16)])
                v.tensor_copy(sif, si)
                sides = sv.rearrange("p (h w) k -> p h w k", w=2)
                first = sides[:, :, 0, :].unsqueeze(3).to_broadcast([P, PH, TOPK, TOPK])
                second = sides[:, :, 1, :].unsqueeze(2).to_broadcast([P, PH, TOPK, TOPK])
                link(v.tensor_tensor(cand.rearrange("p h (i j) -> p h i j", i=TOPK), first, second, ALU.add))
                pos3 = pos.rearrange("p (h k) -> p h k", h=PH)
                top16([cand[:, h, :] for h in range(PH)], [tv[:, h, :] for h in range(PH)],
                      [pos3[:, h, :] for h in range(PH)])
                v.tensor_copy(exs[:, 8:16], tv[:, :, 0])
                v.tensor_scalar(pos2[:, 0:HK], pos, 4, None, ALU.logical_shift_right)
                link(v.tensor_scalar(pos2[:, HK:2 * HK], pos, 15, None, ALU.bitwise_and))
                v.tensor_tensor(tv, tv, exs[:, 8:16].unsqueeze(2).to_broadcast([P, PH, TOPK]), ALU.subtract)\
                    .then_inc(topd_ready, 1)
                link(v.tensor_copy(posf, pos2))
                steps16 = iota[:, 0:TOPK].unsqueeze(1).unsqueeze(1).to_broadcast([P, PH, TOPK, TOPK])
                halves = sif.rearrange("p (h w) k -> p h w k", w=2)
                for w in range(2):
                    at = posf[:, w * HK:(w + 1) * HK].rearrange("p (h k) -> p h k", h=PH)
                    link(v.tensor_tensor(hot, steps16, at.unsqueeze(3).to_broadcast([P, PH, TOPK, TOPK]),
                                         ALU.is_equal))
                    link(v.tensor_tensor(hot, hot, halves[:, :, w, :].unsqueeze(2)
                                         .to_broadcast([P, PH, TOPK, TOPK]), ALU.mult))
                    link(v.tensor_reduce(picks[:, tt, w, :].rearrange("p (h k) -> p h k", h=PH), hot, AX.X, ALU.add))
                dve.wait_ge(topexp_ready, 2 * r + tt + 1)
                link(v.tensor_reduce(exs[:, 0:8], ex, AX.X, ALU.add))
                link(v.reciprocal(exs[:, 8:16], exs[:, 0:8]))
                v.tensor_tensor(picks[:, tt, 2, :].rearrange("p (h k) -> p h k", h=PH), ex,
                                exs[:, 8:16].unsqueeze(2).to_broadcast([P, PH, TOPK]), ALU.mult)\
                    .then_inc(picks_ready, 1)

            def peer(r, l, s):
                for tt in range(2):
                    picks_of(r, tt)
                dve.wait_ge(pickt_copied, 2 * (r + 1))
                for half in range(HALVES):
                    g0 = (r * HALVES + half) * 32
                    n0 = (r * HALVES + half) * ROWS
                    q0 = UV_AT[r] + half * ROWS

                    def rows(i, k):
                        if not isinstance(i, int) or g0 + k >= 2:
                            dve.wait_ge(hot_used, i * 2 + (g0 + k - 1))
                        for q in range(8):
                            t = i * 16 + (k * 8 + q)
                            v.tensor_scalar(hot_j[:, k, q, :], iota, pickt[:, 1, bass.ds(t, 1)], None, ALU.is_equal)
                            last = v.tensor_scalar(hot_i[:, k, q, :], iota[:, half * ROWS:(half + 1) * ROWS],
                                                   pickt[:, 0, bass.ds(t, 1)], pickt[:, 2, bass.ds(t, 1)],
                                                   ALU.is_equal, ALU.mult)
                        last.then_inc(hot_ready, 1)

                    for k in range(2):
                        rows(0, k)
                    with dve.Fori(1, 16) as i:
                        for k in range(2):
                            rows(i, k)
                    dve.wait_ge(gates_copied, g0 + 32)

                    def weigh(i, k):
                        dve.wait_ge(gelu_done, i * 4 + (n0 + k + 1))
                        if not isinstance(i, int) or k >= 2:
                            dve.wait_ge(released, i * 4 + (q0 + k - 1))
                        v.tensor_tensor(wts[:, k % 2, :], ps[:, k, 0:N_LAT], gates[:, i * 4 + k, :], ALU.mult)\
                            .then_inc(w_ready, 1)

                    for k in range(4):
                        weigh(0, k)
                    with dve.Fori(1, ROWS // 4) as i:
                        for k in range(4):
                            weigh(i, k)
                for c in range(DC):
                    dve.wait_ge(outt_done, DC // 2 * r + c // 2 + 1)
                    o = (c % 2) * 256
                    cols = slice(s * N_LAT, (s + 1) * N_LAT)
                    v.scalar_tensor_tensor(x[:, c, cols], ps[:, c // 2, o:o + N_LAT], modc[:, 5 * DC + c, s:s + 1],
                                           x[:, c, cols], ALU.mult, ALU.add).then_inc(x_ready, 1)

            dve.wait_ge(inputs_in, 48)
            for l in range(DEPTH):
                modulation(l)
                norm((0, 3)[l], a1, [0, 1], h1)
                rope(l)
                attention(l)
                head_norm(l)
                merge(l)
                for r, (pl, s) in enumerate(PASSES):
                    if pl == l:
                        norm((1, 2, 4)[r], a2, [s], h2)
                        peer(r, l, s)
            dve.wait_ge(sq_summed, 6 * DC)
            inverse_root(root_at(5), ps[:, 0, 0:N_LAT], rstd[:, 0:N_LAT], D)
            for c in range(DC):
                last = v.scalar_tensor_tensor(h2[:, c, :], x[:, c, 0:N_LAT], small[:, C_GF + c:C_GF + c + 1],
                                              rstd[:, 0:N_LAT], ALU.mult, ALU.mult)
            last.then_inc(out_ready, 1)


IN_SPLITS = (512, 128, 128, 512, 512, 512, 512, 512, 512, 1024, 1024, 1024)


def blocks(w):
    return w.reshape(-1, P, P).transpose(1, 0, 2)


def head_order():
    return np.concatenate([np.arange(h * HD, (h + 1) * HD) for u in range(4) for h in (u, u + 4)])


def weight_stream(w_mod, w_in, wa, wb, wc, w_out, wq, keys):
    at = np.concatenate([[0], np.cumsum(IN_SPLITS)])
    part = [w_in[:, at[i]:at[i + 1]] for i in range(len(IN_SPLITS))]
    part[0] = part[0][:, head_order()]
    wa = wa[head_order(), :]
    out = [blocks(w_mod[:, u * P:(u + 1) * P]) for u in range(MOD_UNITS)]
    which = {"aq": 0, "ak": 1, "bq": 3, "bk": 4, "cq": 6, "ck": 7}
    out += [blocks(part[which[name]][:, u * P:(u + 1) * P]) for name, u in UNITS]
    out.append(blocks(part[2]))
    for i in (5, 8):
        out.append(part[i].reshape(DC, P, 4, P).transpose(1, 0, 2, 3).reshape(P, 4 * DC, P))
    for j in range(DC):
        cols = slice(j * P, (j + 1) * P)
        for gate, branch in ((9, wa), (10, wb), (11, wc)):
            out += [blocks(part[gate][:, cols]), blocks(branch[:, cols])]
    out += [blocks(w_out[:, j * P:(j + 1) * P]) for j in range(DC)]
    out += [blocks(wq[:, u * P:(u + 1) * P]) for u in range(16)]
    out.append(keys.reshape(16, KEYS, P).transpose(2, 0, 1))
    whole = np.concatenate(out, axis=1)
    return np.ascontiguousarray(whole.reshape(P, -1, BLOCKS * P).transpose(1, 0, 2))


def expert_pairs(u, v):
    ut = u.reshape(DEPTH, KEYS, KEYS, DC, P).transpose(0, 1, 4, 3, 2).reshape(DEPTH, KEYS, P, D)
    return np.concatenate([ut, v.reshape(DEPTH, KEYS, KEYS, D)], axis=3)


def bias_tiles(rpb):
    t = np.arange(N_LAT)
    row, col = t // GRID_W, t % GRID_W
    start = np.clip(col - 8, 0, GRID_W - 16)
    inside = (col[None, :] >= start[:, None]) & (col[None, :] < start[:, None] + 16)
    dr = row[None, :] - row[:, None] + 7
    dc = np.clip(col[None, :] - col[:, None], -15, 15) + 15
    n = rpb.shape[2] * rpb.shape[3]
    padded = np.concatenate([rpb.reshape(DEPTH, 8, n), np.full((DEPTH, 8, 1), NEG, rpb.dtype)], axis=2)
    full = padded[:, :, np.where(inside, dr * rpb.shape[3] + dc, n)]
    return np.ascontiguousarray(full.reshape(DEPTH, 4, 2, 2, P, N_LAT).transpose(0, 1, 3, 4, 2, 5))


def columns(v):
    return v.reshape(-1, P).T


def constants():
    out = np.zeros((P, K_ALL), np.float32)
    out[:, K_IDENT:K_IDENT + P] = np.eye(P)
    out[:, K_ONES:K_ONES + P] = 1.0
    out[:, K_IOTA:K_IOTA + P] = np.arange(P)
    for f in range(P):
        if f % HD < HD // 2:
            out[f + HD // 2, K_ROT + f] = -1.0
        else:
            out[f - HD // 2, K_ROT + f] = 1.0
    t = np.arange(N_LAT)
    n_freq = HD // 4
    inv = np.float32(10000.0) ** (-np.arange(n_freq, dtype=np.float32) / np.float32(n_freq))
    ang = np.concatenate([(t // GRID_W).astype(np.float32)[:, None] * inv,
                          (t % GRID_W).astype(np.float32)[:, None] * inv], axis=1)
    f = np.arange(P) % (HD // 2)
    out[:, K_COS:K_COS + N_LAT] = np.cos(ang).T[f]
    out[:, K_SIN:K_SIN + N_LAT] = np.sin(ang).T[f]
    far = np.abs(t[:, None] - t[None, :]) > 128
    out[:, K_MASK:K_MASK + 512] = np.where(far, NEG, 0.0).reshape(2, P, N_LAT).transpose(1, 0, 2).reshape(P, 512)
    return out


def kernel(**inputs):
    import concourse.bacc as bacc
    from concourse.bass_utils import run_bass_kernel_spmd

    a = {k: np.asarray(v) for k, v in inputs.items()}

    def feature_major(m):
        return m.T.reshape(DC, P, -1).transpose(1, 0, 2)

    x = np.ascontiguousarray(np.concatenate([feature_major(a["x"][0]), feature_major(a["ctx"][0])], axis=2))
    small = []
    for l in range(DEPTH):
        small += [columns(a["g_norm1"][l]), columns(a["g_norm2"][l]), columns(a["b_mod"][l]), columns(a["c_subln"][l])]
    small += [columns(a["g_final"]), np.stack([columns(a["c"][0]), columns(a["c_ctx"])], axis=2).reshape(P, 2 * DC)]
    sinks = a["a_sink"].reshape(DEPTH, 2, 4).transpose(0, 2, 1).reshape(1, DEPTH * 8)
    small += [np.repeat(sinks, P, axis=0), np.repeat(a["c_lambda"].reshape(1, -1), P, axis=0)]
    arrays = {
        "x_in": x,
        "small_in": np.ascontiguousarray(np.concatenate(small, axis=1)),
        "const_in": constants(),
        "bias_in": bias_tiles(a["b_rpb"]),
        "stream_in": np.stack([weight_stream(*[a[n][l] for n in (
            "w_mod", "w_in", "w_branch_a", "w_branch_b", "w_branch_c", "w_out", "peer_wq", "peer_keys")])
            for l in range(DEPTH)]),
        "experts_in": expert_pairs(a["peer_u"], a["peer_v"]),
    }
    nc = bacc.Bacc("TRN2", target_bir_lowering=False, num_devices=1)
    args = [nc.dram_tensor(name, m.shape, mybir.dt.from_np(m.dtype), kind="ExternalInput").ap()
            for name, m in arrays.items()]
    out = nc.dram_tensor("out", (P, DC, N_LAT), mybir.dt.float32, kind="ExternalOutput").ap()
    build(nc, *args, out)
    res = run_bass_kernel_spmd(nc, [arrays], core_ids=[0])
    got = res.results[0]["out"]
    return np.ascontiguousarray(got.transpose(2, 1, 0).reshape(1, N_LAT, D))
```

```python
import math
from contextlib import ExitStack

import numpy as np
import concourse.bass as bass
from concourse import mybir

P = 128
D = 1024
DC = D // P
N_LAT = 256
N_CTX = 256
T = N_LAT + N_CTX
TT = T // P
DEPTH = 2
GRID_W = 64
HD = 64
KEYS = 128
PH = 8
TOPK = 16
HK = PH * TOPK
EPS = 1e-6
NEG = -1e30
USED = -3.0e38
LAM_INIT = [0.8 - 0.6 * math.exp(-0.3 * l) for l in range(DEPTH)]

RING = 4
BLOCKS = 16
PAIR = BLOCKS * P
MOD_UNITS = 6 * DC
MOD_PAIRS = MOD_UNITS // 2
QKV_PAIRS = 15
MERGE_PAIRS = 18
WOUT_PAIRS = 4
WQ_PAIRS = 8
HALVES = 2
ROWS = KEYS // HALVES
HOT = 4
GROUPS = N_LAT // 8
MOD_GROUPS = 6 * D // 512

UNITS = ([("aq", u) for u in range(4)] + [("ak", 0)] + [("bq", u) for u in range(4)] + [("bk", u) for u in range(4)]
         + [("cq", u) for u in range(4)] + [("ck", u) for u in range(4)])
NU = len(UNITS)
ROPED = [k for k, (name, _) in enumerate(UNITS) if name[0] != "b"]
UNIT_AT = {unit: k for k, unit in enumerate(UNITS)}

STREAMS = [[0, 1], [0]]
PASSES = [(0, 1), (0, 0), (1, 0)]
STEPS = [[(l, s, u, qt) for s in STREAMS[l] for u in range(12) for qt in range(2)] for l in range(DEPTH)]
STEP0 = [0, len(STEPS[0])]
BIASED = {}
for _l in range(DEPTH):
    for _n, (_, _s, _u, _q) in enumerate(STEPS[_l]):
        if _s == 0 and 4 <= _u < 8:
            BIASED[STEP0[_l] + _n] = len(BIASED)

RUNS, QKV_AT, MERGE_AT, WOUT_AT, WQ_AT, KEYS_AT, UV_AT = [], [], [], [], [], [], []
MOD_AT = [[], []]


def _number():
    at, dram = 0, 0

    def run(count, experts=None, again=None):
        nonlocal at, dram
        RUNS.append((at, count, experts, dram if again is None else again))
        at += count
        if experts is None and again is None:
            dram += count
        return at - count

    for half in range(2):
        MOD_AT[0].append(run(MOD_PAIRS // 2))
    for l in range(DEPTH):
        QKV_AT.append(run(QKV_PAIRS))
        MERGE_AT.append(run(MERGE_PAIRS))
        WOUT_AT.append(run(WOUT_PAIRS))
        first = dram
        for n, stream in enumerate([1, 0] if l == 0 else [0]):
            again = first if n else None
            WQ_AT.append(run(WQ_PAIRS, again=again))
            keys = [run(1, again=None if again is None else again + WQ_PAIRS)]
            if l == 0 and n == 0:
                MOD_AT[1].append(run(MOD_PAIRS // 2))
                keys.append(run(1, again=first + WQ_PAIRS))
                MOD_AT[1].append(run(MOD_PAIRS // 2))
            KEYS_AT.append(keys)
            UV_AT.append(run(KEYS, experts=l))
    return at, dram


TOTAL_PAIRS, DRAM_PAIRS = _number()


def is_experts(p):
    return any(at <= p < at + KEYS for at in UV_AT)


def through(p):
    return sum(is_experts(q) == is_experts(p) for q in range(p + 1))


C_G1, C_G2, C_BMOD, C_SUBLN = 0, DC, 2 * DC, 2 * DC + MOD_UNITS
C_LAYER = C_SUBLN + 4
C_GF = DEPTH * C_LAYER
C_COND = C_GF + DC
C_SINK = C_COND + 2 * DC
C_ALL = C_SINK + DEPTH * 8
K_IDENT, K_ONES, K_IOTA, K_ROT, K_ZERO, K_COS, K_SIN, K_MASK, K_ALL = 0, 128, 256, 384, 512, 640, 896, 1152, 1664


def build(nc, x_in, small_in, lambda_in, const_in_dram, bias_in, stream_in, experts_in, out):
    fp32 = mybir.dt.float32
    fp32r = mybir.dt.float32r
    u32 = mybir.dt.uint32
    ALU = mybir.AluOpType
    ACT = mybir.ActivationFunctionType
    AX = mybir.AxisListType

    ctx = ExitStack()
    with ctx:
        def sb(name, shape, dt=fp32):
            return ctx.enter_context(nc.sbuf_tensor(name, shape, dt))

        def sem(name):
            return ctx.enter_context(nc.semaphore(name))

        x = sb("x", [P, DC, T])
        h2 = sb("h2", [P, DC, N_LAT])
        ring = sb("ring", [P, RING, PAIR])
        small = sb("small", [P, C_ALL])
        const = sb("const", [P, K_ALL])
        cond = sb("cond", [P, DC, 2])
        modc = sb("modc", [P, MOD_UNITS, 2])
        a1 = sb("a1", [P, DC, 2])
        a2 = sb("a2", [P, DC, 2])
        stat = sb("stat", [P, 2, 12])
        lam = sb("lam", [P, 12])
        ps = ctx.enter_context(nc.psum_tensor("ps", [P, 8, 512], fp32))

        ident = const[:, K_IDENT:K_IDENT + P]
        ones = const[:, K_ONES:K_ONES + P]
        iota = const[:, K_IOTA:K_IOTA + P]
        rot = const[:, K_ROT:K_ROT + P]
        zero = const[:, K_ZERO:K_ZERO + P]
        cos = const[:, K_COS:K_COS + N_LAT]
        sin = const[:, K_SIN:K_SIN + N_LAT]
        finite = const[:, K_COS:K_COS + 512]
        mask = const[:, K_MASK:K_MASK + 512].rearrange("p (q k) -> p q k", q=2)

        mod_raw = sb("mod_raw", [P, MOD_UNITS, 2])

        with nc.sbuf_tensor("att", [P, 31744], fp32) as big:
            pass
        feat = big[:, 0:NU * T].rearrange("p (u t) -> p u t", u=NU)
        o = NU * T
        va = big[:, o:o + TT * 128].rearrange("p (t c) -> p t c", t=TT)
        vb = big[:, o + 512:o + 2560].rearrange("p (t c) -> p t c", t=TT)
        vc = big[:, o + 2560:o + 4608].rearrange("p (t c) -> p t c", t=TT)
        o += 4608
        yt = big[:, o:o + 12 * T].rearrange("p (u t) -> p u t", u=12)
        o += 12 * T
        h1 = big[:, o:o + DC * T].rearrange("p (c t) -> p c t", c=DC)
        o += DC * T
        prob = big[:, o:o + 2048].rearrange("p (b m k) -> p b m k", b=2, m=2)
        probt = big[:, o + 2048:o + 4096].rearrange("p (b m k) -> p b m k", b=2, m=2)
        sq = big[:, o:o + 1024].rearrange("p (b t) -> p b t", b=2)
        rstd = big[:, o + 1024:o + 1536]
        ropet = big[:, o + 1536:o + 2048].rearrange("p (b t) -> p b t", b=2)
        sig = big[:, o + 2048:o + 3072].rearrange("p (b t) -> p b t", b=2)
        prodt = big[:, o + 3072:o + 4096].rearrange("p (b t) -> p b t", b=2)
        o += 4096
        bias = big[:, o:o + 1024].rearrange("p (b m k) -> p b m k", b=2, m=2)
        mt = big[:, 0:DC * T].rearrange("p (c t) -> p c t", c=DC)
        big = sb("gate_region", [P, ROWS * N_LAT])
        pickt = sb("pickt", [P, 3, N_LAT])
        hots = sb("hots", [P, HOT * 8 * (ROWS + KEYS)])
        u_hi = sb("u_hi", [P, 2, D], fp32r)
        u_lo = sb("u_lo", [P, 2, D], fp32r)
        v_hi = sb("v_hi", [P, 2, D], fp32r)
        v_lo = sb("v_lo", [P, 2, D], fp32r)
        h_hi = sb("h_hi", [P, DC, N_LAT], fp32r)
        h_lo = sb("h_lo", [P, DC, N_LAT], fp32r)
        w_hi = sb("w_hi", [P, 2, N_LAT], fp32r)
        w_lo = sb("w_lo", [P, 2, N_LAT], fp32r)
        gates = big[:, 0:ROWS * N_LAT].rearrange("p (i t) -> p i t", i=ROWS)
        pq = big[:, 0:16 * N_LAT].rearrange("p (u t) -> p u t", u=16)
        o = 16 * N_LAT
        sv = big[:, o:o + 256].rearrange("p (u k) -> p u k", u=16)
        si = big[:, o + 256:o + 512].bitcast(u32).rearrange("p (u k) -> p u k", u=16)
        sif = big[:, o + 512:o + 768].rearrange("p (u k) -> p u k", u=16)
        work = big[:, o + 768:o + 1792]
        cand = big[:, o + 1792:o + 3840].rearrange("p (h k) -> p h k", h=PH)
        tv = big[:, o + 3840:o + 3968].rearrange("p (h k) -> p h k", h=PH)
        pos = big[:, o + 3968:o + 4096].bitcast(u32)
        pos2 = big[:, o + 4096:o + 4352].bitcast(u32)
        posf = big[:, o + 4352:o + 4608]
        hot = big[:, o + 4608:o + 6656].rearrange("p (h k i) -> p h k i", h=PH, k=TOPK)
        ex = big[:, o + 6656:o + 6784].rearrange("p (h k) -> p h k", h=PH)
        exs = big[:, o + 6784:o + 6800]
        picks = big[:, o + 6912:o + 7680].rearrange("p (b w k) -> p b w k", b=2, w=3)
        hot_i = hots[:, 0:HOT * 8 * ROWS].rearrange("p (b q i) -> p b q i", b=HOT, q=8)
        hot_j = hots[:, HOT * 8 * ROWS:].rearrange("p (b q j) -> p b q j", b=HOT, q=8)
        wfull = hots[:, 0:2 * N_LAT].rearrange("p (b t) -> p b t", b=2)
        mod_rows = hots[0:2, 0:6 * D // 2]
        accs = hots[:, 0:2048].rearrange("p (b d) -> p b d", b=2)

        arrived = [sem(f"arrived{i}") for i in range(RING)]
        released = sem("released")
        inputs_in = sem("inputs_in")
        bias_arrived = [sem(f"bias_arrived{i}") for i in range(2)]
        cond_ready = sem("cond_ready")
        mod_group_done = sem("mod_group_done")
        mod_row_copied = sem("mod_row_copied")
        mod_cols_done = sem("mod_cols_done")
        mod_cols_copied = sem("mod_cols_copied")
        mod_ready = sem("mod_ready")
        lam_dots = sem("lam_dots")
        lam_exps = sem("lam_exps")
        sq_ready = sem("sq_ready")
        inverse_ready = sem("inverse_ready")
        root_ready = sem("root_ready")
        sq_summed = sem("sq_summed")
        scaled = sem("scaled")
        h_ready = sem("h_ready")
        proj_done = sem("proj_done")
        proj_copied = sem("proj_copied")
        rot_done = sem("rot_done")
        roped = sem("roped")
        v_done = sem("v_done")
        v_copied = sem("v_copied")
        scores_done = sem("scores_done")
        max_ready = sem("max_ready")
        exp_ready = sem("exp_ready")
        prob_ready = sem("prob_ready")
        probt_done = sem("probt_done")
        probt_copied = sem("probt_copied")
        y_done = sem("y_done")
        y_copied = sem("y_copied")
        cn_sq = sem("cn_sq")
        cn_sum = sem("cn_sum")
        cn_ready = sem("cn_ready")
        merge_done = sem("merge_done")
        sig_ready = sem("sig_ready")
        prod_done = sem("prod_done")
        m_ready = sem("m_ready")
        wout_done = sem("wout_done")
        x_ready = sem("x_ready")
        pq_done = sem("pq_done")
        pq_copied = sem("pq_copied")
        keys_done = sem("keys_done")
        picks_found = sem("picks_found")
        topd_ready = sem("topd_ready")
        topexp_ready = sem("topexp_ready")
        picks_ready = sem("picks_ready")
        pickt_done = sem("pickt_done")
        pickt_copied = sem("pickt_copied")
        hot_j_ready = sem("hot_j_ready")
        hot_i_equal = sem("hot_i_equal")
        hot_i_ready = sem("hot_i_ready")
        hot_used = sem("hot_used")
        h_hi_ready = sem("h_hi_ready")
        h_lo_ready = sem("h_lo_ready")
        u_hi_ready = sem("u_hi_ready")
        u_lo_ready = sem("u_lo_ready")
        v_hi_ready = sem("v_hi_ready")
        v_lo_ready = sem("v_lo_ready")
        w_full_ready = sem("w_full_ready")
        w_hi_ready = sem("w_hi_ready")
        values_done = sem("values_done")
        gates_copied = sem("gates_copied")
        s_done = sem("s_done")
        gelu_done = sem("gelu_done")
        w_ready = sem("w_ready")
        acc_done = sem("acc_done")
        acc_copied = sem("acc_copied")
        outt_done = sem("outt_done")
        out_ready = sem("out_ready")
        out_stored = sem("out_stored")
        dve_order = sem("dve_order")
        act_order = sem("act_order")

        def wait_pair(eng, p, i=0):
            eng.wait_ge(arrived[p % RING], i * 16 + 16 * (p // RING + 1))

        def block_of(p, b):
            q = p + b // BLOCKS
            return ring[:, q % RING, (b % BLOCKS) * P:(b % BLOCKS + 1) * P]

        def root_at(n=None, l=None, h=None):
            return (0, 5, 6, 7, 12, 13)[n] if n is not None else (1, 8)[l] + h

        def norm_x(n):
            return [(0, 0, T), (8, N_LAT, T), (16, 0, N_LAT), (24, 0, T), (32, 0, N_LAT), (40, 0, N_LAT)][n]

        block = ctx.enter_context(nc.Block())

        @block.sync
        def _(sp):
            sp.dma_start(small[:, :], small_in).then_inc(inputs_in, 16)
            sp.dma_start(h2[:, 0:DEPTH, :], lambda_in).then_inc(inputs_in, 16)

            def load(p, src, i=0):
                if p >= RING:
                    held = p - RING
                    sp.wait_ge(v_lo_ready if is_experts(held) else released, i * RING + through(held))
                sp.dma_start(ring[:, p % RING, :], src).then_inc(arrived[p % RING], 16)

            for p, count, experts, first in RUNS:
                def src(k):
                    return stream_in[first + k, :, :] if experts is None else experts_in[experts, k, :, :]
                for k in range(min(count, RING)):
                    load(p + k, src(k))
                rounds = count // RING
                if rounds > 1:
                    with sp.Fori(0, rounds - 1) as i:
                        for k in range(RING):
                            load(p + RING + k, src(i * RING + RING + k), i)
                for k in range(max(rounds, 1) * RING, count):
                    load(p + k, src(k))
            sp.wait_ge(out_ready, 1)
            sp.dma_start(out, h2[:, :, :]).then_inc(out_stored, 16)
            sp.wait_ge(out_stored, 16)

        @block.tensor
        def _(pe):
            mm = nc.tensor.matmul

            def mod(l, half, banks):
                p0 = MOD_AT[l][half]
                done = (2 * l + half) * (MOD_GROUPS // 2)
                for g in range(MOD_GROUPS // 2):
                    if g >= 2:
                        pe.wait_ge(mod_row_copied, done + g - 1)
                    for c in range(DC):
                        q = p0 + 2 * g + c // 4
                        if c % 4 == 0:
                            wait_pair(pe, q)
                        last = mm(ps[0:2, banks[g % 2], :], cond[:, c, :],
                                  ring[:, q % RING, (c % 4) * 512:(c % 4 + 1) * 512],
                                  start=(c == 0), stop=(c == DC - 1))
                        if c == 3:
                            last.then_inc(released, 1)
                    last.then_inc(mod_group_done, 1)
                    pe.wait_ge(mod_group_done, done + g + 1)
                    pe.sem_inc(released, 1)
                pe.wait_ge(mod_row_copied, done + MOD_GROUPS // 2)
                for u in range(MOD_UNITS // 2):
                    last = nc.tensor.transpose(ps[:, banks[0], 2 * u:2 * u + 2], mod_rows[:, u * P:(u + 1) * P],
                                               ident[0:2, 0:2])
                last.then_inc(mod_cols_done, 1)

            def sums(n):
                _, c0, c1 = norm_x(n)
                for c in range(DC):
                    m = n * DC + c
                    pe.wait_ge(sq_ready, m + 1)
                    mm(ps[:, 0, 0:c1 - c0], ones, sq[:, c % 2, 0:c1 - c0], start=(c == 0), stop=(c == DC - 1))\
                        .then_inc(sq_summed, 1)

            def proj(l):
                p0 = QKV_AT[l]

                def rotate(r):
                    k = ROPED[r]
                    g = l * len(ROPED) + r
                    pe.wait_ge(proj_copied, l * NU + k + 1)
                    if g >= 2:
                        pe.wait_ge(roped, g - 1)
                    mm(ps[:, 4 + g % 2, 0:N_LAT], rot, feat[:, k, 0:N_LAT], start=True, stop=True)\
                        .then_inc(rot_done, 1)

                turn = 0
                for k, (name, u) in enumerate(UNITS):
                    n = N_LAT if (l == DEPTH - 1 and name[1] == "q") else T
                    if k % 2 == 0:
                        wait_pair(pe, p0 + k // 2)
                    if k == 0:
                        pe.wait_ge(h_ready, (0 if l == 0 else 3) * DC + DC)
                    if k >= 4:
                        pe.wait_ge(proj_copied, l * NU + k - 3)
                    for c in range(DC):
                        last = mm(ps[:, k % 4, 0:n], block_of(p0, k * DC + c), h1[:, c, 0:n],
                                  start=(c == 0), stop=(c == DC - 1))
                    last.then_inc(proj_done, 1)
                    if k % 2 == 1:
                        pe.wait_ge(proj_done, l * NU + k + 1)
                        pe.sem_inc(released, 1)
                    while turn < len(ROPED) and ROPED[turn] < k:
                        rotate(turn)
                        turn += 1
                for t in range(TT):
                    for c in range(DC):
                        last = mm(ps[:, 6, t * P:(t + 1) * P], h1[:, c, t * P:(t + 1) * P],
                                  block_of(p0, NU * DC + c), start=(c == 0), stop=(c == DC - 1))
                last.then_inc(v_done, 1)
                while turn < len(ROPED):
                    rotate(turn)
                    turn += 1
                pe.wait_ge(v_done, 9 * l + 1)
                pe.sem_inc(released, 1)
                for w in range(2):
                    q0 = p0 + 11 + 2 * w
                    if w == 0:
                        pe.wait_ge(proj_copied, l * NU + NU)
                    else:
                        pe.wait_ge(roped, (l + 1) * len(ROPED))
                        pe.wait_ge(v_copied, 9 * l + 1)
                    for c in range(DC):
                        if c % 4 == 0:
                            wait_pair(pe, q0 + c // 4)
                        q = (q0 + c // 4) % RING
                        for t in range(TT):
                            last = mm(ps[:, 4 * w + t, :], h1[:, c, t * P:(t + 1) * P],
                                      ring[:, q, (c % 4) * 512:(c % 4 + 1) * 512],
                                      start=(c == 0), stop=(c == DC - 1))
                            if c == DC - 1 and t < TT - 1:
                                last.then_inc(v_done, 1)
                        if c == 3:
                            last.then_inc(released, 1)
                    last.then_inc(v_done, 1)
                    pe.wait_ge(v_done, 9 * l + 1 + 4 * (w + 1))
                    pe.sem_inc(released, 1)

            def attention(l):
                steps = STEPS[l]

                def keys_of(s):
                    return (0, T) if s == 0 else (N_LAT, T)

                def scores(n):
                    _, s, u, qt = steps[n]
                    a = STEP0[l] + n
                    k0, k1 = keys_of(s)
                    q = UNIT_AT[("abc"[u // 4] + "q", u % 4)]
                    k = UNIT_AT[("abc"[u // 4] + "k", 0 if u < 4 else u % 4)]
                    if n >= 2:
                        pe.wait_ge(exp_ready, a - 1)
                    t0 = s * N_LAT + qt * P
                    for m in range(2):
                        last = mm(ps[:, 2 * (a % 2) + m, 0:k1 - k0], feat[64 * m:64 * m + 64, q, t0:t0 + P],
                                  feat[64 * m:64 * m + 64, k, k0:k1], start=True, stop=True)
                    last.then_inc(scores_done, 1)

                def transposes(n):
                    _, s, u, qt = steps[n]
                    a = STEP0[l] + n
                    k0, k1 = keys_of(s)
                    pe.wait_ge(prob_ready, a + 1)
                    if a >= 1:
                        pe.wait_ge(probt_copied, a)
                    for m in range(2 if u < 8 else 1):
                        for t in range((k1 - k0) // P):
                            last = nc.tensor.transpose(ps[:, 4 + m, t * P:(t + 1) * P],
                                                       prob[:, a % 2, m, t * P:(t + 1) * P], ident)
                    last.then_inc(probt_done, 1)

                def values(n):
                    _, s, u, qt = steps[n]
                    a = STEP0[l] + n
                    k0, k1 = keys_of(s)
                    nt = (k1 - k0) // P
                    pe.wait_ge(probt_copied, a + 1)
                    if a >= 2:
                        pe.wait_ge(y_copied, a - 1)
                    y = ps[:, 6 + a % 2, 0:P]
                    for m in range(2 if u < 8 else 1):
                        for t in range(nt):
                            tile = k0 // P + t
                            if u < 4:
                                v, rows = va[:, tile, 64 * m:64 * m + 64], slice(64 * m, 64 * m + 64)
                            elif u < 8:
                                c0 = 128 * (u - 4) + 64 * m
                                v, rows = vb[:, tile, c0:c0 + 64], slice(64 * m, 64 * m + 64)
                            else:
                                v, rows = vc[:, tile, 128 * (u - 8):128 * (u - 7)], slice(0, 128)
                            last = mm(y[rows, :], v, probt[:, a % 2, m, t * P:(t + 1) * P],
                                      start=(t == 0), stop=(t == nt - 1))
                    last.then_inc(y_done, 1)

                pe.wait_ge(roped, (l + 1) * len(ROPED))
                pe.wait_ge(v_copied, 9 * (l + 1))
                scores(0)
                scores(1)
                for n in range(len(steps)):
                    if n + 2 < len(steps):
                        scores(n + 2)
                    transposes(n)
                    if n >= 1:
                        values(n - 1)
                values(len(steps) - 1)

            def head_norm(l):
                n = T if len(STREAMS[l]) == 2 else N_LAT
                for h in range(4):
                    g = 4 * l + h
                    pe.wait_ge(cn_sq, g + 1)
                    mm(ps[:, h, 0:n], ones, sq[:, h % 2, 0:n], start=True, stop=True).then_inc(cn_sum, 1)

            def merge(l):
                n = T if len(STREAMS[l]) == 2 else N_LAT
                p0 = MERGE_AT[l]
                pe.wait_ge(cn_ready, 4 * (l + 1))
                b = 0
                for item in range(6 * DC):
                    g = 6 * DC * l + item
                    branch = item % 6 // 2
                    bank = item % 8
                    if item >= 8:
                        pe.wait_ge(prod_done, 3 * DC * l + (item - 8) // 2 + 1)
                    count = DC if item % 2 == 0 else 4
                    for c in range(count):
                        if b % BLOCKS == 0:
                            wait_pair(pe, p0 + b // BLOCKS)
                        src = h1[:, c, 0:n] if item % 2 == 0 else yt[:, 4 * branch + c, 0:n]
                        last = mm(ps[:, bank, 0:n], block_of(p0, b), src, start=(c == 0), stop=(c == count - 1))
                        b += 1
                        if b % BLOCKS == 0:
                            if c == count - 1:
                                last.then_inc(merge_done, 1)
                                pe.wait_ge(merge_done, g + 1)
                                pe.sem_inc(released, 1)
                            else:
                                last.then_inc(released, 1)
                        elif c == count - 1:
                            last.then_inc(merge_done, 1)

            def w_out(l):
                n = T if len(STREAMS[l]) == 2 else N_LAT
                p0 = WOUT_AT[l]
                pe.wait_ge(m_ready, DC * (l + 1))
                for j in range(DC):
                    if j % 2 == 0:
                        wait_pair(pe, p0 + j // 2)
                    for c in range(DC):
                        last = mm(ps[:, j, 0:n], block_of(p0, j * DC + c), mt[:, c, 0:n],
                                  start=(c == 0), stop=(c == DC - 1))
                    last.then_inc(wout_done, 1)
                    if j % 2 == 1:
                        pe.wait_ge(wout_done, DC * l + j + 1)
                        pe.sem_inc(released, 1)

            def key_scores(r, tt, p):
                wait_pair(pe, p)
                for u in range(16):
                    last = mm(ps[:, 4 * (1 - tt) + u // 4, (u % 4) * P:(u % 4 + 1) * P],
                              pq[:, u, tt * P:(tt + 1) * P], block_of(p, u), start=True, stop=True)
                    if u % 4 == 3:
                        last.then_inc(keys_done, 1)

            def peer(r):
                p0 = WQ_AT[r]
                pe.wait_ge(h_ready, (1, 2, 4)[r] * DC + DC)
                for u in range(16):
                    if u % 2 == 0:
                        wait_pair(pe, p0 + u // 2)
                    if u >= 4:
                        pe.wait_ge(pq_copied, 16 * r + u - 3)
                    for c in range(DC):
                        last = mm(ps[:, u % 4, 0:N_LAT], block_of(p0, u * DC + c), h2[:, c, :],
                                  start=(c == 0), stop=(c == DC - 1))
                    last.then_inc(pq_done, 1)
                    if u % 2 == 1:
                        pe.wait_ge(pq_done, 16 * r + u + 1)
                        pe.sem_inc(released, 1)
                pe.wait_ge(pq_copied, 16 * (r + 1))
                key_scores(r, 0, KEYS_AT[r][0])
                if len(KEYS_AT[r]) == 2:
                    pe.wait_ge(keys_done, 8 * r + 4)
                    pe.sem_inc(released, 1)
                    mod(1, 0, (0, 1))
                    pe.wait_ge(mod_cols_copied, 3)
                key_scores(r, 1, KEYS_AT[r][-1])
                pe.wait_ge(keys_done, 8 * (r + 1))
                pe.sem_inc(released, 1)
                if len(KEYS_AT[r]) == 2:
                    pe.wait_ge(picks_found, 2 * r + 1)
                    mod(1, 1, (5, 6))
                for tt in range(2):
                    pe.wait_ge(picks_ready, 2 * r + tt + 1)
                    for w in range(3):
                        last = nc.tensor.transpose(ps[:, 4 * (1 - tt), w * P:(w + 1) * P], picks[:, tt, w, :], ident)
                    last.then_inc(pickt_done, 1)
                pe.wait_ge(pickt_copied, 2 * (r + 1))
                pe.wait_ge(h_lo_ready, r + 1)
                for b in range(4):
                    mm(ps[:, 4 + b, :], zero, finite, start=True, stop=False)

                for half in range(HALVES):
                    g0 = (r * HALVES + half) * GROUPS
                    n0 = (r * HALVES + half) * ROWS

                    def gate_group(i, k):
                        pe.wait_ge(hot_j_ready, i * HOT + (g0 + k + 1))
                        pe.wait_ge(hot_i_ready, i * HOT + (g0 + k + 1))
                        if not isinstance(i, int) or g0 + k >= HOT:
                            pe.wait_ge(gates_copied, i * HOT + (g0 + k + 1 - HOT))
                        for q in range(8):
                            last = mm(ps[:, k, q * ROWS:(q + 1) * ROWS], hot_j[:, k, q, :], hot_i[:, k, q, :],
                                      start=True, stop=True)
                        last.then_inc(hot_used, 1)

                    for k in range(HOT):
                        gate_group(0, k)
                    with pe.Fori(1, GROUPS // HOT) as i:
                        for k in range(HOT):
                            gate_group(i, k)
                    pe.wait_ge(gates_copied, g0 + GROUPS)

                    def expert_scores(i, k):
                        pe.wait_ge(u_lo_ready, i * 4 + (n0 + k + 1))
                        if not isinstance(i, int) or n0 + k >= 4:
                            pe.wait_ge(w_full_ready, i * 4 + (n0 + k - 3))
                        for c in range(DC):
                            cols = slice(c * P, (c + 1) * P)
                            mm(ps[:, k, 0:N_LAT], u_hi[:, k % 2, cols], h_hi[:, c, :], start=(c == 0), stop=False)
                            mm(ps[:, k, 0:N_LAT], u_hi[:, k % 2, cols], h_lo[:, c, :], start=False, stop=False)
                            last = mm(ps[:, k, 0:N_LAT], u_lo[:, k % 2, cols], h_hi[:, c, :],
                                      start=False, stop=(c == DC - 1))
                        last.then_inc(s_done, 1)

                    def expert_values(i, k):
                        pe.wait_ge(v_lo_ready, i * 4 + (n0 + k + 1))
                        pe.wait_ge(w_ready, i * 4 + (n0 + k + 1))
                        for tt in range(2):
                            toks = slice(tt * P, (tt + 1) * P)
                            for w, v in ((w_hi, v_hi), (w_hi, v_lo), (w_lo, v_hi)):
                                for d in range(2):
                                    last = mm(ps[:, 4 + 2 * tt + d, :], w[:, k % 2, toks],
                                              v[:, k % 2, 512 * d:512 * (d + 1)], start=False, stop=False)
                        last.then_inc(values_done, 1)

                    expert_scores(0, 0)
                    for k in range(1, 4):
                        expert_scores(0, k)
                        expert_values(0, k - 1)
                    with pe.Fori(1, ROWS // 4) as i:
                        for k in range(4):
                            expert_scores(i, k)
                            if k == 0:
                                expert_values(i - 1, 3)
                            else:
                                expert_values(i, k - 1)
                    expert_values(ROWS // 4 - 1, 3)
                for b in range(4):
                    last = mm(ps[:, 4 + b, :], zero, finite, start=False, stop=True)
                last.then_inc(acc_done, 1)
                for c in range(DC):
                    if c == 0:
                        pe.wait_ge(acc_copied, 4 * (r + 1))
                    for tt in range(2):
                        o = (c % 2) * 256 + tt * P
                        last = nc.tensor.transpose(ps[:, c // 2, o:o + P], accs[:, tt, c * P:(c + 1) * P], ident)
                    if c % 2 == 1:
                        last.then_inc(outt_done, 1)

            pe.wait_ge(inputs_in, 64)
            pe.wait_ge(cond_ready, 1)
            n = 0
            for l in range(DEPTH):
                sums((0, 3)[l])
                if l == 0:
                    mod(0, 0, (6, 7))
                    pe.wait_ge(mod_cols_copied, 1)
                    mod(0, 1, (6, 7))
                proj(l)
                attention(l)
                head_norm(l)
                merge(l)
                w_out(l)
                for r, (pl, s) in enumerate(PASSES):
                    if pl == l:
                        sums((1, 2, 4)[r])
                        peer(r)
            sums(5)

        @block.scalar
        def _(act):
            act.dma_start(const[:, :], const_in_dram).then_inc(inputs_in, 16)
            act.dma_start(x[:, :, :], x_in).then_inc(inputs_in, 16)
            order = [0]

            def link(ins):
                order[0] += 1
                ins.then_inc(act_order, 1)
                act.wait_ge(act_order, order[0])

            def root(at, w):
                act.wait_ge(inverse_ready, at + 1)
                nc.scalar.activation(rstd[:, 0:w], rstd[:, 0:w], ACT.Sqrt).then_inc(root_ready, 1)

            def squares(n):
                need, c0, c1 = norm_x(n)
                if need:
                    act.wait_ge(x_ready, need)
                for c in range(DC):
                    m = n * DC + c
                    if m >= 2:
                        act.wait_ge(sq_summed, m - 1)
                    nc.scalar.activation(sq[:, c % 2, 0:c1 - c0], x[:, c, c0:c1], ACT.Square).then_inc(sq_ready, 1)
                if n:
                    root(root_at(n), c1 - c0)

            def mod_half(l, half, banks):
                done = (2 * l + half) * (MOD_GROUPS // 2)
                for g in range(MOD_GROUPS // 2):
                    act.wait_ge(mod_group_done, done + g + 1)
                    if g == 0 and done:
                        act.wait_ge(mod_cols_done, 2 * l + half)
                    nc.scalar.activation(mod_rows[:, g * 512:(g + 1) * 512], ps[0:2, banks[g % 2], :], ACT.Copy)\
                        .then_inc(mod_row_copied, 1)
                act.wait_ge(mod_cols_done, 2 * l + half + 1)
                first = half * MOD_UNITS // 2
                if l and half == 0:
                    act.wait_ge(mod_ready, l)
                nc.scalar.activation(mod_raw[:, first:first + MOD_UNITS // 2, :],
                                     ps[:, banks[0], 0:MOD_UNITS].rearrange("p (u s) -> p u s", s=2),
                                     ACT.Copy).then_inc(mod_cols_copied, 1)

            def shifts(n, l, kind, streams, dst):
                for c in range(DC):
                    act.wait_ge(scaled, n * DC + c + 1)
                    for at, s in enumerate(streams):
                        o = dst[:, c, at * N_LAT:(at + 1) * N_LAT]
                        last = nc.scalar.activation(o, o, ACT.Identity, bias=modc[:, kind * DC + c, s:s + 1])
                    last.then_inc(h_ready, 1)

            act.wait_ge(inputs_in, 64)
            nc.scalar.activation(cond[:, :, :], small[:, C_COND:C_COND + 2 * DC].rearrange("p (c s) -> p c s", s=2),
                                 ACT.Silu).then_inc(cond_ready, 1)
            act.wait_ge(lam_dots, 1)
            nc.scalar.activation(lam[:, 4:8], lam[:, 0:4], ACT.Exp).then_inc(lam_exps, 1)
            for l in range(DEPTH):
                streams = STREAMS[l]
                n = T if len(streams) == 2 else N_LAT
                squares((0, 3)[l])
                if l == 0:
                    mod_half(0, 0, (6, 7))
                    mod_half(0, 1, (6, 7))
                    root(root_at(0), T)
                shifts((0, 3)[l], l, 0, [0, 1], h1)
                for k, (name, u) in enumerate(UNITS):
                    w = N_LAT if (l == DEPTH - 1 and name[1] == "q") else T
                    act.wait_ge(proj_done, l * NU + k + 1)
                    nc.scalar.activation(feat[:, k, 0:w], ps[:, k % 4, 0:w], ACT.Copy,
                                         scale=HD ** -0.5 if name[1] == "q" else 1.0).then_inc(proj_copied, 1)
                steps = STEPS[l]

                def exps(i):
                    _, s, u, qt = steps[i]
                    a = STEP0[l] + i
                    nk = T if s == 0 else N_CTX
                    act.wait_ge(max_ready, a + 1)
                    if i >= 2:
                        act.wait_ge(probt_done, a - 1)
                    st = stat[:, a % 2, :]
                    if u < 4:
                        nc.scalar.activation(st[:, 6:8], st[:, 10:12], ACT.Exp)
                    for m in range(2):
                        last = nc.scalar.activation(prob[:, a % 2, m, 0:nk], ps[:, 2 * (a % 2) + m, 0:nk], ACT.Exp,
                                                    bias=st[:, 2 + m:3 + m], accum_out=st[:, 4 + m:5 + m])
                    last.then_inc(exp_ready, 1)

                def copy_probt(i):
                    _, s, u, qt = steps[i]
                    a = STEP0[l] + i
                    nk = T if s == 0 else N_CTX
                    m = 2 if u < 8 else 1
                    act.wait_ge(probt_done, a + 1)
                    if a >= 2:
                        act.wait_ge(y_done, a - 1)
                    nc.scalar.activation(probt[:, a % 2, 0:m, 0:nk], ps[:, 4:4 + m, 0:nk], ACT.Copy)\
                        .then_inc(probt_copied, 1)

                exps(0)
                for i in range(len(steps)):
                    if i + 1 < len(steps):
                        exps(i + 1)
                    copy_probt(i)
                act.wait_ge(y_copied, STEP0[l] + len(steps))
                for h in range(4):
                    if h >= 2:
                        act.wait_ge(cn_sum, 4 * l + h - 1)
                    nc.scalar.activation(sq[:, h % 2, 0:n], yt[:, 8 + h, 0:n], ACT.Square).then_inc(cn_sq, 1)
                    if h >= 1:
                        root(root_at(l=l, h=h - 1), n)
                root(root_at(l=l, h=3), n)
                for g in range(3 * DC):
                    m = 3 * DC * l + g
                    act.wait_ge(merge_done, 6 * DC * l + 2 * g + 1)
                    if g >= 2:
                        act.wait_ge(prod_done, m - 1)
                    nc.scalar.activation(sig[:, g % 2, 0:n], ps[:, (2 * g) % 8, 0:n], ACT.Sigmoid)\
                        .then_inc(sig_ready, 1)
                for r, (pl, s) in enumerate(PASSES):
                    if pl != l:
                        continue
                    squares((1, 2, 4)[r])
                    shifts((1, 2, 4)[r], l, 3, [s], h2)
                    for u in range(16):
                        act.wait_ge(pq_done, 16 * r + u + 1)
                        nc.scalar.activation(pq[:, u, :], ps[:, u % 4, 0:N_LAT], ACT.Copy).then_inc(pq_copied, 1)
                    act.wait_ge(h_ready, (1, 2, 4)[r] * DC + DC)
                    nc.scalar.activation(h_hi[:, :, :], h2[:, :, :], ACT.Copy).then_inc(h_hi_ready, 1)

                    def split_u(i, m):
                        wait_pair(act, UV_AT[r] + m, i)
                        if not isinstance(i, int) or i * 4 + r * KEYS + m >= 2:
                            act.wait_ge(s_done, i * 4 + (r * KEYS + m - 1))
                        nc.scalar.activation(u_hi[:, m % 2, :], ring[:, (UV_AT[r] + m) % RING, 0:D], ACT.Copy)\
                            .then_inc(u_hi_ready, 1)

                    def split_v(i, m):
                        if not isinstance(i, int) or i * 4 + r * KEYS + m >= 2:
                            act.wait_ge(values_done, i * 4 + (r * KEYS + m - 1))
                        nc.scalar.activation(v_hi[:, m % 2, :], ring[:, (UV_AT[r] + m) % RING, D:2 * D], ACT.Copy)\
                            .then_inc(v_hi_ready, 1)

                    def pick_exps(tt):
                        act.wait_ge(topd_ready, 2 * r + tt + 1)
                        nc.scalar.activation(ex, tv, ACT.Exp).then_inc(topexp_ready, 1)

                    if len(KEYS_AT[r]) == 2:
                        mod_half(1, 0, (0, 1))
                        pick_exps(0)
                        mod_half(1, 1, (5, 6))
                    split_u(0, 0)
                    split_u(0, 1)
                    split_v(0, 0)
                    if len(KEYS_AT[r]) == 1:
                        pick_exps(0)
                    pick_exps(1)
                    for tt in range(2):
                        act.wait_ge(pickt_done, 2 * r + tt + 1)
                        nc.scalar.activation(pickt[:, :, tt * P:(tt + 1) * P],
                                             ps[:, 4 * (1 - tt), 0:3 * P].rearrange("p (w t) -> p w t", w=3),
                                             ACT.Copy).then_inc(pickt_copied, 1)
                    for half in range(HALVES):
                        g0 = (r * HALVES + half) * GROUPS
                        n0 = (r * HALVES + half) * ROWS

                        def copy_gates(i, k):
                            act.wait_ge(hot_used, i * HOT + (g0 + k + 1))
                            nc.scalar.activation(gates[:, :, bass.ds(i * (8 * HOT) + k * 8, 8)],
                                                 ps[:, k, :].rearrange("p (q i) -> p i q", q=8),
                                                 ACT.Copy).then_inc(gates_copied, 1)

                        if half:
                            act.wait_ge(w_full_ready, n0)
                        with act.Fori(0, GROUPS // HOT) as i:
                            for k in range(HOT):
                                copy_gates(i, k)

                        def tile(i, k, left=KEYS):
                            act.wait_ge(s_done, i * 4 + (n0 + k + 1))
                            nc.scalar.activation(ps[:, k, 0:N_LAT], ps[:, k, 0:N_LAT], ACT.Gelu)\
                                .then_inc(gelu_done, 1)
                            m = half * ROWS + k
                            if left > 2:
                                split_u(i, m + 2)
                            if left > 1:
                                split_v(i, m + 1)

                        with act.Fori(0, ROWS // 4 - 1) as i:
                            for k in range(4):
                                tile(i, k)
                        for k in range(4):
                            tile(ROWS // 4 - 1, k, 4 - k if half == HALVES - 1 else KEYS)
                    act.wait_ge(acc_done, r + 1)
                    for b in range(4):
                        nc.scalar.activation(accs[:, b // 2, (b % 2) * 512:(b % 2 + 1) * 512], ps[:, 4 + b, :],
                                             ACT.Copy).then_inc(acc_copied, 1)
            squares(5)

        @block.gpsimd
        def _(pool):
            for l in range(DEPTH):
                for a, b in BIASED.items():
                    if (a >= STEP0[1]) != (l == 1):
                        continue
                    if b % 8 >= 2:
                        back = [k for k, v in BIASED.items() if v == b - 2][0]
                        pool.wait_ge(max_ready, back + 1)
                    elif l > 0:
                        pool.wait_ge(h_ready, 3 * DC + DC)
                    u = b % 8
                    pool.dma_start(bias[:, b % 2, :, :], bias_in[l, u // 2, u % 2, :, :, :])\
                        .then_inc(bias_arrived[b % 2], 16)
                for r, (pl, s) in enumerate(PASSES):
                    if pl != l:
                        continue
                    for half in range(HALVES):
                        g0 = (r * HALVES + half) * GROUPS

                        def weigh(i, k):
                            pool.wait_ge(hot_i_equal, i * HOT + (g0 + k + 1))
                            gate = pickt[:, 2, bass.ds(i * (8 * HOT) + k * 8, 8)]
                            nc.gpsimd.tensor_tensor(hot_i[:, k, :, :], hot_i[:, k, :, :],
                                                    gate.unsqueeze(2).to_broadcast([P, 8, ROWS]), ALU.mult)\
                                .then_inc(hot_i_ready, 1)

                        with pool.Fori(0, GROUPS // HOT) as i:
                            for k in range(HOT):
                                weigh(i, k)

        @block.vector
        def _(dve):
            v = nc.vector
            order = [0]

            def link(ins):
                order[0] += 1
                ins.then_inc(dve_order, 1)
                dve.wait_ge(dve_order, order[0])

            def inverse_root(at, src, dst, count):
                link(v.tensor_scalar(dst, src, 1.0 / count, EPS, ALU.mult, ALU.add))
                v.reciprocal(dst, dst).then_inc(inverse_ready, 1)
                dve.wait_ge(root_ready, at + 1)

            def norm(n, gain, streams, dst):
                need, c0, c1 = norm_x(n)
                dve.wait_ge(sq_summed, (n + 1) * DC)
                inverse_root(root_at(n), ps[:, 0, 0:c1 - c0], rstd[:, 0:c1 - c0], D)
                for c in range(DC):
                    for at, s in enumerate(streams):
                        cols = slice(at * N_LAT, (at + 1) * N_LAT)
                        last = v.scalar_tensor_tensor(dst[:, c, cols], x[:, c, c0 + at * N_LAT:c0 + (at + 1) * N_LAT],
                                                      gain[:, c, s:s + 1], rstd[:, cols], ALU.mult, ALU.mult)
                    last.then_inc(scaled, 1)

            def lambdas():
                for l in range(DEPTH):
                    for d in range(2):
                        o = 2 * d * HD
                        last = v.tensor_tensor_reduce(out=rstd[:, o + l * HD:o + (l + 1) * HD], in0=h2[:, l, o:o + HD],
                                                      in1=h2[:, l, o + HD:o + 2 * HD], scale=1.0, scalar=0.0,
                                                      op0=ALU.mult, op1=ALU.add,
                                                      accum_out=lam[:, 2 * l + d:2 * l + d + 1])
                last.then_inc(lam_dots, 1)
                dve.wait_ge(lam_exps, 1)
                for l in range(DEPTH):
                    minus = lam[:, 8 + l:9 + l]
                    link(v.tensor_tensor(minus, lam[:, 5 + 2 * l:6 + 2 * l], lam[:, 4 + 2 * l:5 + 2 * l], ALU.subtract))
                    link(v.tensor_scalar(minus, minus, -LAM_INIT[l], None, ALU.add))

            def modulation(l):
                base = l * C_LAYER
                dve.wait_ge(mod_cols_copied, 2 * (l + 1))
                if l:
                    dve.wait_ge(x_ready, norm_x(3)[0])
                link(v.tensor_tensor(modc[:, :, :], mod_raw[:, :, :],
                                     small[:, base + C_BMOD:base + C_BMOD + MOD_UNITS].unsqueeze(2)
                                     .to_broadcast([P, MOD_UNITS, 2]), ALU.add))
                for kind, gcol, dst in ((1, C_G1, a1), (4, C_G2, a2)):
                    last = v.scalar_tensor_tensor(dst[:, :, :], modc[:, kind * DC:(kind + 1) * DC, :], 1.0,
                                                  small[:, base + gcol:base + gcol + DC].unsqueeze(2)
                                                  .to_broadcast([P, DC, 2]), ALU.add, ALU.mult)
                last.then_inc(mod_ready, 1)
                dve.wait_ge(mod_ready, l + 1)

            def rope(l):
                for r, k in enumerate(ROPED):
                    g = l * len(ROPED) + r
                    dve.wait_ge(rot_done, g + 1)
                    t = ropet[:, g % 2, :]
                    f = feat[:, k, 0:N_LAT]
                    v.tensor_tensor(t, ps[:, 4 + g % 2, 0:N_LAT], sin, ALU.mult)
                    link(v.tensor_tensor(f, f, cos, ALU.mult))
                    v.tensor_tensor(f, f, t, ALU.add).then_inc(roped, 1)
                dve.wait_ge(v_done, 9 * l + 1)
                v.tensor_copy(va, ps[:, 6, :].rearrange("p (t c) -> p t c", t=TT)).then_inc(v_copied, 1)
                for w, dst in enumerate((vb, vc)):
                    for t in range(TT):
                        dve.wait_ge(v_done, 9 * l + 2 + 4 * w + t)
                        v.tensor_copy(dst[:, t, :], ps[:, 4 * w + t, :]).then_inc(v_copied, 1)

            def attention(l):
                steps = STEPS[l]
                sinks = small[:, C_SINK + 8 * l:C_SINK + 8 * (l + 1)]

                def maxima(i):
                    _, s, u, qt = steps[i]
                    a = STEP0[l] + i
                    nk = T if s == 0 else N_CTX
                    st = stat[:, a % 2, :]
                    b = 2 * (a % 2)
                    dve.wait_ge(scores_done, a + 1)
                    if s == 0 and u < 8:
                        if u < 4:
                            add = mask[:, qt, :].unsqueeze(1).to_broadcast([P, 2, N_LAT])
                        else:
                            tile = BIASED[a]
                            dve.wait_ge(bias_arrived[tile % 2], 16 * (tile // 2 + 1))
                            add = bias[:, tile % 2, :, :]
                        link(v.tensor_tensor(ps[:, b:b + 2, 0:N_LAT], ps[:, b:b + 2, 0:N_LAT], add, ALU.add))
                    link(v.tensor_reduce(st[:, 0:2], ps[:, b:b + 2, 0:nk], AX.X, ALU.max))
                    if u < 4:
                        link(v.tensor_tensor(st[:, 0:2], st[:, 0:2], sinks[:, 2 * u:2 * u + 2], ALU.max))
                        v.tensor_tensor(st[:, 10:12], sinks[:, 2 * u:2 * u + 2], st[:, 0:2], ALU.subtract)
                    v.tensor_scalar(st[:, 2:4], st[:, 0:2], -1.0, None, ALU.mult).then_inc(max_ready, 1)

                def normalise(i):
                    _, s, u, qt = steps[i]
                    a = STEP0[l] + i
                    nk = T if s == 0 else N_CTX
                    st = stat[:, a % 2, :]
                    dve.wait_ge(exp_ready, a + 1)
                    if u < 4:
                        link(v.tensor_tensor(st[:, 4:6], st[:, 4:6], st[:, 6:8], ALU.add))
                    link(v.reciprocal(st[:, 8:10], st[:, 4:6]))
                    p0, p1 = prob[:, a % 2, 0, 0:nk], prob[:, a % 2, 1, 0:nk]
                    if u < 8:
                        v.tensor_scalar(p0, p0, st[:, 8:9], None, ALU.mult)
                        v.tensor_scalar(p1, p1, st[:, 9:10], None, ALU.mult).then_inc(prob_ready, 1)
                    else:
                        link(v.tensor_scalar(p1, p1, st[:, 9:10], lam[:, 8 + l:9 + l], ALU.mult, ALU.mult))
                        v.scalar_tensor_tensor(p0, p0, st[:, 8:9], p1, ALU.mult, ALU.add).then_inc(prob_ready, 1)

                def copy_y(i):
                    _, s, u, qt = steps[i]
                    a = STEP0[l] + i
                    dve.wait_ge(y_done, a + 1)
                    t0 = s * N_LAT + qt * P
                    v.tensor_copy(yt[:, u, t0:t0 + P], ps[:, 6 + a % 2, 0:P]).then_inc(y_copied, 1)

                maxima(0)
                for i in range(len(steps)):
                    if i + 1 < len(steps):
                        maxima(i + 1)
                    normalise(i)
                    if i >= 2:
                        copy_y(i - 2)
                copy_y(len(steps) - 2)
                copy_y(len(steps) - 1)

            def head_norm(l):
                n = T if len(STREAMS[l]) == 2 else N_LAT
                for h in range(4):
                    dve.wait_ge(cn_sum, 4 * l + h + 1)
                    inverse_root(root_at(l=l, h=h), ps[:, h, 0:n], rstd[:, 0:n], P)
                    link(v.scalar_tensor_tensor(yt[:, 8 + h, 0:n], yt[:, 8 + h, 0:n],
                                                small[:, l * C_LAYER + C_SUBLN + h:l * C_LAYER + C_SUBLN + h + 1],
                                                rstd[:, 0:n], ALU.mult, ALU.mult))
                    v.tensor_scalar(yt[:, 8 + h, 0:n], yt[:, 8 + h, 0:n], 1.0 - LAM_INIT[l], None, ALU.mult)\
                        .then_inc(cn_ready, 1)

            def merge(l):
                n = T if len(STREAMS[l]) == 2 else N_LAT
                for j in range(DC):
                    for b in range(3):
                        g = 3 * j + b
                        m = 3 * DC * l + g
                        dve.wait_ge(sig_ready, m + 1)
                        dve.wait_ge(merge_done, 6 * DC * l + 2 * g + 2)
                        dst = mt[:, j, 0:n] if b == 0 else prodt[:, b % 2, 0:n]
                        v.tensor_tensor(dst, ps[:, (2 * g + 1) % 8, 0:n], sig[:, g % 2, 0:n], ALU.mult)\
                            .then_inc(prod_done, 1)
                        if b:
                            dve.wait_ge(prod_done, m + 1)
                            add = v.tensor_tensor(mt[:, j, 0:n], mt[:, j, 0:n], dst, ALU.add)
                            if b == 1:
                                link(add)
                            else:
                                add.then_inc(m_ready, 1)
                for j in range(DC):
                    dve.wait_ge(wout_done, DC * l + j + 1)
                    for at, s in enumerate(STREAMS[l]):
                        cols = slice(at * N_LAT, (at + 1) * N_LAT)
                        last = v.scalar_tensor_tensor(x[:, j, cols], ps[:, j, cols], modc[:, 2 * DC + j, s:s + 1],
                                                      x[:, j, cols], ALU.mult, ALU.add)
                    last.then_inc(x_ready, 1)

            def top16(srcs, values, indices):
                for q in range(0, len(srcs), 4):
                    four = range(q, q + 4)
                    size = 1024 // 4
                    for u in four:
                        last = v.max(values[u][:, 0:8], srcs[u])
                    link(last)
                    for u in four:
                        w = work[:, (u - q) * size:(u - q) * size + srcs[u].shape[-1]]
                        last = v.match_replace(w, values[u][:, 0:8], srcs[u], USED)
                    link(last)
                    for u in four:
                        w = work[:, (u - q) * size:(u - q) * size + srcs[u].shape[-1]]
                        last = v.max(values[u][:, 8:16], w)
                    link(last)
                    for u in four:
                        w = work[:, (u - q) * size:(u - q) * size + srcs[u].shape[-1]]
                        v.max_index(indices[u][:, 0:8], values[u][:, 0:8], srcs[u])
                        last = v.max_index(indices[u][:, 8:16], values[u][:, 8:16], w)
                link(last)

            def picks_of(r, tt):
                for q in range(4):
                    dve.wait_ge(keys_done, 8 * r + 4 * tt + q + 1)
                srcs = [ps[:, 4 * (1 - tt) + u // 4, (u % 4) * P:(u % 4 + 1) * P] for u in range(16)]
                top16(srcs, [sv[:, u, :] for u in range(16)], [si[:, u, :] for u in range(16)])
                v.tensor_copy(sif, si).then_inc(picks_found, 1)
                sides = sv.rearrange("p (h w) k -> p h w k", w=2)
                first = sides[:, :, 0, :].unsqueeze(3).to_broadcast([P, PH, TOPK, TOPK])
                second = sides[:, :, 1, :].unsqueeze(2).to_broadcast([P, PH, TOPK, TOPK])
                link(v.tensor_tensor(cand.rearrange("p h (i j) -> p h i j", i=TOPK), first, second, ALU.add))
                pos3 = pos.rearrange("p (h k) -> p h k", h=PH)
                top16([cand[:, h, :] for h in range(PH)], [tv[:, h, :] for h in range(PH)],
                      [pos3[:, h, :] for h in range(PH)])
                v.tensor_copy(exs[:, 8:16], tv[:, :, 0])
                v.tensor_scalar(pos2[:, 0:HK], pos, 4, None, ALU.logical_shift_right)
                link(v.tensor_scalar(pos2[:, HK:2 * HK], pos, 15, None, ALU.bitwise_and))
                v.tensor_tensor(tv, tv, exs[:, 8:16].unsqueeze(2).to_broadcast([P, PH, TOPK]), ALU.subtract)\
                    .then_inc(topd_ready, 1)
                link(v.tensor_copy(posf, pos2))
                steps16 = iota[:, 0:TOPK].unsqueeze(1).unsqueeze(1).to_broadcast([P, PH, TOPK, TOPK])
                halves = sif.rearrange("p (h w) k -> p h w k", w=2)
                for w in range(2):
                    at = posf[:, w * HK:(w + 1) * HK].rearrange("p (h k) -> p h k", h=PH)
                    link(v.tensor_tensor(hot, steps16, at.unsqueeze(3).to_broadcast([P, PH, TOPK, TOPK]),
                                         ALU.is_equal))
                    link(v.tensor_tensor(hot, hot, halves[:, :, w, :].unsqueeze(2)
                                         .to_broadcast([P, PH, TOPK, TOPK]), ALU.mult))
                    link(v.tensor_reduce(picks[:, tt, w, :].rearrange("p (h k) -> p h k", h=PH), hot, AX.X, ALU.add))
                dve.wait_ge(topexp_ready, 2 * r + tt + 1)
                link(v.tensor_reduce(exs[:, 0:8], ex, AX.X, ALU.add))
                link(v.reciprocal(exs[:, 8:16], exs[:, 0:8]))
                v.tensor_tensor(picks[:, tt, 2, :].rearrange("p (h k) -> p h k", h=PH), ex,
                                exs[:, 8:16].unsqueeze(2).to_broadcast([P, PH, TOPK]), ALU.mult)\
                    .then_inc(picks_ready, 1)

            def peer(r, l, s):
                dve.wait_ge(h_hi_ready, r + 1)
                v.tensor_tensor(h_lo[:, :, :], h2[:, :, :], h_hi[:, :, :], ALU.subtract).then_inc(h_lo_ready, 1)

                def split_u(i, m):
                    dve.wait_ge(u_hi_ready, i * 4 + (r * KEYS + m + 1))
                    v.tensor_tensor(u_lo[:, m % 2, :], ring[:, (UV_AT[r] + m) % RING, 0:D], u_hi[:, m % 2, :],
                                    ALU.subtract).then_inc(u_lo_ready, 1)

                def split_v(i, m):
                    dve.wait_ge(v_hi_ready, i * 4 + (r * KEYS + m + 1))
                    v.tensor_tensor(v_lo[:, m % 2, :], ring[:, (UV_AT[r] + m) % RING, D:2 * D], v_hi[:, m % 2, :],
                                    ALU.subtract).then_inc(v_lo_ready, 1)

                for tt in range(2):
                    picks_of(r, tt)
                split_u(0, 0)
                split_u(0, 1)
                split_v(0, 0)
                dve.wait_ge(pickt_copied, 2 * (r + 1))
                for half in range(HALVES):
                    g0 = (r * HALVES + half) * GROUPS
                    n0 = (r * HALVES + half) * ROWS

                    def rows(i, k):
                        if not isinstance(i, int) or g0 + k >= HOT:
                            dve.wait_ge(hot_used, i * HOT + (g0 + k + 1 - HOT))
                        toks = bass.ds(i * (8 * HOT) + k * 8, 8)
                        v.tensor_tensor(hot_i[:, k, :, :],
                                        iota[:, half * ROWS:(half + 1) * ROWS].unsqueeze(1).to_broadcast([P, 8, ROWS]),
                                        pickt[:, 0, toks].unsqueeze(2).to_broadcast([P, 8, ROWS]),
                                        ALU.is_equal).then_inc(hot_i_equal, 1)
                        v.tensor_tensor(hot_j[:, k, :, :], iota.unsqueeze(1).to_broadcast([P, 8, KEYS]),
                                        pickt[:, 1, toks].unsqueeze(2).to_broadcast([P, 8, KEYS]),
                                        ALU.is_equal).then_inc(hot_j_ready, 1)

                    if n0:
                        dve.wait_ge(w_ready, n0)
                    for k in range(HOT):
                        rows(0, k)
                    with dve.Fori(1, GROUPS // HOT) as i:
                        for k in range(HOT):
                            rows(i, k)
                    dve.wait_ge(gates_copied, g0 + GROUPS)

                    def tile(i, k, left=KEYS):
                        n = n0 + k
                        dve.wait_ge(gelu_done, i * 4 + (n + 1))
                        v.tensor_tensor(wfull[:, k % 2, :], ps[:, k, 0:N_LAT], gates[:, i * 4 + k, :], ALU.mult)\
                            .then_inc(w_full_ready, 1)
                        if not isinstance(i, int) or i * 4 + n >= 2:
                            dve.wait_ge(values_done, i * 4 + (n - 1))
                        dve.wait_ge(w_full_ready, i * 4 + (n + 1))
                        v.tensor_copy(w_hi[:, k % 2, :], wfull[:, k % 2, :]).then_inc(w_hi_ready, 1)
                        dve.wait_ge(w_hi_ready, i * 4 + (n + 1))
                        v.tensor_tensor(w_lo[:, k % 2, :], wfull[:, k % 2, :], w_hi[:, k % 2, :], ALU.subtract)\
                            .then_inc(w_ready, 1)
                        m = half * ROWS + k
                        if left > 2:
                            split_u(i, m + 2)
                        if left > 1:
                            split_v(i, m + 1)

                    for k in range(4):
                        tile(0, k)
                    with dve.Fori(1, ROWS // 4 - 1) as i:
                        for k in range(4):
                            tile(i, k)
                    for k in range(4):
                        tile(ROWS // 4 - 1, k, 4 - k if half == HALVES - 1 else KEYS)
                for c in range(DC):
                    dve.wait_ge(outt_done, DC // 2 * r + c // 2 + 1)
                    o = (c % 2) * 256
                    cols = slice(s * N_LAT, (s + 1) * N_LAT)
                    v.scalar_tensor_tensor(x[:, c, cols], ps[:, c // 2, o:o + N_LAT], modc[:, 5 * DC + c, s:s + 1],
                                           x[:, c, cols], ALU.mult, ALU.add).then_inc(x_ready, 1)

            dve.wait_ge(inputs_in, 64)
            lambdas()
            for l in range(DEPTH):
                modulation(l)
                norm((0, 3)[l], a1, [0, 1], h1)
                rope(l)
                attention(l)
                head_norm(l)
                merge(l)
                for r, (pl, s) in enumerate(PASSES):
                    if pl == l:
                        norm((1, 2, 4)[r], a2, [s], h2)
                        peer(r, l, s)
            dve.wait_ge(sq_summed, 6 * DC)
            inverse_root(root_at(5), ps[:, 0, 0:N_LAT], rstd[:, 0:N_LAT], D)
            for c in range(DC):
                last = v.scalar_tensor_tensor(h2[:, c, :], x[:, c, 0:N_LAT], small[:, C_GF + c:C_GF + c + 1],
                                              rstd[:, 0:N_LAT], ALU.mult, ALU.mult)
            last.then_inc(out_ready, 1)


IN_SPLITS = (512, 128, 128, 512, 512, 512, 512, 512, 512, 1024, 1024, 1024)


def blocks(w):
    return w.reshape(-1, P, P).transpose(1, 0, 2)


def head_order():
    return np.concatenate([np.arange(h * HD, (h + 1) * HD) for u in range(4) for h in (u, u + 4)])


def wide(w):
    n = w.shape[1] // 512
    return w.reshape(DC, P, n, 4, P).transpose(1, 2, 0, 3, 4).reshape(P, n * DC * 4, P)


def pairs(parts):
    whole = np.concatenate(parts, axis=1)
    return whole.reshape(P, -1, BLOCKS * P).transpose(1, 0, 2)


def weight_stream(w_in, wa, wb, wc, w_out, wq, keys):
    at = np.concatenate([[0], np.cumsum(IN_SPLITS)])
    part = [w_in[:, at[i]:at[i + 1]] for i in range(len(IN_SPLITS))]
    part[0] = part[0][:, head_order()]
    wa = wa[head_order(), :]
    which = {"aq": 0, "ak": 1, "bq": 3, "bk": 4, "cq": 6, "ck": 7}
    out = [blocks(part[which[name]][:, u * P:(u + 1) * P]) for name, u in UNITS]
    out.append(blocks(part[2]))
    for i in (5, 8):
        out.append(wide(part[i]))
    for j in range(DC):
        cols = slice(j * P, (j + 1) * P)
        for gate, branch in ((9, wa), (10, wb), (11, wc)):
            out += [blocks(part[gate][:, cols]), blocks(branch[:, cols])]
    out += [blocks(w_out[:, j * P:(j + 1) * P]) for j in range(DC)]
    out += [blocks(wq[:, u * P:(u + 1) * P]) for u in range(16)]
    out.append(keys.reshape(16, KEYS, P).transpose(2, 0, 1))
    return pairs(out)


def expert_pairs(u, v):
    ut = u.reshape(DEPTH, KEYS, KEYS, DC, P).transpose(0, 1, 4, 3, 2).reshape(DEPTH, KEYS, P, D)
    return np.concatenate([ut, v.reshape(DEPTH, KEYS, KEYS, D)], axis=3)


def bias_tiles(rpb):
    t = np.arange(N_LAT)
    row, col = t // GRID_W, t % GRID_W
    start = np.clip(col - 8, 0, GRID_W - 16)
    inside = (col[None, :] >= start[:, None]) & (col[None, :] < start[:, None] + 16)
    dr = row[None, :] - row[:, None] + 7
    dc = np.clip(col[None, :] - col[:, None], -15, 15) + 15
    n = rpb.shape[2] * rpb.shape[3]
    padded = np.concatenate([rpb.reshape(DEPTH, 8, n), np.full((DEPTH, 8, 1), NEG, rpb.dtype)], axis=2)
    full = padded[:, :, np.where(inside, dr * rpb.shape[3] + dc, n)]
    return np.ascontiguousarray(full.reshape(DEPTH, 4, 2, 2, P, N_LAT).transpose(0, 1, 3, 4, 2, 5))


def columns(v):
    return v.reshape(-1, P).T


def constants():
    out = np.zeros((P, K_ALL), np.float32)
    out[:, K_IDENT:K_IDENT + P] = np.eye(P)
    out[:, K_ONES:K_ONES + P] = 1.0
    out[:, K_IOTA:K_IOTA + P] = np.arange(P)
    for f in range(P):
        if f % HD < HD // 2:
            out[f + HD // 2, K_ROT + f] = -1.0
        else:
            out[f - HD // 2, K_ROT + f] = 1.0
    t = np.arange(N_LAT)
    n_freq = HD // 4
    inv = np.float32(10000.0) ** (-np.arange(n_freq, dtype=np.float32) / np.float32(n_freq))
    ang = np.concatenate([(t // GRID_W).astype(np.float32)[:, None] * inv,
                          (t % GRID_W).astype(np.float32)[:, None] * inv], axis=1)
    f = np.arange(P) % (HD // 2)
    out[:, K_COS:K_COS + N_LAT] = np.cos(ang).T[f]
    out[:, K_SIN:K_SIN + N_LAT] = np.sin(ang).T[f]
    far = np.abs(t[:, None] - t[None, :]) > 128
    out[:, K_MASK:K_MASK + 512] = np.where(far, NEG, 0.0).reshape(2, P, N_LAT).transpose(1, 0, 2).reshape(P, 512)
    return out


def kernel(**inputs):
    import concourse.bacc as bacc
    from concourse.bass_utils import run_bass_kernel_spmd

    a = {k: np.asarray(v) for k, v in inputs.items()}

    def feature_major(m):
        return m.T.reshape(DC, P, -1).transpose(1, 0, 2)

    x = np.ascontiguousarray(np.concatenate([feature_major(a["x"][0]), feature_major(a["ctx"][0])], axis=2))
    small = []
    for l in range(DEPTH):
        small += [columns(a["g_norm1"][l]), columns(a["g_norm2"][l]), columns(a["b_mod"][l]), columns(a["c_subln"][l])]
    small += [columns(a["g_final"]), np.stack([columns(a["c"][0]), columns(a["c_ctx"])], axis=2).reshape(P, 2 * DC)]
    sinks = a["a_sink"].reshape(DEPTH, 2, 4).transpose(0, 2, 1).reshape(1, DEPTH * 8)
    small.append(np.repeat(sinks, P, axis=0))
    mods = [pairs([wide(w)]) for w in a["w_mod"]]
    layers = [weight_stream(*[a[n][l] for n in (
        "w_in", "w_branch_a", "w_branch_b", "w_branch_c", "w_out", "peer_wq", "peer_keys")]) for l in range(DEPTH)]
    stream = np.concatenate([mods[0], layers[0], mods[1], layers[1]], axis=0)
    assert stream.shape[0] == DRAM_PAIRS
    arrays = {
        "x_in": x,
        "small_in": np.ascontiguousarray(np.concatenate(small, axis=1)),
        "lambda_in": np.repeat(a["c_lambda"].reshape(1, DEPTH, 4 * HD), P, axis=0),
        "const_in": constants(),
        "bias_in": bias_tiles(a["b_rpb"]),
        "stream_in": stream,
        "experts_in": expert_pairs(a["peer_u"], a["peer_v"]),
    }
    nc = bacc.Bacc("TRN2", target_bir_lowering=False, num_devices=1)
    args = [nc.dram_tensor(name, m.shape, mybir.dt.from_np(m.dtype), kind="ExternalInput").ap()
            for name, m in arrays.items()]
    out = nc.dram_tensor("out", (P, DC, N_LAT), mybir.dt.float32, kind="ExternalOutput").ap()
    build(nc, *args, out)
    res = run_bass_kernel_spmd(nc, [arrays], core_ids=[0])
    got = res.results[0]["out"]
    return np.ascontiguousarray(got.transpose(2, 1, 0).reshape(1, N_LAT, D))
```

```python
import math
from contextlib import ExitStack

import numpy as np
import concourse.bass as bass
from concourse import mybir

P = 128
D = 1024
DC = D // P
N_LAT = 256
N_CTX = 256
T = N_LAT + N_CTX
TT = T // P
DEPTH = 2
GRID_W = 64
HD = 64
KEYS = 128
PH = 8
TOPK = 16
HK = PH * TOPK
EPS = 1e-6
NEG = -1e30
USED = -3.0e38
LAM_INIT = [0.8 - 0.6 * math.exp(-0.3 * l) for l in range(DEPTH)]

RING = 4
BLOCKS = 16
PAIR = BLOCKS * P
MOD_UNITS = 6 * DC
MOD_PAIRS = MOD_UNITS // 2
QKV_PAIRS = 15
MERGE_PAIRS = 18
WOUT_PAIRS = 4
WQ_PAIRS = 8
HALVES = 2
ROWS = KEYS // HALVES
HOT = 4
GROUPS = N_LAT // 8
MOD_GROUPS = 6 * D // 512

UNITS = ([("aq", u) for u in range(4)] + [("ak", 0)] + [("bq", u) for u in range(4)] + [("bk", u) for u in range(4)]
         + [("cq", u) for u in range(4)] + [("ck", u) for u in range(4)])
NU = len(UNITS)
ROPED = [k for k, (name, _) in enumerate(UNITS) if name[0] != "b"]
UNIT_AT = {unit: k for k, unit in enumerate(UNITS)}

STREAMS = [[0, 1], [0]]
PASSES = [(0, 1), (0, 0), (1, 0)]
STEPS = [[(l, s, u, qt) for s in STREAMS[l] for u in range(12) for qt in range(2)] for l in range(DEPTH)]
STEP0 = [0, len(STEPS[0])]
BIASED = {}
for _l in range(DEPTH):
    for _n, (_, _s, _u, _q) in enumerate(STEPS[_l]):
        if _s == 0 and 4 <= _u < 8:
            BIASED[STEP0[_l] + _n] = len(BIASED)

RUNS, QKV_AT, MERGE_AT, WOUT_AT, WQ_AT, UV_AT = [], [], [], [], [], []
MOD_AT = [[], []]
KEYS_DRAM = []


def _number():
    at, dram = 0, 0

    def run(count, kind, l=0, again=None):
        nonlocal at, dram
        RUNS.append((at, count, kind, l, dram if again is None else again))
        at += count
        if kind != "experts" and again is None:
            dram += count
        return at - count

    for half in range(2):
        MOD_AT[0].append(run(MOD_PAIRS // 2, "raw"))
    for l in range(DEPTH):
        QKV_AT.append(run(QKV_PAIRS, "dense"))
        MERGE_AT.append(run(MERGE_PAIRS, "dense"))
        WOUT_AT.append(run(WOUT_PAIRS, "dense"))
        first = dram
        for n, stream in enumerate([1, 0] if l == 0 else [0]):
            again = first if n else None
            WQ_AT.append(run(WQ_PAIRS, "dense", again=again))
            KEYS_DRAM.append(first + WQ_PAIRS)
            if n == 0:
                dram += 1
            if l == 0:
                MOD_AT[1].append(run(MOD_PAIRS // 2, "raw", again=dram + n * MOD_PAIRS // 2))
                if n == 1:
                    dram += MOD_PAIRS
            UV_AT.append(run(KEYS, "experts", l))
    return at, dram


TOTAL_PAIRS, DRAM_PAIRS = _number()


def kind_of(p):
    return [kind for at, count, kind, _, _ in RUNS if at <= p < at + count][0]


def through(p):
    return sum(kind_of(q) == kind_of(p) for q in range(p + 1))


DENSE = [p for p in range(TOTAL_PAIRS) if kind_of(p) == "dense"]


def dense(p):
    return DENSE.index(p)


MERGE_BLOCK = [0]
for _i in range(6 * DC):
    MERGE_BLOCK.append(MERGE_BLOCK[-1] + (DC if _i % 2 == 0 else 4))
MERGE_ENDS = [[j for j in range(MERGE_PAIRS) if MERGE_BLOCK[i] < BLOCKS * (j + 1) <= MERGE_BLOCK[i + 1]]
              for i in range(6 * DC)]


C_G1, C_G2, C_BMOD, C_SUBLN = 0, DC, 2 * DC, 2 * DC + MOD_UNITS
C_LAYER = C_SUBLN + 4
C_GF = DEPTH * C_LAYER
C_COND = C_GF + DC
C_SINK = C_COND + 2 * DC
C_ALL = C_SINK + DEPTH * 8
K_IDENT, K_ONES, K_IOTA, K_ROT, K_ZERO, K_MASK, K_ALL = 0, 128, 256, 384, 512, 640, 1152


def build(nc, x_in, small_in, lambda_in, const_in_dram, rope_in, bias_in, stream_in, experts_in, out):
    fp32 = mybir.dt.float32
    fp32r = mybir.dt.float32r
    u32 = mybir.dt.uint32
    ALU = mybir.AluOpType
    ACT = mybir.ActivationFunctionType
    AX = mybir.AxisListType

    ctx = ExitStack()
    with ctx:
        def sb(name, shape, dt=fp32):
            return ctx.enter_context(nc.sbuf_tensor(name, shape, dt))

        def sem(name):
            return ctx.enter_context(nc.semaphore(name))

        x = sb("x", [P, DC, T])
        ring = sb("ring", [P, RING, PAIR])
        small = sb("small", [P, C_ALL])
        const = sb("const", [P, K_ALL])
        cond = sb("cond", [P, DC, 2])
        modc = sb("modc", [P, MOD_UNITS, 2])
        a1 = sb("a1", [P, DC, 2])
        a2 = sb("a2", [P, DC, 2])
        stat = sb("stat", [P, 2, 12])
        lam = sb("lam", [P, 12])
        ps = ctx.enter_context(nc.psum_tensor("ps", [P, 8, 512], fp32))

        ident = const[:, K_IDENT:K_IDENT + P]
        ones = const[:, K_ONES:K_ONES + P]
        iota = const[:, K_IOTA:K_IOTA + P]
        rot = const[:, K_ROT:K_ROT + P]
        zero = const[:, K_ZERO:K_ZERO + P]
        finite = const[:, 0:512]
        mask = const[:, K_MASK:K_MASK + 512].rearrange("p (q k) -> p q k", q=2)

        mod_raw = sb("mod_raw", [P, MOD_UNITS, 2])

        wt_hi = sb("wt_hi", [P, 2, PAIR], fp32r)
        wt_lo = sb("wt_lo", [P, 2, PAIR], fp32r)
        u_hi, v_hi = wt_hi[:, :, 0:D], wt_hi[:, :, D:2 * D]
        u_lo, v_lo = wt_lo[:, :, 0:D], wt_lo[:, :, D:2 * D]

        with nc.sbuf_tensor("att", [P, 30720], fp32) as big:
            pass
        with nc.sbuf_tensor("ys_hi", [P, 12, T], fp32r) as ys_hi, \
                nc.sbuf_tensor("ys_lo", [P, 12, T], fp32r) as ys_lo, \
                nc.sbuf_tensor("h1_hi", [P, DC, T], fp32r) as h1_hi, \
                nc.sbuf_tensor("h1_lo", [P, DC, T], fp32r) as h1_lo, \
                nc.sbuf_tensor("m_hi", [P, DC, T], fp32r) as m_hi, \
                nc.sbuf_tensor("m_lo", [P, DC, T], fp32r) as m_lo:
            pass
        first_hi, first_lo = m_hi, m_lo
        feat = big[:, 0:NU * T].rearrange("p (u t) -> p u t", u=NU)
        lambdas_sb = big[:, 0:DEPTH * 4 * HD].rearrange("p (l d) -> p l d", l=DEPTH)
        head_sq = big[:, 20 * T:24 * T].rearrange("p (h t) -> p h t", h=4)
        o = NU * T
        va = big[:, o:o + TT * 128].rearrange("p (t c) -> p t c", t=TT)
        vb = big[:, o + 512:o + 2560].rearrange("p (t c) -> p t c", t=TT)
        vc = big[:, o + 2560:o + 4608].rearrange("p (t c) -> p t c", t=TT)
        o += 4608
        prob = big[:, o:o + 2048].rearrange("p (b m k) -> p b m k", b=2, m=2)
        probt = big[:, o + 2048:o + 4096].rearrange("p (b m k) -> p b m k", b=2, m=2)
        sq = big[:, o:o + 1024].rearrange("p (b t) -> p b t", b=2)
        ropet = big[:, o + 1536:o + 2048].rearrange("p (b t) -> p b t", b=2)
        rope_tables = big[:, o + 3072:o + 3584]
        cos, sin = rope_tables[:, 0:N_LAT], rope_tables[:, N_LAT:2 * N_LAT]
        o += 4096
        bias = big[:, o:o + 1024].rearrange("p (b m k) -> p b m k", b=2, m=2)
        o += 1024
        yt = big[:, o:o + 12 * T].rearrange("p (u t) -> p u t", u=12)
        o += 12 * T
        head_diag = big[:, o:o + 2048].rearrange("p (h t k) -> p h t k", h=4, t=TT)
        o += 2048
        head_rstd = big[:, o + 1536:o + 1536 + 4 * TT].rearrange("p (h t) -> p h t", h=4)
        rstd = big[:, o:o + 512]
        chunk = big[:, o + 512:o + 1536].rearrange("p (b t) -> p b t", b=2)
        sig = big[:, o:o + 2048].rearrange("p (b t) -> p b t", b=4)
        big = sb("gate_region", [P, ROWS * N_LAT])
        pickt = sb("pickt", [P, 3, N_LAT])
        hots = sb("hots", [P, HOT * 8 * (ROWS + KEYS)])
        h_hi = sb("h_hi", [P, DC, N_LAT], fp32r)
        h_lo = sb("h_lo", [P, DC, N_LAT], fp32r)
        w_hi = sb("w_hi", [P, 2, N_LAT], fp32r)
        w_lo = sb("w_lo", [P, 2, N_LAT], fp32r)
        sb("norm_region", [P, 1792])
        wfull_region = sb("wfull", [P, 2 * N_LAT])
        final = big[:, 0:DC * N_LAT].rearrange("p (c t) -> p c t", c=DC)
        gates = big[:, 0:ROWS * N_LAT].rearrange("p (i t) -> p i t", i=ROWS)
        pq = big[:, 0:16 * N_LAT].rearrange("p (u t) -> p u t", u=16)
        o = 16 * N_LAT
        best = [big[:, at:at + 768].rearrange("p (w u k) -> p w u k", w=3, u=16) for at in (o, 14 * D)]
        o += 768
        work = big[:, o:o + 1024]
        cand = big[:, o + 1024:o + 1920].rearrange("p (h k) -> p h k", h=PH)
        tv = big[:, o + 1920:o + 2048].rearrange("p (h k) -> p h k", h=PH)
        pos = big[:, o + 2048:o + 2176].bitcast(u32)
        parts = big[:, o + 2176:o + 2688].bitcast(u32)
        partsf = big[:, o + 2688:o + 3200]
        places = big[:, o + 3200:o + 3456]
        hot = big[:, o + 3456:o + 5504].rearrange("p (h k i) -> p h k i", h=PH, k=TOPK)
        ex = big[:, o + 5504:o + 5632].rearrange("p (h k) -> p h k", h=PH)
        exs = big[:, o + 5632:o + 5648]
        picks = big[:, o + 5648:o + 6416].rearrange("p (b w k) -> p b w k", b=2, w=3)
        keys = big[:, 12 * D:14 * D]
        hot_i = hots[:, 0:HOT * 8 * ROWS].rearrange("p (b q i) -> p b q i", b=HOT, q=8)
        hot_j = hots[:, HOT * 8 * ROWS:].rearrange("p (b q j) -> p b q j", b=HOT, q=8)
        wfull = wfull_region[:, :].rearrange("p (b t) -> p b t", b=2)
        mod_rows = hots[0:2, 0:6 * D // 2]
        accs = hots[:, 0:2048].rearrange("p (b d) -> p b d", b=2)

        arrived = [sem(f"arrived{i}") for i in range(RING)]
        mod_pair_used = sem("mod_pair_used")
        small_in_sem = sem("small_in_sem")
        inputs_in = sem("inputs_in")
        bias_arrived = [sem(f"bias_arrived{i}") for i in range(2)]
        cond_ready = sem("cond_ready")
        mod_group_done = sem("mod_group_done")
        mod_row_copied = sem("mod_row_copied")
        mod_cols_done = sem("mod_cols_done")
        mod_cols_copied = sem("mod_cols_copied")
        mod_ready = sem("mod_ready")
        lam_dots = sem("lam_dots")
        lam_exps = sem("lam_exps")
        sq_ready = sem("sq_ready")
        inverse_ready = sem("inverse_ready")
        root_ready = sem("root_ready")
        sq_summed = sem("sq_summed")
        scaled = sem("scaled")
        shifted = sem("shifted")
        h_ready = sem("h_ready")
        proj_done = sem("proj_done")
        proj_copied = sem("proj_copied")
        rot_done = sem("rot_done")
        roped = sem("roped")
        v_done = sem("v_done")
        v_copied = sem("v_copied")
        scores_done = sem("scores_done")
        max_ready = sem("max_ready")
        exp_ready = sem("exp_ready")
        prob_ready = sem("prob_ready")
        probt_done = sem("probt_done")
        probt_copied = sem("probt_copied")
        y_done = sem("y_done")
        y_copied = sem("y_copied")
        cn_sq = sem("cn_sq")
        cn_sum = sem("cn_sum")
        head_diag_ready = sem("head_diag_ready")
        head_spread = sem("head_spread")
        cn_ready = sem("cn_ready")
        merge_done = sem("merge_done")
        sig_ready = sem("sig_ready")
        prod_done = sem("prod_done")
        m_ready = sem("m_ready")
        wout_done = sem("wout_done")
        x_ready = sem("x_ready")
        pq_done = sem("pq_done")
        pq_copied = sem("pq_copied")
        keys_done = sem("keys_done")
        keys_in = sem("keys_in")
        sides_found = sem("sides_found")
        topd_ready = sem("topd_ready")
        topexp_ready = sem("topexp_ready")
        picks_ready = sem("picks_ready")
        pickt_done = sem("pickt_done")
        pickt_copied = sem("pickt_copied")
        hot_j_ready = sem("hot_j_ready")
        hot_i_equal = sem("hot_i_equal")
        hot_i_ready = sem("hot_i_ready")
        hot_used = sem("hot_used")
        dense_hi_ready = sem("dense_hi_ready")
        dense_lo_ready = sem("dense_lo_ready")
        rope_in_sem = sem("rope_in_sem")
        v_half_done = sem("v_half_done")
        y_hi_ready = sem("y_hi_ready")
        y_lo_ready = sem("y_lo_ready")
        added = sem("added")
        m_hi_ready = sem("m_hi_ready")
        u_hi_ready = sem("u_hi_ready")
        u_lo_ready = sem("u_lo_ready")
        v_hi_ready = sem("v_hi_ready")
        v_lo_ready = sem("v_lo_ready")
        w_full_ready = sem("w_full_ready")
        w_hi_ready = sem("w_hi_ready")
        values_done = sem("values_done")
        gates_copied = sem("gates_copied")
        s_done = sem("s_done")
        gelu_done = sem("gelu_done")
        w_ready = sem("w_ready")
        acc_done = sem("acc_done")
        acc_copied = sem("acc_copied")
        outt_done = sem("outt_done")
        out_ready = sem("out_ready")
        out_stored = sem("out_stored")
        dve_order = sem("dve_order")
        act_order = sem("act_order")

        def wait_pair(eng, p, i=0):
            eng.wait_ge(arrived[p % RING], i * 16 + 16 * (p // RING + 1))

        def root_at(n=None, l=None):
            return (0, 2, 3, 4, 6, 7)[n] if n is not None else (1, 5)[l]

        def used(d):
            p = DENSE[d]
            for l in range(DEPTH):
                j = p - QKV_AT[l]
                if 0 <= j < 10:
                    return proj_done, l * NU + 2 * j + 2
                if j == 10:
                    return v_done, 9 * l + 1
                if j in (11, 13):
                    return v_half_done, 2 * l + (j - 11) // 2 + 1
                if j in (12, 14):
                    return v_done, 9 * l + 1 + 4 * (j - 10) // 2
                j = p - MERGE_AT[l]
                if 0 <= j < MERGE_PAIRS:
                    item = [i for i in range(6 * DC) if j in MERGE_ENDS[i]][0]
                    return merge_done, 6 * DC * l + item + 1
                j = p - WOUT_AT[l]
                if 0 <= j < WOUT_PAIRS:
                    return wout_done, DC * l + 2 * j + 2
            r = [r for r in range(3) if 0 <= p - WQ_AT[r] < WQ_PAIRS][0]
            return pq_done, 16 * r + 2 * (p - WQ_AT[r]) + 2

        def dense_slot(p, b):
            d = dense(p + b // BLOCKS)
            cols = slice((b % BLOCKS) * P, (b % BLOCKS + 1) * P)
            return wt_hi[:, d % 2, cols], wt_lo[:, d % 2, cols]

        def event(n, again=False):
            return (0, 2, 3, 4, 6)[n] + again

        def norm_x(n):
            return [(0, 0, T), (8, N_LAT, T), (16, 0, N_LAT), (24, 0, T), (32, 0, N_LAT), (40, 0, N_LAT)][n]

        def sums_bank(n):
            return 4 if n in (2, 3, 5) else 0

        block = ctx.enter_context(nc.Block())

        @block.sync
        def _(sp):
            sp.dma_start(small[:, :], small_in).then_inc(small_in_sem, 16)
            sp.dma_start(lambdas_sb, lambda_in).then_inc(inputs_in, 16)

            def load(p, src, i=0):
                if p >= RING:
                    held = p - RING
                    n, kind = through(held), kind_of(held)
                    if kind == "raw":
                        sp.wait_ge(mod_pair_used if n % 2 else mod_group_done, i * (RING // 2) + (n + 1) // 2)
                    else:
                        sp.wait_ge(dense_lo_ready if kind == "dense" else v_lo_ready, i * RING + n)
                sp.dma_start(ring[:, p % RING, :], src).then_inc(arrived[p % RING], 16)

            for p, count, kind, l, first in RUNS:
                def src(k):
                    return experts_in[l, k, :, :] if kind == "experts" else stream_in[first + k, :, :]
                for k in range(min(count, RING)):
                    load(p + k, src(k))
                rounds = count // RING
                if rounds > 1:
                    with sp.Fori(0, rounds - 1) as i:
                        for k in range(RING):
                            load(p + RING + k, src(i * RING + RING + k), i)
                for k in range(max(rounds, 1) * RING, count):
                    load(p + k, src(k))
            sp.wait_ge(out_ready, 1)
            sp.dma_start(out, final).then_inc(out_stored, 16)
            sp.wait_ge(out_stored, 16)

        @block.tensor
        def _(pe):
            mm = nc.tensor.matmul

            def mm3(dst, a, b, start, stop):
                mm(dst, a[0], b[0], start=start, stop=False)
                mm(dst, a[0], b[1], start=False, stop=False)
                return mm(dst, a[1], b[0], start=False, stop=stop)

            def wait_dense(p):
                pe.wait_ge(dense_lo_ready, dense(p) + 1)

            def mod(l, half, banks):
                p0 = MOD_AT[l][half]
                done = (2 * l + half) * (MOD_GROUPS // 2)
                for g in range(MOD_GROUPS // 2):
                    if g >= 2:
                        pe.wait_ge(mod_row_copied, done + g - 1)
                    for c in range(DC):
                        q = p0 + 2 * g + c // 4
                        if c % 4 == 0:
                            wait_pair(pe, q)
                        last = mm(ps[0:2, banks[g % 2], :], cond[:, c, :],
                                  ring[:, q % RING, (c % 4) * 512:(c % 4 + 1) * 512],
                                  start=(c == 0), stop=(c == DC - 1))
                        if c == 3:
                            last.then_inc(mod_pair_used, 1)
                    last.then_inc(mod_group_done, 1)
                pe.wait_ge(mod_row_copied, done + MOD_GROUPS // 2)
                pe.wait_ge(inputs_in, 48)
                for u in range(MOD_UNITS // 2):
                    last = nc.tensor.transpose(ps[:, banks[0], 2 * u:2 * u + 2], mod_rows[:, u * P:(u + 1) * P],
                                               ident[0:2, 0:2])
                last.then_inc(mod_cols_done, 1)

            def sums(n):
                _, c0, c1 = norm_x(n)
                for c in range(DC):
                    m = n * DC + c
                    pe.wait_ge(sq_ready, m + 1)
                    mm(ps[:, sums_bank(n), 0:c1 - c0], ones, sq[:, c % 2, 0:c1 - c0], start=(c == 0), stop=(c == DC - 1))\
                        .then_inc(sq_summed, 1)

            def proj(l):
                p0 = QKV_AT[l]

                def rotate(r):
                    k = ROPED[r]
                    g = l * len(ROPED) + r
                    pe.wait_ge(proj_copied, l * NU + k + 1)
                    if g >= 2:
                        pe.wait_ge(roped, g - 1)
                    mm(ps[:, 4 + g % 2, 0:N_LAT], rot, feat[:, k, 0:N_LAT], start=True, stop=True)\
                        .then_inc(rot_done, 1)

                def h1(c, cols):
                    return first_hi[:, c, cols], first_lo[:, c, cols]

                turn = 0
                for k, (name, u) in enumerate(UNITS):
                    n = N_LAT if (l == DEPTH - 1 and name[1] == "q") else T
                    if k % 2 == 0:
                        wait_dense(p0 + k // 2)
                    if k >= 4:
                        pe.wait_ge(proj_copied, l * NU + k - 3)
                    for c in range(DC):
                        if k == 0:
                            pe.wait_ge(h_ready, event((0, 3)[l]) * DC + c + 1)
                        last = mm3(ps[:, k % 4, 0:n], dense_slot(p0, k * DC + c), h1(c, slice(0, n)),
                                   c == 0, c == DC - 1)
                    last.then_inc(proj_done, 1)
                    while turn < len(ROPED) and ROPED[turn] < k:
                        rotate(turn)
                        turn += 1
                for t in range(TT):
                    for c in range(DC):
                        last = mm3(ps[:, 6, t * P:(t + 1) * P], h1(c, slice(t * P, (t + 1) * P)),
                                   dense_slot(p0, NU * DC + c), c == 0, c == DC - 1)
                last.then_inc(v_done, 1)
                while turn < len(ROPED):
                    rotate(turn)
                    turn += 1
                for w in range(2):
                    q0 = p0 + 11 + 2 * w
                    if w == 0:
                        pe.wait_ge(proj_copied, l * NU + NU)
                    else:
                        pe.wait_ge(roped, (l + 1) * len(ROPED))
                        pe.wait_ge(v_copied, 9 * l + 1)
                    for c in range(DC):
                        if c % 4 == 0:
                            wait_dense(q0 + c // 4)
                        d = dense(q0 + c // 4) % 2
                        cols = slice((c % 4) * 512, (c % 4 + 1) * 512)
                        for t in range(TT):
                            last = mm3(ps[:, 4 * w + t, :], h1(c, slice(t * P, (t + 1) * P)),
                                       (wt_hi[:, d, cols], wt_lo[:, d, cols]), c == 0, c == DC - 1)
                            if c == DC - 1:
                                last.then_inc(v_done, 1)
                        if c == 3:
                            last.then_inc(v_half_done, 1)

            def attention(l):
                steps = STEPS[l]

                def keys_of(s):
                    return (0, T) if s == 0 else (N_LAT, T)

                def scores(n):
                    _, s, u, qt = steps[n]
                    a = STEP0[l] + n
                    k0, k1 = keys_of(s)
                    q = UNIT_AT[("abc"[u // 4] + "q", u % 4)]
                    k = UNIT_AT[("abc"[u // 4] + "k", 0 if u < 4 else u % 4)]
                    if n >= 2:
                        pe.wait_ge(exp_ready, a - 1)
                    t0 = s * N_LAT + qt * P
                    for m in range(2):
                        last = mm(ps[:, 2 * (a % 2) + m, 0:k1 - k0], feat[64 * m:64 * m + 64, q, t0:t0 + P],
                                  feat[64 * m:64 * m + 64, k, k0:k1], start=True, stop=True)
                    last.then_inc(scores_done, 1)

                def transposes(n):
                    _, s, u, qt = steps[n]
                    a = STEP0[l] + n
                    k0, k1 = keys_of(s)
                    pe.wait_ge(prob_ready, a + 1)
                    if a >= 1:
                        pe.wait_ge(probt_copied, a)
                    for m in range(2 if u < 8 else 1):
                        for t in range((k1 - k0) // P):
                            last = nc.tensor.transpose(ps[:, 4 + m, t * P:(t + 1) * P],
                                                       prob[:, a % 2, m, t * P:(t + 1) * P], ident)
                    last.then_inc(probt_done, 1)

                def values(n):
                    _, s, u, qt = steps[n]
                    a = STEP0[l] + n
                    k0, k1 = keys_of(s)
                    nt = (k1 - k0) // P
                    pe.wait_ge(probt_copied, a + 1)
                    if a >= 2:
                        pe.wait_ge(y_copied, a - 1)
                    y = ps[:, 6 + a % 2, 0:P]
                    for m in range(2 if u < 8 else 1):
                        for t in range(nt):
                            tile = k0 // P + t
                            if u < 4:
                                v, rows = va[:, tile, 64 * m:64 * m + 64], slice(64 * m, 64 * m + 64)
                            elif u < 8:
                                c0 = 128 * (u - 4) + 64 * m
                                v, rows = vb[:, tile, c0:c0 + 64], slice(64 * m, 64 * m + 64)
                            else:
                                v, rows = vc[:, tile, 128 * (u - 8):128 * (u - 7)], slice(0, 128)
                            last = mm(y[rows, :], v, probt[:, a % 2, m, t * P:(t + 1) * P],
                                      start=(t == 0), stop=(t == nt - 1))
                    last.then_inc(y_done, 1)

                pe.wait_ge(roped, (l + 1) * len(ROPED))
                pe.wait_ge(v_copied, 9 * (l + 1))
                scores(0)
                scores(1)
                for n in range(len(steps)):
                    if n + 2 < len(steps):
                        scores(n + 2)
                    transposes(n)
                    if n >= 1:
                        values(n - 1)
                values(len(steps) - 1)

            def head_norm(l):
                n = T if len(STREAMS[l]) == 2 else N_LAT
                for h in range(4):
                    pe.wait_ge(cn_sq, 4 * l + h + 1)
                    for t in range(n // P):
                        last = mm(ps[:, 4, h * TT + t:h * TT + t + 1], head_sq[:, h, t * P:(t + 1) * P],
                                  ones[:, 0:1], start=True, stop=True)
                last.then_inc(cn_sum, 1)
                for h in range(4):
                    pe.wait_ge(head_diag_ready, 4 * l + h + 1)
                    mm(ps[:, 4 + h, 0:n], ones, head_diag[:, h, 0:n // P, :].rearrange("p t k -> p (t k)"),
                       start=True, stop=True).then_inc(head_spread, 1)

            def merge(l):
                n = T if len(STREAMS[l]) == 2 else N_LAT
                p0 = MERGE_AT[l]
                for item in range(6 * DC):
                    branch = item % 6 // 2
                    bank = item % 8
                    if 4 <= item < 8:
                        pe.wait_ge(cn_ready, 4 * l + item - 3)
                    if item >= 8:
                        pe.wait_ge(prod_done, 3 * DC * l + (item - 8) // 2 + 1)
                    if item in (1, 3, 5):
                        pe.wait_ge(y_lo_ready, 12 * l + 4 * (branch + 1))
                    count = DC if item % 2 == 0 else 4
                    for c in range(count):
                        b = MERGE_BLOCK[item] + c
                        if b % BLOCKS == 0:
                            wait_dense(p0 + b // BLOCKS)
                        if item == 0:
                            pe.wait_ge(h_ready, event((0, 3)[l], True) * DC + c + 1)
                        if item % 2 == 0:
                            src = h1_hi[:, c, 0:n], h1_lo[:, c, 0:n]
                        else:
                            src = ys_hi[:, 4 * branch + c, 0:n], ys_lo[:, 4 * branch + c, 0:n]
                        last = mm3(ps[:, bank, 0:n], dense_slot(p0, b), src, c == 0, c == count - 1)
                    last.then_inc(merge_done, 1)

            def w_out(l):
                n = T if len(STREAMS[l]) == 2 else N_LAT
                p0 = WOUT_AT[l]
                pe.wait_ge(m_ready, DC * (l + 1))
                for j in range(DC):
                    if j % 2 == 0:
                        wait_dense(p0 + j // 2)
                    for c in range(DC):
                        last = mm3(ps[:, j, 0:n], dense_slot(p0, j * DC + c), (m_hi[:, c, 0:n], m_lo[:, c, 0:n]),
                                   c == 0, c == DC - 1)
                    last.then_inc(wout_done, 1)

            def key_scores(r, g):
                pe.wait_ge(keys_in, 16 * (r + 1))
                pe.wait_ge(pq_copied, 16 * r + 4 * g + 4)
                for tt in range(2):
                    n = 2 * g + tt
                    if n >= 6:
                        pe.wait_ge(sides_found, 8 * r + n - 5)
                    for u in range(4 * g, 4 * g + 4):
                        last = mm(ps[:, 2 + n % 6, (u % 4) * P:(u % 4 + 1) * P], pq[:, u, tt * P:(tt + 1) * P],
                                  keys[:, u * P:(u + 1) * P], start=True, stop=True)
                    last.then_inc(keys_done, 1)

            def peer(r):
                p0 = WQ_AT[r]
                for u in range(16):
                    if u % 2 == 0:
                        wait_dense(p0 + u // 2)
                    if u >= 2:
                        pe.wait_ge(pq_copied, 16 * r + u - 1)
                    for c in range(DC):
                        if u == 0:
                            pe.wait_ge(h_ready, event((1, 2, 4)[r]) * DC + c + 1)
                        last = mm3(ps[:, u % 2, 0:N_LAT], dense_slot(p0, u * DC + c), (h_hi[:, c, :], h_lo[:, c, :]),
                                   c == 0, c == DC - 1)
                    last.then_inc(pq_done, 1)
                    if u % 4 == 0 and u:
                        key_scores(r, u // 4 - 1)
                key_scores(r, 3)
                if r < 2:
                    mod(1, r, (0, 1))
                    pe.wait_ge(mod_cols_copied, 3 + r)
                for tt in range(2):
                    pe.wait_ge(picks_ready, 2 * r + tt + 1)
                    for w in range(3):
                        last = nc.tensor.transpose(ps[:, 2 + tt, w * P:(w + 1) * P], picks[:, tt, w, :], ident)
                    last.then_inc(pickt_done, 1)
                pe.wait_ge(pickt_copied, 2 * (r + 1))
                for b in range(4):
                    mm(ps[:, 4 + b, :], zero, finite, start=True, stop=False)

                for half in range(HALVES):
                    g0 = (r * HALVES + half) * GROUPS
                    n0 = (r * HALVES + half) * ROWS

                    def gate_group(i, k):
                        pe.wait_ge(hot_j_ready, i * HOT + (g0 + k + 1))
                        pe.wait_ge(hot_i_ready, i * HOT + (g0 + k + 1))
                        if not isinstance(i, int) or g0 + k >= HOT:
                            pe.wait_ge(gates_copied, i * HOT + (g0 + k + 1 - HOT))
                        for q in range(8):
                            last = mm(ps[:, k, q * ROWS:(q + 1) * ROWS], hot_j[:, k, q, :], hot_i[:, k, q, :],
                                      start=True, stop=True)
                        last.then_inc(hot_used, 1)

                    for k in range(HOT):
                        gate_group(0, k)
                    with pe.Fori(1, GROUPS // HOT) as i:
                        for k in range(HOT):
                            gate_group(i, k)
                    pe.wait_ge(gates_copied, g0 + GROUPS)

                    def expert_scores(i, k):
                        pe.wait_ge(u_lo_ready, i * 4 + (n0 + k + 1))
                        if not isinstance(i, int) or n0 + k >= 4:
                            pe.wait_ge(w_full_ready, i * 4 + (n0 + k - 3))
                        for c in range(DC):
                            cols = slice(c * P, (c + 1) * P)
                            last = mm3(ps[:, k, 0:N_LAT], (u_hi[:, k % 2, cols], u_lo[:, k % 2, cols]),
                                       (h_hi[:, c, :], h_lo[:, c, :]), c == 0, c == DC - 1)
                        last.then_inc(s_done, 1)

                    def expert_values(i, k):
                        pe.wait_ge(v_lo_ready, i * 4 + (n0 + k + 1))
                        pe.wait_ge(w_ready, i * 4 + (n0 + k + 1))
                        for tt in range(2):
                            toks = slice(tt * P, (tt + 1) * P)
                            for w, v in ((w_hi, v_hi), (w_hi, v_lo), (w_lo, v_hi)):
                                for d in range(2):
                                    last = mm(ps[:, 4 + 2 * tt + d, :], w[:, k % 2, toks],
                                              v[:, k % 2, 512 * d:512 * (d + 1)], start=False, stop=False)
                        last.then_inc(values_done, 1)

                    expert_scores(0, 0)
                    for k in range(1, 4):
                        expert_scores(0, k)
                        expert_values(0, k - 1)
                    with pe.Fori(1, ROWS // 4) as i:
                        for k in range(4):
                            expert_scores(i, k)
                            if k == 0:
                                expert_values(i - 1, 3)
                            else:
                                expert_values(i, k - 1)
                    expert_values(ROWS // 4 - 1, 3)
                for b in range(4):
                    last = mm(ps[:, 4 + b, :], zero, finite, start=False, stop=True)
                last.then_inc(acc_done, 1)
                for c in range(DC):
                    if c == 0:
                        pe.wait_ge(acc_copied, 4 * (r + 1))
                    for tt in range(2):
                        o = (c % 2) * 256 + tt * P
                        last = nc.tensor.transpose(ps[:, c // 2, o:o + P], accs[:, tt, c * P:(c + 1) * P], ident)
                    if c % 2 == 1:
                        last.then_inc(outt_done, 1)

            pe.wait_ge(cond_ready, 1)
            for l in range(DEPTH):
                if l == 0:
                    mod(0, 0, (6, 7))
                sums((0, 3)[l])
                if l == 0:
                    pe.wait_ge(mod_cols_copied, 1)
                    mod(0, 1, (6, 7))
                proj(l)
                attention(l)
                head_norm(l)
                merge(l)
                w_out(l)
                for r, (pl, s) in enumerate(PASSES):
                    if pl == l:
                        sums((1, 2, 4)[r])
                        peer(r)
            sums(5)

        @block.scalar
        def _(act):
            act.dma_start(const[:, :], const_in_dram).then_inc(inputs_in, 16)
            act.dma_start(x[:, :, :], x_in).then_inc(inputs_in, 16)
            order = [0]

            def link(ins):
                order[0] += 1
                ins.then_inc(act_order, 1)
                act.wait_ge(act_order, order[0])

            def root(at, w):
                act.wait_ge(inverse_ready, at + 1)
                nc.scalar.activation(rstd[:, 0:w], rstd[:, 0:w], ACT.Sqrt).then_inc(root_ready, 1)

            def split(d, first=False):
                if not first:
                    act.wait_ge(*used(d - 2))
                wait_pair(act, DENSE[d])
                nc.scalar.activation(wt_hi[:, d % 2, :], ring[:, DENSE[d] % RING, :], ACT.Copy)\
                    .then_inc(dense_hi_ready, 1)

            def squares(n):
                need, c0, c1 = norm_x(n)
                for c in range(DC):
                    m = n * DC + c
                    if need:
                        act.wait_ge(x_ready, need - DC + c + 1)
                    if m >= 2:
                        act.wait_ge(sq_summed, m - 1)
                    nc.scalar.activation(sq[:, c % 2, 0:c1 - c0], x[:, c, c0:c1], ACT.Square).then_inc(sq_ready, 1)
                if n:
                    root(root_at(n), c1 - c0)

            def mod_half(l, half, banks, between=None):
                done = (2 * l + half) * (MOD_GROUPS // 2)
                for g in range(MOD_GROUPS // 2):
                    act.wait_ge(mod_group_done, done + g + 1)
                    if g == 0 and done:
                        act.wait_ge(mod_cols_done, 2 * l + half)
                    nc.scalar.activation(mod_rows[:, g * 512:(g + 1) * 512], ps[0:2, banks[g % 2], :], ACT.Copy)\
                        .then_inc(mod_row_copied, 1)
                    if g == 3 and between:
                        between()
                act.wait_ge(mod_cols_done, 2 * l + half + 1)
                first = half * MOD_UNITS // 2
                if l and half == 0:
                    act.wait_ge(mod_ready, l)
                nc.scalar.activation(mod_raw[:, first:first + MOD_UNITS // 2, :],
                                     ps[:, banks[0], 0:MOD_UNITS].rearrange("p (u s) -> p u s", s=2),
                                     ACT.Copy).then_inc(mod_cols_copied, 1)

            def shifts(e, l, kind, streams, dst):
                w = len(streams) * N_LAT
                for c in range(DC):
                    m = e * DC + c
                    act.wait_ge(scaled, m + 1)
                    for at, s in enumerate(streams):
                        o = chunk[:, c % 2, at * N_LAT:(at + 1) * N_LAT]
                        shift = modc[:, kind * DC + c, s:s + 1]
                        nc.scalar.activation(dst[:, c, at * N_LAT:(at + 1) * N_LAT], o, ACT.Identity, bias=shift)
                        last = nc.scalar.activation(o, o, ACT.Identity, bias=shift)
                    last.then_inc(shifted, 1)

            act.wait_ge(small_in_sem, 16)
            nc.scalar.activation(cond[:, :, :], small[:, C_COND:C_COND + 2 * DC].rearrange("p (c s) -> p c s", s=2),
                                 ACT.Silu).then_inc(cond_ready, 1)
            act.wait_ge(lam_dots, 1)
            nc.scalar.activation(lam[:, 4:8], lam[:, 0:4], ACT.Exp).then_inc(lam_exps, 1)
            for l in range(DEPTH):
                streams = STREAMS[l]
                n = T if len(streams) == 2 else N_LAT
                if l == 0:
                    mod_half(0, 0, (6, 7))
                    act.wait_ge(inputs_in, 48)
                squares((0, 3)[l])
                if l == 0:
                    root(root_at(0), T)
                    mod_half(0, 1, (6, 7))
                split(dense(QKV_AT[l]), True)
                shifts(event((0, 3)[l]), l, 0, [0, 1], first_hi)
                split(dense(QKV_AT[l]) + 1, True)
                for k, (name, u) in enumerate(UNITS):
                    w = N_LAT if (l == DEPTH - 1 and name[1] == "q") else T
                    act.wait_ge(proj_done, l * NU + k + 1)
                    nc.scalar.activation(feat[:, k, 0:w], ps[:, k % 4, 0:w], ACT.Copy,
                                         scale=HD ** -0.5 if name[1] == "q" else 1.0).then_inc(proj_copied, 1)
                    if k % 2 == 1:
                        split(dense(QKV_AT[l]) + k // 2 + 2)
                for j in range(12, QKV_PAIRS + 2):
                    split(dense(QKV_AT[l]) + j)
                steps = STEPS[l]

                def exps(i):
                    _, s, u, qt = steps[i]
                    a = STEP0[l] + i
                    nk = T if s == 0 else N_CTX
                    act.wait_ge(max_ready, a + 1)
                    if i >= 2:
                        act.wait_ge(probt_done, a - 1)
                    st = stat[:, a % 2, :]
                    if u < 4:
                        nc.scalar.activation(st[:, 6:8], st[:, 10:12], ACT.Exp)
                    for m in range(2):
                        last = nc.scalar.activation(prob[:, a % 2, m, 0:nk], ps[:, 2 * (a % 2) + m, 0:nk], ACT.Exp,
                                                    bias=st[:, 2 + m:3 + m], accum_out=st[:, 4 + m:5 + m])
                    last.then_inc(exp_ready, 1)

                def copy_probt(i):
                    _, s, u, qt = steps[i]
                    a = STEP0[l] + i
                    nk = T if s == 0 else N_CTX
                    m = 2 if u < 8 else 1
                    act.wait_ge(probt_done, a + 1)
                    if a >= 2:
                        act.wait_ge(y_done, a - 1)
                    nc.scalar.activation(probt[:, a % 2, 0:m, 0:nk], ps[:, 4:4 + m, 0:nk], ACT.Copy)\
                        .then_inc(probt_copied, 1)

                exps(0)
                for i in range(len(steps)):
                    if i + 1 < len(steps):
                        exps(i + 1)
                    copy_probt(i)
                act.wait_ge(y_copied, STEP0[l] + len(steps))
                for h in range(4):
                    nc.scalar.activation(head_sq[:, h, 0:n], yt[:, 8 + h, 0:n], ACT.Square).then_inc(cn_sq, 1)
                act.wait_ge(inverse_ready, root_at(l=l) + 1)
                nc.scalar.activation(head_rstd[:, :, 0:n // P], head_rstd[:, :, 0:n // P], ACT.Sqrt)\
                    .then_inc(root_ready, 1)
                shifts(event((0, 3)[l], True), l, 0, streams, h1_hi)
                for u in range(12):
                    if u >= 8:
                        act.wait_ge(cn_ready, 4 * l + u - 7)
                    nc.scalar.activation(ys_hi[:, u, 0:n], yt[:, u, 0:n], ACT.Copy).then_inc(y_hi_ready, 1)

                def m_high(j):
                    act.wait_ge(added, 2 * (DC * l + j + 1))
                    nc.scalar.activation(m_hi[:, j, 0:n], sig[:, (3 * j + 2) % 4, 0:n], ACT.Copy).then_inc(m_hi_ready, 1)

                act.wait_ge(h_ready, event((0, 3)[l], True) * DC + DC)
                for item in range(6 * DC):
                    if item % 2 == 0:
                        g = item // 2
                        act.wait_ge(merge_done, 6 * DC * l + item + 1)
                        if g >= 4:
                            j, b = (g - 4) // 3, (g - 4) % 3
                            if b < 2:
                                act.wait_ge(added, 2 * (DC * l + j) + b + 1)
                            else:
                                act.wait_ge(m_ready, DC * l + j + 1)
                        nc.scalar.activation(sig[:, g % 4, 0:n], ps[:, item % 8, 0:n], ACT.Sigmoid)\
                            .then_inc(sig_ready, 1)
                    for j in MERGE_ENDS[item]:
                        split(dense(MERGE_AT[l]) + j + 2)
                    if item % 6 == 2 and item > 6:
                        m_high(item // 6 - 1)
                m_high(DC - 1)
                for j in range(WOUT_PAIRS):
                    split(dense(WOUT_AT[l]) + j + 2)
                for r, (pl, s) in enumerate(PASSES):
                    if pl != l:
                        continue
                    squares((1, 2, 4)[r])
                    if r == 1:
                        split(dense(WQ_AT[r]), True)
                    shifts(event((1, 2, 4)[r]), l, 3, [s], h_hi)
                    if r == 1:
                        split(dense(WQ_AT[r]) + 1, True)
                    for u in range(16):
                        act.wait_ge(pq_done, 16 * r + u + 1)
                        nc.scalar.activation(pq[:, u, :], ps[:, u % 2, 0:N_LAT], ACT.Copy).then_inc(pq_copied, 1)
                        if u % 2 == 1 and u // 2 + 2 < WQ_PAIRS:
                            split(dense(WQ_AT[r]) + u // 2 + 2)

                    def split_u(i, m):
                        wait_pair(act, UV_AT[r] + m, i)
                        if not isinstance(i, int) or i * 4 + r * KEYS + m >= 2:
                            act.wait_ge(s_done, i * 4 + (r * KEYS + m - 1))
                        nc.scalar.activation(u_hi[:, m % 2, :], ring[:, (UV_AT[r] + m) % RING, 0:D], ACT.Copy)\
                            .then_inc(u_hi_ready, 1)

                    def split_v(i, m):
                        if not isinstance(i, int) or i * 4 + r * KEYS + m >= 2:
                            act.wait_ge(values_done, i * 4 + (r * KEYS + m - 1))
                        nc.scalar.activation(v_hi[:, m % 2, :], ring[:, (UV_AT[r] + m) % RING, D:2 * D], ACT.Copy)\
                            .then_inc(v_hi_ready, 1)

                    def pick_exps(tt):
                        act.wait_ge(topd_ready, 2 * r + tt + 1)
                        nc.scalar.activation(ex, tv, ACT.Exp).then_inc(topexp_ready, 1)

                    if r < 2:
                        mod_half(1, r, (0, 1), lambda: pick_exps(0))
                    split_u(0, 0)
                    split_u(0, 1)
                    split_v(0, 0)
                    if r == 2:
                        pick_exps(0)
                    pick_exps(1)
                    for tt in range(2):
                        act.wait_ge(pickt_done, 2 * r + tt + 1)
                        nc.scalar.activation(pickt[:, :, tt * P:(tt + 1) * P],
                                             ps[:, 2 + tt, 0:3 * P].rearrange("p (w t) -> p w t", w=3),
                                             ACT.Copy).then_inc(pickt_copied, 1)
                    for half in range(HALVES):
                        g0 = (r * HALVES + half) * GROUPS
                        n0 = (r * HALVES + half) * ROWS

                        def copy_gates(i, k):
                            act.wait_ge(hot_used, i * HOT + (g0 + k + 1))
                            nc.scalar.activation(gates[:, :, bass.ds(i * (8 * HOT) + k * 8, 8)],
                                                 ps[:, k, :].rearrange("p (q i) -> p i q", q=8),
                                                 ACT.Copy).then_inc(gates_copied, 1)

                        if half:
                            act.wait_ge(w_full_ready, n0)
                        with act.Fori(0, GROUPS // HOT) as i:
                            for k in range(HOT):
                                copy_gates(i, k)

                        def tile(i, k, left=KEYS):
                            act.wait_ge(s_done, i * 4 + (n0 + k + 1))
                            nc.scalar.activation(ps[:, k, 0:N_LAT], ps[:, k, 0:N_LAT], ACT.Gelu)\
                                .then_inc(gelu_done, 1)
                            m = half * ROWS + k
                            if left > 2:
                                split_u(i, m + 2)
                            if left > 1:
                                split_v(i, m + 1)

                        with act.Fori(0, ROWS // 4 - 1) as i:
                            for k in range(4):
                                tile(i, k)
                        for k in range(4):
                            tile(ROWS // 4 - 1, k, 4 - k if half == HALVES - 1 else KEYS)
                    act.wait_ge(acc_done, r + 1)
                    for b in range(4):
                        nc.scalar.activation(accs[:, b // 2, (b % 2) * 512:(b % 2 + 1) * 512], ps[:, 4 + b, :],
                                             ACT.Copy).then_inc(acc_copied, 1)
            squares(5)

        @block.gpsimd
        def _(pool):
            for l in range(DEPTH):
                if l:
                    pool.wait_ge(x_ready, norm_x(3)[0])
                pool.wait_ge(mod_cols_copied, 2 * (l + 1))
                pool.dma_start(rope_tables, rope_in).then_inc(rope_in_sem, 16)
                for a, b in BIASED.items():
                    if (a >= STEP0[1]) != (l == 1):
                        continue
                    if b % 8 >= 2:
                        back = [k for k, v in BIASED.items() if v == b - 2][0]
                        pool.wait_ge(max_ready, back + 1)
                    u = b % 8
                    pool.dma_start(bias[:, b % 2, :, :], bias_in[l, u // 2, u % 2, :, :, :])\
                        .then_inc(bias_arrived[b % 2], 16)
                for r, (pl, s) in enumerate(PASSES):
                    if pl != l:
                        continue
                    pool.wait_ge(x_ready, norm_x((1, 2, 4)[r])[0])
                    pool.dma_start(keys, stream_in[KEYS_DRAM[r], :, :]).then_inc(keys_in, 16)
                    for half in range(HALVES):
                        g0 = (r * HALVES + half) * GROUPS

                        def weigh(i, k):
                            pool.wait_ge(hot_i_equal, i * HOT + (g0 + k + 1))
                            gate = pickt[:, 2, bass.ds(i * (8 * HOT) + k * 8, 8)]
                            nc.gpsimd.tensor_tensor(hot_i[:, k, :, :], hot_i[:, k, :, :],
                                                    gate.unsqueeze(2).to_broadcast([P, 8, ROWS]), ALU.mult)\
                                .then_inc(hot_i_ready, 1)

                        with pool.Fori(0, GROUPS // HOT) as i:
                            for k in range(HOT):
                                weigh(i, k)

        @block.vector
        def _(dve):
            v = nc.vector
            order = [0]

            def link(ins):
                order[0] += 1
                ins.then_inc(dve_order, 1)
                dve.wait_ge(dve_order, order[0])

            def inverse(src, dst, count):
                link(v.tensor_scalar(dst, src, 1.0 / count, EPS, ALU.mult, ALU.add))
                v.reciprocal(dst, dst).then_inc(inverse_ready, 1)

            def inverse_root(at, src, dst, count):
                inverse(src, dst, count)
                dve.wait_ge(root_ready, at + 1)

            def split(d):
                dve.wait_ge(dense_hi_ready, d + 1)
                v.tensor_tensor(wt_lo[:, d % 2, :], ring[:, DENSE[d] % RING, :], wt_hi[:, d % 2, :], ALU.subtract)\
                    .then_inc(dense_lo_ready, 1)

            def norm(n, gain, streams, dst, again=False, rooted=False, pair=None):
                need, c0, c1 = norm_x(n)
                e = event(n, again)
                if not (again or rooted):
                    dve.wait_ge(sq_summed, (n + 1) * DC)
                    inverse(ps[:, sums_bank(n), 0:c1 - c0], rstd[:, 0:c1 - c0], D)
                if pair is not None:
                    split(pair)
                if not again:
                    dve.wait_ge(root_ready, root_at(n) + 1)

                def low(c):
                    dve.wait_ge(shifted, e * DC + c + 1)
                    w = len(streams) * N_LAT
                    v.tensor_tensor(dst[1][:, c, 0:w], chunk[:, c % 2, 0:w], dst[0][:, c, 0:w], ALU.subtract)\
                        .then_inc(h_ready, 1)

                for c in range(DC):
                    if c >= 2:
                        low(c - 2)
                        dve.wait_ge(h_ready, e * DC + c - 1)
                    for at, s in enumerate(streams):
                        cols = slice(at * N_LAT, (at + 1) * N_LAT)
                        last = v.scalar_tensor_tensor(chunk[:, c % 2, cols], x[:, c, c0 + at * N_LAT:c0 + (at + 1) * N_LAT],
                                                      gain[:, c, s:s + 1], rstd[:, cols], ALU.mult, ALU.mult)
                    last.then_inc(scaled, 1)
                low(DC - 2)
                low(DC - 1)
                if pair is not None:
                    split(pair + 1)

            def lambdas():
                for l in range(DEPTH):
                    for d in range(2):
                        o = 2 * d * HD
                        last = v.tensor_tensor_reduce(out=rstd[:, o + l * HD:o + (l + 1) * HD], in0=lambdas_sb[:, l, o:o + HD],
                                                      in1=lambdas_sb[:, l, o + HD:o + 2 * HD], scale=1.0, scalar=0.0,
                                                      op0=ALU.mult, op1=ALU.add,
                                                      accum_out=lam[:, 2 * l + d:2 * l + d + 1])
                last.then_inc(lam_dots, 1)
                dve.wait_ge(lam_exps, 1)
                for l in range(DEPTH):
                    minus = lam[:, 8 + l:9 + l]
                    link(v.tensor_tensor(minus, lam[:, 5 + 2 * l:6 + 2 * l], lam[:, 4 + 2 * l:5 + 2 * l], ALU.subtract))
                    link(v.tensor_scalar(minus, minus, -LAM_INIT[l], None, ALU.add))

            def modulation(l):
                base = l * C_LAYER
                dve.wait_ge(mod_cols_copied, 2 * (l + 1))
                if l:
                    dve.wait_ge(x_ready, norm_x(3)[0])
                link(v.tensor_tensor(modc[:, :, :], mod_raw[:, :, :],
                                     small[:, base + C_BMOD:base + C_BMOD + MOD_UNITS].unsqueeze(2)
                                     .to_broadcast([P, MOD_UNITS, 2]), ALU.add))
                for kind, gcol, dst in ((1, C_G1, a1), (4, C_G2, a2)):
                    last = v.scalar_tensor_tensor(dst[:, :, :], modc[:, kind * DC:(kind + 1) * DC, :], 1.0,
                                                  small[:, base + gcol:base + gcol + DC].unsqueeze(2)
                                                  .to_broadcast([P, DC, 2]), ALU.add, ALU.mult)
                last.then_inc(mod_ready, 1)
                dve.wait_ge(mod_ready, l + 1)

            def rope(l):
                dve.wait_ge(rope_in_sem, 16 * (l + 1))

                def turn(k):
                    g = l * len(ROPED) + ROPED.index(k)
                    dve.wait_ge(rot_done, g + 1)
                    t = ropet[:, g % 2, :]
                    f = feat[:, k, 0:N_LAT]
                    v.tensor_tensor(t, ps[:, 4 + g % 2, 0:N_LAT], sin, ALU.mult)
                    link(v.tensor_tensor(f, f, cos, ALU.mult))
                    v.tensor_tensor(f, f, t, ALU.add).then_inc(roped, 1)

                d0 = dense(QKV_AT[l])
                for k in range(NU):
                    if k - 1 in ROPED:
                        turn(k - 1)
                    if k % 2 == 1:
                        split(d0 + k // 2 + 2)
                turn(NU - 1)
                dve.wait_ge(v_done, 9 * l + 1)
                v.tensor_copy(va, ps[:, 6, :].rearrange("p (t c) -> p t c", t=TT)).then_inc(v_copied, 1)
                split(d0 + 12)
                for w, dst in enumerate((vb, vc)):
                    split(d0 + 13 + 2 * w)
                    for t in range(TT):
                        dve.wait_ge(v_done, 9 * l + 2 + 4 * w + t)
                        v.tensor_copy(dst[:, t, :], ps[:, 4 * w + t, :]).then_inc(v_copied, 1)
                    split(d0 + 14 + 2 * w)

            def attention(l):
                steps = STEPS[l]
                sinks = small[:, C_SINK + 8 * l:C_SINK + 8 * (l + 1)]

                def maxima(i):
                    _, s, u, qt = steps[i]
                    a = STEP0[l] + i
                    nk = T if s == 0 else N_CTX
                    st = stat[:, a % 2, :]
                    b = 2 * (a % 2)
                    dve.wait_ge(scores_done, a + 1)
                    if s == 0 and u < 8:
                        if u < 4:
                            add = mask[:, qt, :].unsqueeze(1).to_broadcast([P, 2, N_LAT])
                        else:
                            tile = BIASED[a]
                            dve.wait_ge(bias_arrived[tile % 2], 16 * (tile // 2 + 1))
                            add = bias[:, tile % 2, :, :]
                        link(v.tensor_tensor(ps[:, b:b + 2, 0:N_LAT], ps[:, b:b + 2, 0:N_LAT], add, ALU.add))
                    link(v.tensor_reduce(st[:, 0:2], ps[:, b:b + 2, 0:nk], AX.X, ALU.max))
                    if u < 4:
                        link(v.tensor_tensor(st[:, 0:2], st[:, 0:2], sinks[:, 2 * u:2 * u + 2], ALU.max))
                        v.tensor_tensor(st[:, 10:12], sinks[:, 2 * u:2 * u + 2], st[:, 0:2], ALU.subtract)
                    v.tensor_scalar(st[:, 2:4], st[:, 0:2], -1.0, None, ALU.mult).then_inc(max_ready, 1)

                def normalise(i):
                    _, s, u, qt = steps[i]
                    a = STEP0[l] + i
                    nk = T if s == 0 else N_CTX
                    st = stat[:, a % 2, :]
                    dve.wait_ge(exp_ready, a + 1)
                    if u < 4:
                        link(v.tensor_tensor(st[:, 4:6], st[:, 4:6], st[:, 6:8], ALU.add))
                    link(v.reciprocal(st[:, 8:10], st[:, 4:6]))
                    p0, p1 = prob[:, a % 2, 0, 0:nk], prob[:, a % 2, 1, 0:nk]
                    if u < 8:
                        v.tensor_scalar(p0, p0, st[:, 8:9], None, ALU.mult)
                        v.tensor_scalar(p1, p1, st[:, 9:10], None, ALU.mult).then_inc(prob_ready, 1)
                    else:
                        link(v.tensor_scalar(p1, p1, st[:, 9:10], lam[:, 8 + l:9 + l], ALU.mult, ALU.mult))
                        v.scalar_tensor_tensor(p0, p0, st[:, 8:9], p1, ALU.mult, ALU.add).then_inc(prob_ready, 1)

                def copy_y(i):
                    _, s, u, qt = steps[i]
                    a = STEP0[l] + i
                    dve.wait_ge(y_done, a + 1)
                    t0 = s * N_LAT + qt * P
                    v.tensor_copy(yt[:, u, t0:t0 + P], ps[:, 6 + a % 2, 0:P]).then_inc(y_copied, 1)

                maxima(0)
                for i in range(len(steps)):
                    if i + 1 < len(steps):
                        maxima(i + 1)
                    normalise(i)
                    if i >= 2:
                        copy_y(i - 2)
                copy_y(len(steps) - 2)
                copy_y(len(steps) - 1)

            def head_norm(l):
                n = T if len(STREAMS[l]) == 2 else N_LAT

                def y_low(u):
                    dve.wait_ge(y_hi_ready, 12 * l + u + 1)
                    v.tensor_tensor(ys_lo[:, u, 0:n], yt[:, u, 0:n], ys_hi[:, u, 0:n], ALU.subtract)\
                        .then_inc(y_lo_ready, 1)

                tiles = n // P
                dve.wait_ge(cn_sum, l + 1)
                sums = ps[:, 4, 0:4 * TT].rearrange("p (h t) -> p h t", h=4)[:, :, 0:tiles]
                inverse(sums, head_rstd[:, :, 0:tiles], P)
                dve.wait_ge(root_ready, root_at(l=l) + 1)
                for h in range(4):
                    for t in range(tiles):
                        last = v.tensor_scalar(head_diag[:, h, t, :], ident, head_rstd[:, h, t:t + 1], None, ALU.mult)
                    last.then_inc(head_diag_ready, 1)
                norm((0, 3)[l], a1, STREAMS[l], (h1_hi, h1_lo), True)
                for u in range(4):
                    y_low(u)
                for h in range(4):
                    dve.wait_ge(head_spread, 4 * l + h + 1)
                    link(v.scalar_tensor_tensor(yt[:, 8 + h, 0:n], yt[:, 8 + h, 0:n],
                                                small[:, l * C_LAYER + C_SUBLN + h:l * C_LAYER + C_SUBLN + h + 1],
                                                ps[:, 4 + h, 0:n], ALU.mult, ALU.mult))
                    v.tensor_scalar(yt[:, 8 + h, 0:n], yt[:, 8 + h, 0:n], 1.0 - LAM_INIT[l], None, ALU.mult)\
                        .then_inc(cn_ready, 1)
                for u in range(4, 12):
                    y_low(u)

            def merge(l):
                n = T if len(STREAMS[l]) == 2 else N_LAT

                def m_low(j):
                    dve.wait_ge(m_hi_ready, DC * l + j + 1)
                    v.tensor_tensor(m_lo[:, j, 0:n], sig[:, (3 * j + 2) % 4, 0:n], m_hi[:, j, 0:n], ALU.subtract)\
                        .then_inc(m_ready, 1)

                for item in range(6 * DC):
                    if item % 2 == 1:
                        j, b, g = item // 6, item % 6 // 2, item // 2
                        m = 3 * DC * l + g
                        gated = sig[:, g % 4, 0:n]
                        dve.wait_ge(sig_ready, m + 1)
                        dve.wait_ge(merge_done, 6 * DC * l + item + 1)
                        v.tensor_tensor(gated, ps[:, item % 8, 0:n], gated, ALU.mult).then_inc(prod_done, 1)
                        if b:
                            dve.wait_ge(prod_done, m + 1)
                            if b == 2:
                                dve.wait_ge(added, 2 * (DC * l + j) + 1)
                            v.tensor_tensor(gated, gated, sig[:, (g - 1) % 4, 0:n], ALU.add).then_inc(added, 1)
                    for j in MERGE_ENDS[item]:
                        split(dense(MERGE_AT[l]) + j + 2)
                    if item % 6 == 3 and item > 6:
                        m_low(item // 6 - 1)
                m_low(DC - 1)
                for j in range(WOUT_PAIRS):
                    split(dense(WOUT_AT[l]) + j + 2)
                for j in range(DC):
                    dve.wait_ge(wout_done, DC * l + j + 1)
                    for at, s in enumerate(STREAMS[l]):
                        cols = slice(at * N_LAT, (at + 1) * N_LAT)
                        last = v.scalar_tensor_tensor(x[:, j, cols], ps[:, j, cols], modc[:, 2 * DC + j, s:s + 1],
                                                      x[:, j, cols], ALU.mult, ALU.add)
                    last.then_inc(x_ready, 1)

            def top16(srcs, values, indices):
                copies = [work[:, k * 256:k * 256 + src.shape[-1]] for k, src in enumerate(srcs)]
                for k in range(4):
                    last = v.max(values[k][:, 0:8], srcs[k])
                link(last)
                for k in range(4):
                    last = v.match_replace(copies[k], values[k][:, 0:8], srcs[k], USED)
                link(last)
                for k in range(4):
                    last = v.max(values[k][:, 8:16], copies[k])
                link(last)
                for k in range(4):
                    v.max_index(indices[k][:, 0:8], values[k][:, 0:8], srcs[k])
                    last = v.max_index(indices[k][:, 8:16], values[k][:, 8:16], copies[k])
                return last

            def sides_of(r, g, tt):
                n = 2 * g + tt
                dve.wait_ge(keys_done, 8 * r + n + 1)
                units = range(4 * g, 4 * g + 4)
                top16([ps[:, 2 + n % 6, (u % 4) * P:(u % 4 + 1) * P] for u in units],
                      [best[tt][:, 0, u, :] for u in units],
                      [best[tt][:, 1, u, :].bitcast(u32) for u in units]).then_inc(sides_found, 1)

            def picks_of(r, tt):
                sv, sif = best[tt][:, 0], best[tt][:, 2]
                dve.wait_ge(sides_found, 8 * (r + 1))
                v.tensor_copy(sif, best[tt][:, 1].bitcast(u32))
                sides = sv.rearrange("p (h w) k -> p h w k", w=2)
                for at, r0, r1, width in ((0, 0, 4, 16), (64, 4, 16, 4)):
                    shape = [P, PH, r1 - r0, width]
                    last = v.tensor_tensor(cand[:, :, at:at + (r1 - r0) * width].rearrange("p h (i j) -> p h i j", j=width),
                                           sides[:, :, 0, r0:r1].unsqueeze(3).to_broadcast(shape),
                                           sides[:, :, 1, 0:width].unsqueeze(2).to_broadcast(shape), ALU.add)
                link(last)
                pos3 = pos.rearrange("p (h k) -> p h k", h=PH)
                for h in (range(0, 4), range(4, 8)):
                    last = top16([cand[:, k, :] for k in h], [tv[:, k, :] for k in h], [pos3[:, k, :] for k in h])
                link(last)
                v.tensor_copy(exs[:, 8:16], tv[:, :, 0])
                for part, (by, op) in enumerate(((4, ALU.logical_shift_right), (2, ALU.logical_shift_right),
                                                 (3, ALU.bitwise_and), (12, ALU.bitwise_and))):
                    last = v.tensor_scalar(parts[:, part * HK:(part + 1) * HK], pos, by, None, op)
                link(last)
                v.tensor_tensor(tv, tv, exs[:, 8:16].unsqueeze(2).to_broadcast([P, PH, TOPK]), ALU.subtract)\
                    .then_inc(topd_ready, 1)
                link(v.tensor_copy(partsf, parts))
                by16, by4, low2, next2 = [partsf[:, part * HK:(part + 1) * HK] for part in range(4)]
                v.scalar_tensor_tensor(places[:, 0:HK], by4, -12.0, by16, ALU.add, ALU.max)
                link(v.scalar_tensor_tensor(next2, by16, 4.0, next2, ALU.is_lt, ALU.mult))
                link(v.tensor_tensor(places[:, HK:2 * HK], next2, low2, ALU.add))
                steps16 = iota[:, 0:TOPK].unsqueeze(1).unsqueeze(1).to_broadcast([P, PH, TOPK, TOPK])
                halves = sif.rearrange("p (h w) k -> p h w k", w=2)
                for w in range(2):
                    at = places[:, w * HK:(w + 1) * HK].rearrange("p (h k) -> p h k", h=PH)
                    link(v.tensor_tensor(hot, steps16, at.unsqueeze(3).to_broadcast([P, PH, TOPK, TOPK]),
                                         ALU.is_equal))
                    link(v.tensor_tensor(hot, hot, halves[:, :, w, :].unsqueeze(2)
                                         .to_broadcast([P, PH, TOPK, TOPK]), ALU.mult))
                    link(v.tensor_reduce(picks[:, tt, w, :].rearrange("p (h k) -> p h k", h=PH), hot, AX.X, ALU.add))
                dve.wait_ge(topexp_ready, 2 * r + tt + 1)
                link(v.tensor_reduce(exs[:, 0:8], ex, AX.X, ALU.add))
                link(v.reciprocal(exs[:, 8:16], exs[:, 0:8]))
                v.tensor_tensor(picks[:, tt, 2, :].rearrange("p (h k) -> p h k", h=PH), ex,
                                exs[:, 8:16].unsqueeze(2).to_broadcast([P, PH, TOPK]), ALU.mult)\
                    .then_inc(picks_ready, 1)

            def peer(r, l, s):
                turns = [(g, tt) for g in range(4) for tt in range(2)]
                for j in range(2, WQ_PAIRS):
                    split(dense(WQ_AT[r]) + j)
                    if j >= 3:
                        sides_of(r, *turns[j - 3])
                for g, tt in turns[WQ_PAIRS - 3:]:
                    sides_of(r, g, tt)

                def split_u(i, m):
                    dve.wait_ge(u_hi_ready, i * 4 + (r * KEYS + m + 1))
                    v.tensor_tensor(u_lo[:, m % 2, :], ring[:, (UV_AT[r] + m) % RING, 0:D], u_hi[:, m % 2, :],
                                    ALU.subtract).then_inc(u_lo_ready, 1)

                def split_v(i, m):
                    dve.wait_ge(v_hi_ready, i * 4 + (r * KEYS + m + 1))
                    v.tensor_tensor(v_lo[:, m % 2, :], ring[:, (UV_AT[r] + m) % RING, D:2 * D], v_hi[:, m % 2, :],
                                    ALU.subtract).then_inc(v_lo_ready, 1)

                for tt in range(2):
                    picks_of(r, tt)
                split_u(0, 0)
                split_u(0, 1)
                split_v(0, 0)
                dve.wait_ge(pickt_copied, 2 * (r + 1))
                for half in range(HALVES):
                    g0 = (r * HALVES + half) * GROUPS
                    n0 = (r * HALVES + half) * ROWS

                    def rows(i, k, g0=g0, half=half):
                        if not isinstance(i, int) or g0 + k >= HOT:
                            dve.wait_ge(hot_used, i * HOT + (g0 + k + 1 - HOT))
                        toks = bass.ds(i * (8 * HOT) + k * 8, 8)
                        v.tensor_tensor(hot_i[:, k, :, :],
                                        iota[:, half * ROWS:(half + 1) * ROWS].unsqueeze(1).to_broadcast([P, 8, ROWS]),
                                        pickt[:, 0, toks].unsqueeze(2).to_broadcast([P, 8, ROWS]),
                                        ALU.is_equal).then_inc(hot_i_equal, 1)
                        v.tensor_tensor(hot_j[:, k, :, :], iota.unsqueeze(1).to_broadcast([P, 8, KEYS]),
                                        pickt[:, 1, toks].unsqueeze(2).to_broadcast([P, 8, KEYS]),
                                        ALU.is_equal).then_inc(hot_j_ready, 1)

                    if half == 0:
                        for k in range(HOT):
                            rows(0, k)
                    with dve.Fori(1, GROUPS // HOT) as i:
                        for k in range(HOT):
                            rows(i, k)
                    dve.wait_ge(gates_copied, g0 + GROUPS)

                    def tile(i, k, left=KEYS):
                        n = n0 + k
                        dve.wait_ge(gelu_done, i * 4 + (n + 1))
                        v.tensor_tensor(wfull[:, k % 2, :], ps[:, k, 0:N_LAT], gates[:, i * 4 + k, :], ALU.mult)\
                            .then_inc(w_full_ready, 1)
                        if not isinstance(i, int) or i * 4 + n >= 2:
                            dve.wait_ge(values_done, i * 4 + (n - 1))
                        dve.wait_ge(w_full_ready, i * 4 + (n + 1))
                        v.tensor_copy(w_hi[:, k % 2, :], wfull[:, k % 2, :]).then_inc(w_hi_ready, 1)
                        dve.wait_ge(w_hi_ready, i * 4 + (n + 1))
                        v.tensor_tensor(w_lo[:, k % 2, :], wfull[:, k % 2, :], w_hi[:, k % 2, :], ALU.subtract)\
                            .then_inc(w_ready, 1)
                        m = half * ROWS + k
                        if left > 2:
                            split_u(i, m + 2)
                        if left > 1:
                            split_v(i, m + 1)

                    for k in range(4):
                        tile(0, k)
                    with dve.Fori(1, ROWS // 4 - 1) as i:
                        for k in range(4):
                            tile(i, k)
                    for k in range(4):
                        tile(ROWS // 4 - 1, k, 4 - k if half == HALVES - 1 else KEYS)
                        if half == 0:
                            rows(0, k, g0 + GROUPS, half + 1)
                for c in range(DC):
                    dve.wait_ge(outt_done, DC // 2 * r + c // 2 + 1)
                    o = (c % 2) * 256
                    cols = slice(s * N_LAT, (s + 1) * N_LAT)
                    v.scalar_tensor_tensor(x[:, c, cols], ps[:, c // 2, o:o + N_LAT], modc[:, 5 * DC + c, s:s + 1],
                                           x[:, c, cols], ALU.mult, ALU.add).then_inc(x_ready, 1)

            dve.wait_ge(small_in_sem, 16)
            dve.wait_ge(inputs_in, 48)
            lambdas()
            dve.wait_ge(sq_summed, DC)
            inverse(ps[:, sums_bank(0), :], rstd, D)
            for l in range(DEPTH):
                modulation(l)
                norm((0, 3)[l], a1, [0, 1], (first_hi, first_lo), rooted=(l == 0), pair=dense(QKV_AT[l]))
                rope(l)
                attention(l)
                head_norm(l)
                merge(l)
                for r, (pl, s) in enumerate(PASSES):
                    if pl == l:
                        norm((1, 2, 4)[r], a2, [s], (h_hi, h_lo), pair=dense(WQ_AT[r]) if r == 1 else None)
                        peer(r, l, s)
            dve.wait_ge(sq_summed, 6 * DC)
            inverse_root(root_at(5), ps[:, sums_bank(5), 0:N_LAT], rstd[:, 0:N_LAT], D)
            for c in range(DC):
                last = v.scalar_tensor_tensor(final[:, c, :], x[:, c, 0:N_LAT], small[:, C_GF + c:C_GF + c + 1],
                                              rstd[:, 0:N_LAT], ALU.mult, ALU.mult)
            last.then_inc(out_ready, 1)


IN_SPLITS = (512, 128, 128, 512, 512, 512, 512, 512, 512, 1024, 1024, 1024)


def blocks(w):
    return w.reshape(-1, P, P).transpose(1, 0, 2)


def head_order():
    return np.concatenate([np.arange(h * HD, (h + 1) * HD) for u in range(4) for h in (u, u + 4)])


def wide(w):
    n = w.shape[1] // 512
    return w.reshape(DC, P, n, 4, P).transpose(1, 2, 0, 3, 4).reshape(P, n * DC * 4, P)


def pairs(parts):
    whole = np.concatenate(parts, axis=1)
    return whole.reshape(P, -1, BLOCKS * P).transpose(1, 0, 2)


def weight_stream(w_in, wa, wb, wc, w_out, wq, keys):
    at = np.concatenate([[0], np.cumsum(IN_SPLITS)])
    part = [w_in[:, at[i]:at[i + 1]] for i in range(len(IN_SPLITS))]
    part[0] = part[0][:, head_order()]
    wa = wa[head_order(), :]
    which = {"aq": 0, "ak": 1, "bq": 3, "bk": 4, "cq": 6, "ck": 7}
    out = [blocks(part[which[name]][:, u * P:(u + 1) * P]) for name, u in UNITS]
    out.append(blocks(part[2]))
    for i in (5, 8):
        out.append(wide(part[i]))
    for j in range(DC):
        cols = slice(j * P, (j + 1) * P)
        for gate, branch in ((9, wa), (10, wb), (11, wc)):
            out += [blocks(part[gate][:, cols]), blocks(branch[:, cols])]
    out += [blocks(w_out[:, j * P:(j + 1) * P]) for j in range(DC)]
    out += [blocks(wq[:, u * P:(u + 1) * P]) for u in range(16)]
    out.append(keys.reshape(16, KEYS, P).transpose(2, 0, 1))
    return pairs(out)


def expert_pairs(u, v):
    ut = u.reshape(DEPTH, KEYS, KEYS, DC, P).transpose(0, 1, 4, 3, 2).reshape(DEPTH, KEYS, P, D)
    return np.concatenate([ut, v.reshape(DEPTH, KEYS, KEYS, D)], axis=3)


def bias_tiles(rpb):
    t = np.arange(N_LAT)
    row, col = t // GRID_W, t % GRID_W
    start = np.clip(col - 8, 0, GRID_W - 16)
    inside = (col[None, :] >= start[:, None]) & (col[None, :] < start[:, None] + 16)
    dr = row[None, :] - row[:, None] + 7
    dc = np.clip(col[None, :] - col[:, None], -15, 15) + 15
    n = rpb.shape[2] * rpb.shape[3]
    padded = np.concatenate([rpb.reshape(DEPTH, 8, n), np.full((DEPTH, 8, 1), NEG, rpb.dtype)], axis=2)
    full = padded[:, :, np.where(inside, dr * rpb.shape[3] + dc, n)]
    return np.ascontiguousarray(full.reshape(DEPTH, 4, 2, 2, P, N_LAT).transpose(0, 1, 3, 4, 2, 5))


def columns(v):
    return v.reshape(-1, P).T


def rope():
    t = np.arange(N_LAT)
    n_freq = HD // 4
    inv = np.float32(10000.0) ** (-np.arange(n_freq, dtype=np.float32) / np.float32(n_freq))
    ang = np.concatenate([(t // GRID_W).astype(np.float32)[:, None] * inv,
                          (t % GRID_W).astype(np.float32)[:, None] * inv], axis=1)
    f = np.arange(P) % (HD // 2)
    return np.ascontiguousarray(np.concatenate([np.cos(ang).T[f], np.sin(ang).T[f]], axis=1).astype(np.float32))


def constants():
    out = np.zeros((P, K_ALL), np.float32)
    out[:, K_IDENT:K_IDENT + P] = np.eye(P)
    out[:, K_ONES:K_ONES + P] = 1.0
    out[:, K_IOTA:K_IOTA + P] = np.arange(P)
    for f in range(P):
        if f % HD < HD // 2:
            out[f + HD // 2, K_ROT + f] = -1.0
        else:
            out[f - HD // 2, K_ROT + f] = 1.0
    t = np.arange(N_LAT)
    far = np.abs(t[:, None] - t[None, :]) > 128
    out[:, K_MASK:K_MASK + 512] = np.where(far, NEG, 0.0).reshape(2, P, N_LAT).transpose(1, 0, 2).reshape(P, 512)
    return out


def kernel(**inputs):
    import concourse.bacc as bacc
    from concourse.bass_utils import run_bass_kernel_spmd

    a = {k: np.asarray(v) for k, v in inputs.items()}

    def feature_major(m):
        return m.T.reshape(DC, P, -1).transpose(1, 0, 2)

    x = np.ascontiguousarray(np.concatenate([feature_major(a["x"][0]), feature_major(a["ctx"][0])], axis=2))
    small = []
    for l in range(DEPTH):
        small += [columns(a["g_norm1"][l]), columns(a["g_norm2"][l]), columns(a["b_mod"][l]), columns(a["c_subln"][l])]
    small += [columns(a["g_final"]), np.stack([columns(a["c"][0]), columns(a["c_ctx"])], axis=2).reshape(P, 2 * DC)]
    sinks = a["a_sink"].reshape(DEPTH, 2, 4).transpose(0, 2, 1).reshape(1, DEPTH * 8)
    small.append(np.repeat(sinks, P, axis=0))
    mods = [pairs([wide(w)]) for w in a["w_mod"]]
    layers = [weight_stream(*[a[n][l] for n in (
        "w_in", "w_branch_a", "w_branch_b", "w_branch_c", "w_out", "peer_wq", "peer_keys")]) for l in range(DEPTH)]
    stream = np.concatenate([mods[0], layers[0], mods[1], layers[1]], axis=0)
    assert stream.shape[0] == DRAM_PAIRS
    arrays = {
        "x_in": x,
        "small_in": np.ascontiguousarray(np.concatenate(small, axis=1)),
        "lambda_in": np.repeat(a["c_lambda"].reshape(1, DEPTH, 4 * HD), P, axis=0),
        "const_in": constants(),
        "rope_in": rope(),
        "bias_in": bias_tiles(a["b_rpb"]),
        "stream_in": stream,
        "experts_in": expert_pairs(a["peer_u"], a["peer_v"]),
    }
    nc = bacc.Bacc("TRN2", target_bir_lowering=False, num_devices=1)
    args = [nc.dram_tensor(name, m.shape, mybir.dt.from_np(m.dtype), kind="ExternalInput").ap()
            for name, m in arrays.items()]
    out = nc.dram_tensor("out", (P, DC, N_LAT), mybir.dt.float32, kind="ExternalOutput").ap()
    build(nc, *args, out)
    res = run_bass_kernel_spmd(nc, [arrays], core_ids=[0])
    got = res.results[0]["out"]
    return np.ascontiguousarray(got.transpose(2, 1, 0).reshape(1, N_LAT, D))
```
